# Optimizing a Trainium2 kernel written in Bass

```python
import math
import jax, jax.numpy as jnp
from jax import lax
import numpy as np

D_MODEL = 1024
BATCH = 1
SEQ = 512
DEPTH = 1
DEC_BATCH = 8
DEC_SEQ = 4
PAST_LEN = 1024
PAGE_SIZE = 128

D_CONV = D_MODEL // 2
CONV_GROUPS = 8
CONV_W = 3
N_HEADS = 4
HEAD_DK = 64
HEAD_DV = 2 * HEAD_DK
D_ATTN = N_HEADS * HEAD_DV
D_MIX = D_CONV + D_ATTN
D_IN = 3 * D_CONV + 3 * D_ATTN
N_MEM = 256
MEM_HEADS = 4
MEM_DH = D_MODEL // MEM_HEADS
D_FF = 2816
FFN_W = 3
REL_BUCKETS = 32
REL_MAX_EXACT = 16
REL_MAX_DIST = 128
Q_BLOCK = 128
EPS = 1e-6
NEG = -1e30

kernel_name = "hymba_conv_diffattn_decoder_step"

def rmsnorm(x, w):
    xf = x.astype(jnp.float32)
    y = xf * lax.rsqrt(jnp.mean(xf * xf, axis=-1, keepdims=True) + EPS)
    return (y * w.astype(jnp.float32)).astype(x.dtype)

def causal_dwconv(x, prefix, w, b):
    width = w.shape[0]
    t = x.shape[1]
    xp = jnp.concatenate([prefix.astype(x.dtype), x], axis=1)
    y = b
    for j in range(width):
        y = y + w[j] * xp[:, j:j + t]
    return y, xp[:, -(width - 1):]

def t5_bucket(rel):
    n = jnp.maximum(rel, 0)
    nf = jnp.maximum(n, 1).astype(jnp.float32)
    large = REL_MAX_EXACT + (jnp.log(nf / REL_MAX_EXACT) / math.log(REL_MAX_DIST / REL_MAX_EXACT)
                             * (REL_BUCKETS - REL_MAX_EXACT)).astype(jnp.int32)
    large = jnp.minimum(large, REL_BUCKETS - 1)
    return jnp.where(n < REL_MAX_EXACT, n, large)

def diff_attn_core(q, k, v, q_pos, k_pos, rel_bias, lam):
    rel = q_pos[:, None] - k_pos[None, :]
    bias = rel_bias[t5_bucket(rel)].astype(jnp.float32)
    bias = jnp.where((rel >= 0)[..., None], bias, NEG)
    bias = jnp.transpose(bias, (2, 0, 1))[None, :, None]
    s = jnp.einsum('bqhcd,bkhcd->bhcqk', q, k).astype(jnp.float32) * (HEAD_DK ** -0.5) + bias
    p = jax.nn.softmax(s, axis=-1)
    a = p[:, :, 0] - lam * p[:, :, 1]
    return jnp.einsum('bhqk,bkhd->bqhd', a.astype(v.dtype), v)

def diff_attn_prompt(q, k, v, rel_bias, lam):
    b, s = q.shape[0], q.shape[1]
    nb = s // Q_BLOCK
    qb = jnp.transpose(q.reshape(b, nb, Q_BLOCK, N_HEADS, 2, HEAD_DK), (1, 0, 2, 3, 4, 5))
    k_pos = jnp.arange(s)

    def block(args):
        i, q_i = args
        q_pos = i * Q_BLOCK + jnp.arange(Q_BLOCK)
        return diff_attn_core(q_i, k, v, q_pos, k_pos, rel_bias, lam)

    out = lax.map(block, (jnp.arange(nb), qb))
    return jnp.transpose(out, (1, 0, 2, 3, 4)).reshape(b, s, N_HEADS, HEAD_DV)

def split_mix(z):
    o = [0, D_CONV, 2 * D_CONV, 3 * D_CONV, 3 * D_CONV + D_ATTN, 3 * D_CONV + 2 * D_ATTN, D_IN]
    return [z[..., o[i]:o[i + 1]] for i in range(6)]

def head_norm(o, w, lam_init):
    o = rmsnorm(o, w) * (1.0 - lam_init)
    return o.reshape(o.shape[0], o.shape[1], D_ATTN)

def memory_kv(mem, norm_mem_w, w_ckv):
    kv = rmsnorm(mem, norm_mem_w) @ w_ckv
    b, m = mem.shape[0], mem.shape[1]
    return (kv[..., :D_MODEL].reshape(b, m, MEM_HEADS, MEM_DH),
            kv[..., D_MODEL:].reshape(b, m, MEM_HEADS, MEM_DH))

def cross_attn(h, mk, mv, w_cq, w_co):
    b, t = h.shape[0], h.shape[1]
    q = (h @ w_cq).reshape(b, t, MEM_HEADS, MEM_DH)
    s = jnp.einsum('bqhd,bkhd->bhqk', q, mk).astype(jnp.float32) * (MEM_DH ** -0.5)
    p = jax.nn.softmax(s, axis=-1)
    o = jnp.einsum('bhqk,bkhd->bqhd', p.astype(mv.dtype), mv).reshape(b, t, D_MODEL)
    return o @ w_co

def conv_ffn(h, prefix, w_up, conv_w, conv_b, w_down):
    up = h @ w_up
    c, new_state = causal_dwconv(up, prefix, conv_w, conv_b)
    g, u = c[..., :D_FF], c[..., D_FF:]
    return (jax.nn.silu(g) * u) @ w_down, new_state

def setup_inputs(seed: int = 0) -> dict:
    key = jax.random.key(seed)
    ks = jax.random.split(key, 40)
    n_pages = PAST_LEN // PAGE_SIZE
    n_used = DEC_BATCH * n_pages
    n_phys = n_used + n_used // 4
    f32 = jnp.float32

    def nrm(k, shape, scale=1.0):
        return jax.random.normal(k, shape, f32) * scale

    page_table = jax.random.permutation(ks[0], n_phys)[:n_used].reshape(DEC_BATCH, n_pages).astype(jnp.int32)
    return {
        "x_prompt": nrm(ks[1], (BATCH, SEQ, D_MODEL)),
        "x_sample": nrm(ks[2], (DEC_BATCH, DEC_SEQ, D_MODEL)),
        "mem_prompt": nrm(ks[3], (BATCH, N_MEM, D_MODEL)),
        "cache_k": nrm(ks[4], (DEPTH, n_phys, PAGE_SIZE, N_HEADS, 2 * HEAD_DK)),
        "cache_v": nrm(ks[5], (DEPTH, n_phys, PAGE_SIZE, N_HEADS, HEAD_DV)),
        "page_table": page_table,
        "state_conv_mix": nrm(ks[6], (DEPTH, DEC_BATCH, CONV_W - 1, D_CONV)),
        "state_conv_ffn": nrm(ks[7], (DEPTH, DEC_BATCH, FFN_W - 1, 2 * D_FF)),
        "cache_mem_k": nrm(ks[8], (DEPTH, DEC_BATCH, N_MEM, MEM_HEADS, MEM_DH)),
        "cache_mem_v": nrm(ks[9], (DEPTH, DEC_BATCH, N_MEM, MEM_HEADS, MEM_DH)),
        "rel_bias": nrm(ks[10], (REL_BUCKETS, N_HEADS), 0.5),
        "norm_mix_w": 1.0 + nrm(ks[11], (DEPTH, D_MODEL), 0.02),
        "w_in": nrm(ks[12], (DEPTH, D_MODEL, D_IN), D_MODEL ** -0.5),
        "conv_mix_w": nrm(ks[13], (DEPTH, CONV_W, D_CONV), CONV_W ** -0.5),
        "conv_mix_b": nrm(ks[14], (DEPTH, D_CONV), 0.02),
        "lambda_q1": nrm(ks[15], (DEPTH, HEAD_DK), 0.1),
        "lambda_k1": nrm(ks[16], (DEPTH, HEAD_DK), 0.1),
        "lambda_q2": nrm(ks[17], (DEPTH, HEAD_DK), 0.1),
        "lambda_k2": nrm(ks[18], (DEPTH, HEAD_DK), 0.1),
        "subln_w": 1.0 + nrm(ks[19], (DEPTH, HEAD_DV), 0.02),
        "w_out": nrm(ks[20], (DEPTH, D_MIX, D_MODEL), D_MIX ** -0.5),
        "norm_cross_w": 1.0 + nrm(ks[21], (DEPTH, D_MODEL), 0.02),
        "norm_mem_w": 1.0 + nrm(ks[22], (DEPTH, D_MODEL), 0.02),
        "w_cq": nrm(ks[23], (DEPTH, D_MODEL, D_MODEL), D_MODEL ** -0.5),
        "w_ckv": nrm(ks[24], (DEPTH, D_MODEL, 2 * D_MODEL), D_MODEL ** -0.5),
        "w_co": nrm(ks[25], (DEPTH, D_MODEL, D_MODEL), D_MODEL ** -0.5),
        "norm_ffn_w": 1.0 + nrm(ks[26], (DEPTH, D_MODEL), 0.02),
        "w_up": nrm(ks[27], (DEPTH, D_MODEL, 2 * D_FF), D_MODEL ** -0.5),
        "conv_ffn_w": nrm(ks[28], (DEPTH, FFN_W, 2 * D_FF), FFN_W ** -0.5),
        "conv_ffn_b": nrm(ks[29], (DEPTH, 2 * D_FF), 0.02),
        "w_down": nrm(ks[30], (DEPTH, D_FF, D_MODEL), D_FF ** -0.5),
        "norm_final_w": 1.0 + nrm(ks[31], (D_MODEL,), 0.02),
    }

def reference(x_prompt, x_sample, mem_prompt, cache_k, cache_v, page_table, state_conv_mix,
              state_conv_ffn, cache_mem_k, cache_mem_v, rel_bias, norm_mix_w, w_in, conv_mix_w,
              conv_mix_b, lambda_q1, lambda_k1, lambda_q2, lambda_k2, subln_w, w_out,
              norm_cross_w, norm_mem_w, w_cq, w_ckv, w_co, norm_ffn_w, w_up, conv_ffn_w,
              conv_ffn_b, w_down, norm_final_w):
    n_pages = PAST_LEN // PAGE_SIZE
    bp, sp = x_prompt.shape[0], x_prompt.shape[1]
    bs, ts = x_sample.shape[0], x_sample.shape[1]
    xp, xs = x_prompt, x_sample
    kp_l, vp_l, ks_l, vs_l = [], [], [], []
    cmp_l, cms_l, cfp_l, cfs_l, mkp_l, mvp_l = [], [], [], [], [], []
    for l in range(DEPTH):
        lam_init = 0.8 - 0.6 * math.exp(-0.3 * l)
        lam = (jnp.exp(jnp.sum(lambda_q1[l].astype(jnp.float32) * lambda_k1[l].astype(jnp.float32)))
               - jnp.exp(jnp.sum(lambda_q2[l].astype(jnp.float32) * lambda_k2[l].astype(jnp.float32)))
               + lam_init)

        gbp, gcp, up_, qp, kp, vp = split_mix(rmsnorm(xp, norm_mix_w[l]) @ w_in[l])
        gbs, gcs, us, qs, kn, vn = split_mix(rmsnorm(xs, norm_mix_w[l]) @ w_in[l])

        pre_p = gcp * up_
        cp, conv_mix_p = causal_dwconv(pre_p, jnp.zeros((bp, CONV_W - 1, D_CONV), pre_p.dtype),
                                       conv_mix_w[l], conv_mix_b[l])
        yconv_p = gbp * cp
        cs, conv_mix_s = causal_dwconv(gcs * us, state_conv_mix[l], conv_mix_w[l], conv_mix_b[l])
        yconv_s = gbs * cs

        qp5 = qp.reshape(bp, sp, N_HEADS, 2, HEAD_DK)
        kp4 = kp.reshape(bp, sp, N_HEADS, 2 * HEAD_DK)
        vp4 = vp.reshape(bp, sp, N_HEADS, HEAD_DV)
        op = diff_attn_prompt(qp5, kp4.reshape(bp, sp, N_HEADS, 2, HEAD_DK), vp4, rel_bias, lam)
        yattn_p = head_norm(op, subln_w[l], lam_init)

        qs5 = qs.reshape(bs, ts, N_HEADS, 2, HEAD_DK)
        kn4 = kn.reshape(bs, ts, N_HEADS, 2 * HEAD_DK)
        vn4 = vn.reshape(bs, ts, N_HEADS, HEAD_DV)
        k_past = cache_k[l][page_table].reshape(bs, n_pages * PAGE_SIZE, N_HEADS, 2 * HEAD_DK)
        v_past = cache_v[l][page_table].reshape(bs, n_pages * PAGE_SIZE, N_HEADS, HEAD_DV)
        k_all = jnp.concatenate([k_past.astype(kn4.dtype), kn4], axis=1)
        v_all = jnp.concatenate([v_past.astype(vn4.dtype), vn4], axis=1)
        q_pos = PAST_LEN + jnp.arange(ts)
        k_pos = jnp.arange(PAST_LEN + ts)
        os_ = diff_attn_core(qs5, k_all.reshape(bs, PAST_LEN + ts, N_HEADS, 2, HEAD_DK), v_all,
                             q_pos, k_pos, rel_bias, lam)
        yattn_s = head_norm(os_, subln_w[l], lam_init)

        xp = xp + jnp.concatenate([yconv_p, yattn_p], axis=-1) @ w_out[l]
        xs = xs + jnp.concatenate([yconv_s, yattn_s], axis=-1) @ w_out[l]

        mkp, mvp = memory_kv(mem_prompt, norm_mem_w[l], w_ckv[l])
        xp = xp + cross_attn(rmsnorm(xp, norm_cross_w[l]), mkp, mvp, w_cq[l], w_co[l])
        xs = xs + cross_attn(rmsnorm(xs, norm_cross_w[l]), cache_mem_k[l].astype(xs.dtype),
                             cache_mem_v[l].astype(xs.dtype), w_cq[l], w_co[l])

        fp, conv_ffn_p = conv_ffn(rmsnorm(xp, norm_ffn_w[l]),
                                  jnp.zeros((bp, FFN_W - 1, 2 * D_FF), xp.dtype),
                                  w_up[l], conv_ffn_w[l], conv_ffn_b[l], w_down[l])
        fs, conv_ffn_s = conv_ffn(rmsnorm(xs, norm_ffn_w[l]), state_conv_ffn[l],
                                  w_up[l], conv_ffn_w[l], conv_ffn_b[l], w_down[l])
        xp = xp + fp
        xs = xs + fs

        kp_l.append(kp4); vp_l.append(vp4); ks_l.append(kn4); vs_l.append(vn4)
        cmp_l.append(conv_mix_p); cms_l.append(conv_mix_s)
        cfp_l.append(conv_ffn_p); cfs_l.append(conv_ffn_s)
        mkp_l.append(mkp); mvp_l.append(mvp)

    y_prompt = rmsnorm(xp, norm_final_w)
    y_sample = rmsnorm(xs, norm_final_w)
    return (y_prompt, y_sample, jnp.stack(kp_l), jnp.stack(vp_l), jnp.stack(ks_l), jnp.stack(vs_l),
            jnp.stack(cmp_l), jnp.stack(cms_l), jnp.stack(cfp_l), jnp.stack(cfs_l),
            jnp.stack(mkp_l), jnp.stack(mvp_l))


_drawn_inputs = setup_inputs


def setup_inputs(seed=0):
    import zlib

    import numpy as np

    out = dict(_drawn_inputs(seed))
    spreads = {}
    factors = {'conv_mix_b': 5.322,
     'lambda_k1': 2.876,
     'lambda_k2': 4.525,
     'subln_w': 6.432,
     'norm_cross_w': 8.0,
     'norm_mem_w': 2.821,
     'norm_ffn_w': 2.793,
     'conv_ffn_b': 4.885,
     'norm_final_w': 2.901}
    for name, (base, spread) in spreads.items():
        noise = np.random.default_rng([zlib.crc32(name.encode()), seed]).standard_normal(out[name].shape)
        drawn = base * np.exp(spread * noise) if base else spread * noise
        out[name] = __import__('jax').numpy.asarray(drawn.astype(out[name].dtype))
    for name, factor in factors.items():
        out[name] = (out[name] * factor).astype(out[name].dtype)
    return out
```

```python
from contextlib import ExitStack

import numpy as np

import concourse.bass as bass
from concourse import mybir

F32 = mybir.dt.float32
F32R = mybir.dt.float32r
I32 = mybir.dt.int32
ALU = mybir.AluOpType
ACT = mybir.ActivationFunctionType
AX = mybir.AxisListType

P = 128
D_MODEL, SEQ, DEC_BATCH, DEC_SEQ, PAST, PAGE = 1024, 512, 8, 4, 1024, 128
D_CONV, HEADS, DK, DV, N_MEM, D_FF, BUCKETS = 512, 4, 64, 128, 256, 2816, 32
MEM_DH = D_MODEL // HEADS
EPS, NEG = 1e-6, -1e30
LAM_INIT = 0.2
KT = D_MODEL // P
CT = D_CONV // P
FT = D_FF // P
HALF_P, HALF_S = SEQ // 2, DEC_BATCH * DEC_SEQ // 2
HALF = HALF_P + HALF_S
TOK = 2 * HALF
BLOCK = [0, P, HALF + HALF_S, HALF + HALF_S + P]
NPAGES = PAST // PAGE
GROUPS, GB = 2, 4
FFN_GROUPS = [range(0, 8), range(8, 15), range(15, 22)]
DIST = 384
W_STAGE, W_SPLIT = 3, 3
PAGE_RING = 8
VEC_ROWS = 5 * KT + 3 * CT + CT + 1
V_MIX, V_CROSS, V_MEM, V_FFN, V_FINAL = 0, KT, 2 * KT, 3 * KT, 4 * KT
V_CW, V_CB, V_SUB = 5 * KT, 5 * KT + 3 * CT, 5 * KT + 4 * CT


def bucket_onehot():
    import math
    m = np.zeros((BUCKETS + 1, DIST), np.float32)
    for col in range(DIST):
        n = col - (P - 1)
        if n < 0:
            m[BUCKETS, col] = 1.0
            continue
        big = 16 + int(np.float32(np.log(np.float32(max(n, 1) / 16.0))) / np.float32(math.log(8.0)) * 16) if n >= 16 else n
        m[min(big, BUCKETS - 1), col] = 1.0
    return m


def row_columns():
    m = np.zeros((P, 5), np.float32)
    for r in range(P):
        if r % 32 < 16:
            m[r, (r % 32) // DEC_SEQ] = 1.0
        else:
            m[r, 4] = 1.0
    return m


def make_tiles():
    tiles = []

    def add(phase, kind, i, weight, row0, rows, col):
        tiles.append(dict(phase=phase, kind=kind, i=i, weight=weight, row0=row0, kt=rows // P,
                          col=col, first=not tiles or tiles[-1]["phase"] != phase, n=len(tiles)))

    for h in range(HEADS):
        add("in", "q", h, "w_in", 0, D_MODEL, 3 * D_CONV + h * P)
    for h in range(HEADS):
        add("in", "k", h, "w_in", 0, D_MODEL, 3 * D_CONV + 512 + h * P)
    for h in range(HEADS):
        add("in", "v", h, "w_in", 0, D_MODEL, 3 * D_CONV + 1024 + h * P)
    for c in range(CT):
        for j, kind in enumerate(("gb", "gc", "u")):
            add("in", kind, c, "w_in", 0, D_MODEL, j * D_CONV + c * P)
    for n in range(KT):
        add("out", "add", n, "w_out", 0, D_MODEL, n * P)
    for n in range(2 * KT):
        add("mem", "mem", n, "w_ckv", 0, D_MODEL, n * P)
    for n in range(KT):
        add("cq", "cq", n, "w_cq", 0, D_MODEL, n * P)
    for n in range(KT):
        add("co", "add", n, "w_co", 0, D_MODEL, n * P)
    for g, group in enumerate(FFN_GROUPS):
        for i in group:
            add("up", "gate", i, "w_up", 0, D_MODEL, i * P)
            add("up", "up", i, "w_up", 0, D_MODEL, D_FF + i * P)
        for n in range(KT):
            add(f"down{g}", "add", n, "w_down", group[0] * P, len(group) * P, n * P)
    return tiles


TILES = make_tiles()
TILE = {(t["phase"], t["kind"], t["i"]): t["n"] for t in TILES}


def make_schedule():
    s = []

    def tile(phase, kind, i):
        s.append(("tile", TILE[phase, kind, i]))

    s.append(("setup",))
    s += [("x_in", i) for i in range(5)]
    s += [("squares", k, "x") for k in range(KT)]
    s.append(("norm", "in"))
    for h in range(HEADS):
        tile("in", "q", h)
    s.append(("bias",))
    s.append(("q_blocks",))
    fill = [("in", "k", h) for h in range(HEADS)] + [("in", "v", h) for h in range(HEADS)]
    fill += [("in", kind, c) for c in range(CT) for kind in ("gb", "gc", "u")]
    after = {("in", "k", h): [("k_out", h)] for h in range(HEADS)}
    after |= {("in", "v", h): [("v_out", h)] for h in range(HEADS)}
    def keys(g, kq):
        tick = [("k_score", g, kq - 1, 1)] if kq else []
        return tick + [("k_turn", g, kq, 0), ("k_score", g, kq, 0), ("k_turn", g, kq, 1)]

    plan = [keys(0, kq) for kq in range(4)]
    plan.append([("k_score", 0, 3, 1), ("s_soft", 0)])
    plan.append([("s_turn", 0), ("s_pv", 0, 0), ("s_pv", 0, 1)])
    plan.append([("s_pv", 0, 2), ("s_pv", 0, 3)])
    plan += [keys(1, 0), keys(1, 1), keys(1, 2) + [("s_new", 0), ("s_norm", 0)]]
    plan.append(keys(1, 3) + [("s_out", 0)])
    plan.append([("k_score", 1, 3, 1), ("s_soft", 1)])
    plan.append([("s_turn", 1), ("s_pv", 1, 0), ("s_pv", 1, 1)])
    plan.append([("s_pv", 1, 2), ("s_pv", 1, 3), ("s_new", 1), ("s_norm", 1)])
    units = [(i, h) for i in range(SEQ // P) for h in range(HEADS)]
    ticks = []
    for u in range(len(units) + 3):
        tick = [("s_out", 1)] if u == 0 else []
        if u < len(units):
            tick.append(("p_score", *units[u]))
        if 0 <= u - 1 < len(units):
            tick.append(("p_turn", *units[u - 1]))
        if 0 <= u - 2 < len(units):
            tick.append(("p_pv", *units[u - 2]))
            if units[u - 2][1] == HEADS - 1:
                tick.append(("p_norm", units[u - 2][0]))
        if u >= 3 and units[u - 3][1] == HEADS - 1:
            tick.append(("p_out", units[u - 3][0]))
        ticks.append(tick)
    rest = len(fill) - len(plan)
    late = []
    for j, f in enumerate(fill):
        tile(*f)
        s.extend(late)
        late = after.get(f, [])
        if j < len(plan):
            s.extend(plan[j])
        else:
            m = j - len(plan)
            for tick in ticks[m * len(ticks) // rest:(m + 1) * len(ticks) // rest]:
                s.extend(tick)
        if f[1] == "u":
            s.append(("conv", f[2]))
    s.append(("mem_in",))
    s += [("squares", k, "mem") for k in range(KT)]
    for n in range(KT):
        tile("out", "add", n)
        if n == 0:
            s.append(("norm", "mem"))
        if n:
            s.append(("squares", n - 1, "x"))
    s.append(("squares", KT - 1, "x"))
    for n in range(2 * KT):
        tile("mem", "mem", n)
        if n:
            s.append(("mem_out", n - 1))
        if n == 0:
            s.append(("norm", "cq"))
    for n in range(KT):
        tile("cq", "cq", n)
        if n == 0:
            s.append(("mem_out", 2 * KT - 1))
    s.append(("cq_blocks",))
    units = [(hp, i) for hp in range(2) for i in range(4)]
    parts = []
    for g in range(GROUPS):
        for kt in range(2):
            parts += [[("ck_turn", g, kt, 0)], [("ck_score", g, kt, 0), ("ck_turn", g, kt, 1)],
                      [("ck_score", g, kt, 1)]]
        parts[-1].append(("cs_soft", g))
        parts += [[("cs_turn", g), ("cs_pv", g, 0)], [("cs_pv", g, 1), ("cs_out", g)]]
    for j, part in enumerate(parts):
        if j < 8:
            s.append(("c_score", *units[j]))
        if 1 <= j < 9:
            s.append(("c_turn", *units[j - 1]))
        s += part
        if 8 <= j < 16:
            s.append(("c_pv", j - 8))
    for n in range(KT):
        tile("co", "add", n)
        if n:
            s.append(("squares", n - 1, "x"))
    s += [("squares", KT - 1, "x"), ("state_in",), ("norm", "up")]
    for g, group in enumerate(FFN_GROUPS):
        for i in group:
            tile("up", "gate", i)
            tile("up", "up", i)
            s.append(("ffn", g, i))
        if g == 2:
            s += [("state_out", j) for j in range(2 * FT // 4)]
        for n in range(KT):
            tile(f"down{g}", "add", n)
            if g == 2 and n:
                s.append(("squares", n - 1, "x"))
    s += [("squares", KT - 1, "x"), ("norm", "final")]
    s += [("final", i) for i in range(5)]
    return s


SCHEDULE = make_schedule()
FILLS = {
    "setup": ["T0", "T1"], "x_in": ["T0", "T1"], "norm": ["S0", "S1"], "bias": ["S0"],
    "k_out": ["T0", "T1"], "v_out": ["T0", "T1"], "k_turn": ["T0", "T1"] * 2,
    "s_turn": ["T0", "T1", "T0"], "p_score": ["S0", "S1"], "p_turn": ["T0"],
    "s_out": ["T0"], "p_out": ["T0"],
    "mem_in": ["T0", "T1", "T0", "T1", "S0"], "mem_out": ["T0"], "c_score": ["S1"],
    "c_turn": ["T0"], "c_pv": ["S1"], "ck_turn": ["T0", "T1"] * 2,
    "cs_turn": ["T0"], "state_in": ["T0", "T1"], "final": ["T0", "T1"],
}


def number_fills():
    count = dict(S0=0, S1=0, T0=0, T1=0)
    out, held = [], {}

    def use(slot):
        count[slot] += 1
        return slot, count[slot] - 1

    for step in SCHEDULE:
        kind = step[0]
        uses = [use(slot) for slot in FILLS.get(kind, [])]
        if kind == "k_score":
            if step[3] == 0:
                held["k"] = use("S0")
            uses = [held["k"]]
            if step[2] == 3 and step[3] == 1:
                uses.append(use("S1"))
        if kind == "norm" and step[1] == "mem":
            count["S1"] -= 1
            uses = uses[:1]
        if kind == "s_pv":
            if step[2] == 0:
                held["s", step[1]] = use("S1")
            uses = [held["s", step[1]]]
        if kind in ("s_new", "s_norm"):
            uses = [held["s", step[1]]]
        if kind == "p_pv":
            if step[2] == 0:
                held["p", step[1]] = use("T1")
            uses = [held["p", step[1]]]
        if kind == "p_norm":
            uses = [held["p", step[1]]]
        if kind == "ck_score":
            if step[3] == 0:
                held["ck"] = use("S0")
            uses = [held["ck"]]
        if kind == "cs_pv":
            if step[2] == 0:
                held["cs"] = [use("S0"), use("T1")]
            uses = list(held["cs"])
        if kind == "cs_out":
            uses = [*held["cs"], use("T0"), use("T1")]
        if kind == "state_out":
            uses = [use("T0" if step[1] % 2 == 0 else "T1")]
        latest = {slot: n - 1 for slot, n in count.items()}
        out.append((step, uses, latest))
    return out


NUMBERED = number_fills()


def self_page(g, cache, kq, b, pg):
    n = (g * 2 + (cache == "v")) * 4 + kq
    return (n * 2 + pg) * GB + b if cache == "v" else (n * GB + b) * 2 + pg


def cross_page(g, cache, kt, b):
    return ((g * 2 + (cache == "v")) * 2 + kt) * GB + b


def build(nc, t):
    ctx = ExitStack()
    with ctx:
        sems = {}

        def sem(name):
            if name not in sems:
                sems[name] = ctx.enter_context(nc.semaphore(name))
            return sems[name]

        def sb(name, shape, dtype=F32, stack=ctx, side=None):
            return stack.enter_context(nc.sbuf_tensor(name, shape, dtype, side=side))

        w_stage = sb("w_stage", [P, W_STAGE, KT, P])
        w_hi = sb("w_hi", [P, W_SPLIT, KT, P], F32R)
        w_lo = sb("w_lo", [P, W_SPLIT, KT, P], F32R)
        x = sb("x", [P, KT, TOK])
        a_hi = sb("a_hi", [P, KT, TOK], F32R)
        a_lo = sb("a_lo", [P, KT, TOK], F32R)
        ident = sb("ident", [P, P])
        ones = sb("ones", [P, P])
        vec = sb("vec", [P, VEC_ROWS])
        fvec = sb("fvec", [P, 8 * FT])
        eps = sb("eps", [P, 1])
        neg_lam = sb("neg_lam", [P, 1])
        sub_w = sb("sub_w", [P, 1])
        norm_area = sb("norm_area", [P, 7 * TOK])

        def lend(area, start, shape):
            n = int(np.prod(shape))
            v = area[:, start:start + n]
            if len(shape) == 1:
                return v
            names = " ".join(f"d{i}" for i in range(len(shape)))
            return v.rearrange(f"p ({names}) -> p {names}", **{f"d{i}": m for i, m in enumerate(shape)})

        normed = lend(norm_area, 0, (3, TOK))
        square = lend(norm_area, 3 * TOK, (2, TOK))
        sums = lend(norm_area, 5 * TOK, (TOK,))
        rstd = lend(norm_area, 6 * TOK, (TOK,))

        right = ExitStack()
        b_hi = sb("b_hi", [P, KT, TOK], F32R, right, "right")
        b_lo = sb("b_lo", [P, KT, TOK], F32R, right, "right")
        right.close()
        right = ExitStack()
        c_hi = sb("c_hi", [P, KT, TOK], F32R, right, "right")
        c_lo = sb("c_lo", [P, KT, TOK], F32R, right, "right")
        right.close()
        right = ExitStack()
        c_keys = sb("c_keys", [P, HEADS * 2, SEQ], F32, right, "right")
        c_turned = sb("c_turned", [P, GB, 4 * P], F32, right, "right")
        right.close()
        d_hi = sb("d_hi", [P, KT, TOK], F32R, ctx, "right")
        d_lo = sb("d_lo", [P, KT, TOK], F32R, ctx, "right")

        one = ExitStack()
        q_t = sb("q_t", [P, HEADS, TOK], F32, one)
        k_t = sb("k_t", [P, HEADS, TOK], F32, one)
        v_tok = sb("v_tok", [P, 5, HEADS * DV], F32, one)
        near = sb("near", [P, HEADS, 2 * P], F32, one)
        near_s = sb("near_s", [P, P + DEC_SEQ], F32, one)
        new_bias = sb("new_bias", [P, GROUPS, 32], F32, one)
        q_rows = sb("q_rows", [P, HEADS, DEC_BATCH, 32], F32, one)
        row_cols = sb("row_cols", [P, 5], F32, one)
        lam_row = sb("lam_row", [P, 1], F32, one)
        small = sb("small", [P, 64], F32, one)
        pages = sb("pages", [P, PAGE_RING * HEADS * DV], F32, one)
        turned = sb("turned", [P, GB * 4 * P], F32, one)
        pre = sb("pre", [P, 2 + SEQ], F32, one)
        pre_s = sb("pre_s", [P, DEC_BATCH, 2 + DEC_SEQ], F32, one)
        mix_prefix = sb("mix_prefix", [P, CT * 16], F32, one)
        mix_state = sb("mix_state", [P, CT, 18], F32, one)
        page_ids = sb("page_ids", [1, DEC_BATCH * NPAGES], I32, one)
        one.close()
        page = lend(pages, 0, (PAGE_RING, HEADS * DV))
        x_tok = lend(pages, 0, (4, D_MODEL))
        p_exp = lend(pages, 0, (2, 2, SEQ))
        p_keys = lend(pages, 2048, (2, 4, P))
        o_blk = lend(pages, 3072, (HEADS * DV,))
        o_sq = lend(pages, 3584, (HEADS * DV,))
        k_turned = lend(turned, 0, (GB, 4 * P))
        x_tok_s = lend(turned, 0, (D_MODEL,))
        packed = lend(turned, D_MODEL, (3, P))
        onehot = lend(turned, 1536, (DIST,))
        rel = turned[:, 1536 + DIST:1536 + DIST + HEADS]
        mem_tok = lend(turned, 0, (2, D_MODEL))
        mem_t = lend(q_t[:, :, :].rearrange("p a b -> p (a b)"), 0, (KT, N_MEM))
        mix_in = v_tok[:, 0, :]
        lams = lend(v_tok[:, 1, :], 0, (4, DK))
        gates = lend(norm_area, 0, (2, TOK))
        s_sb = lend(norm_area, 2 * TOK, (PAST + 32,))
        s_keys = lend(norm_area, 2 * TOK + PAST + 32, (9 * GB, 32))
        o_sb = lend(norm_area, 2 * TOK + PAST + 32 + 9 * GB * 32, (HEADS * DV,))
        near_raw = lend(norm_area, 2 * TOK, (HEADS, 2 * P))
        near_s_raw = o_sb[:, 0:P + DEC_SEQ]
        dist_vec = s_keys[:, 0:12, :].rearrange("p a b -> p (a b)")
        k_out = o_sb
        k_out_s = pre[0:32, 2:2 + P]
        mix_out = lend(k_t[:, :, :].rearrange("p a b -> p (a b)"), 0, (HEADS * DV,))

        two = ExitStack()
        qc_t = sb("qc_t", [P, KT, TOK], F32, two)
        mk_t = sb("mk_t", [P, KT, N_MEM], F32, two)
        mv_tok = sb("mv_tok", [P, 2, D_MODEL], F32, two)
        m_stage = sb("m_stage", [P, 2, 2, P], F32, two)
        mv_t = sb("mv_t", [P, 2, N_MEM], F32, two)
        qc_rows = sb("qc_rows", [P, KT, DEC_BATCH, 32], F32, two)
        c_pages = sb("c_pages", [P, GB, D_MODEL], F32, two)
        c_small = sb("c_small", [P, 32], F32, two)
        two.close()
        c_exp = lend(norm_area, 0, (2, 2, N_MEM))
        c_s = lend(norm_area, 1024, (N_MEM,))
        cs_keys = lend(norm_area, 1280, (2, P))
        o_cross = lend(norm_area, 1536, (D_MODEL,))

        three = ExitStack()
        f_rows = sb("f_rows", [18, 2 * D_FF], F32, three)
        f_prefix = sb("f_prefix", [P, 2 * FT, 16], F32, three)
        f_state = sb("f_state", [P, 2 * FT, 18], F32, three)
        up_pad = sb("up_pad", [P, 2, 2, 2 + SEQ], F32, three)
        up_pad_s = sb("up_pad_s", [P, 2, 2, DEC_BATCH, 2 + DEC_SEQ], F32, three)
        conv = sb("conv", [P, 2, TOK], F32, three)
        three.close()
        y_out = lend(norm_area, 0, (3, D_MODEL))

        proj = [ctx.enter_context(nc.psum_tensor(f"proj{i}", [P, 2, 512], F32)) for i in range(2)]
        score = ctx.enter_context(nc.psum_tensor("score", [P, 2, 512], F32))
        bank = {"S0": score[:, 0, :], "S1": score[:, 1, :]}
        for name in ("T0", "T1"):
            bank[name] = ctx.enter_context(nc.psum_tensor(name, [P, 512], F32))[:, :]
        quads = {name: ap.rearrange("p (j c) -> p j c", c=P) for name, ap in bank.items()}

        w_loaded = [sem(f"w_loaded{i}") for i in range(W_STAGE)]
        w_hi_ready, w_lo_ready = sem("w_hi_ready"), sem("w_lo_ready")
        tile_done = sem("tile_done")
        tile_out = [sem("tile_out0"), sem("tile_out1")]
        full = {s: sem(f"full_{s}") for s in ("S0", "S1", "T0", "T1")}
        free = {s: sem(f"free_{s}") for s in ("S0", "S1", "T0", "T1")}
        ready = {ph: sem(f"ready_{ph}") for ph in ("in", "mem", "cq", "up", "final")}

        def wait_full(eng, use):
            eng.wait_ge(full[use[0]], use[1] + 1)

        def wait_empty(eng, use):
            if use[1] > 0:
                eng.wait_ge(free[use[0]], use[1])

        def wait_taken(eng, slot, n):
            eng.wait_ge(free[slot], n + 1)

        def wait_tile_out(eng, n):
            eng.wait_ge(tile_out[n % 2], n // 2 + 1)

        def free_dims(ap, start, dims):
            return bass.AP(ap.tensor, ap.offset + start, [list(ap.ap[0])] + [list(d) for d in dims])

        def prompt(ap):
            return free_dims(ap, 0, [(HALF + HALF_S, 2), (1, HALF_P)])

        def samples(ap):
            return ap[:, HALF_P:HALF + HALF_S].rearrange("p (a b q) -> p a b q", a=2, q=DEC_SEQ)

        def prompt_of(banks):
            return free_dims(banks, 0, [(512 + HALF_S, 2), (1, HALF_P)])

        def samples_of(banks):
            return free_dims(banks, HALF_P, [(512 - HALF_P, 2), (DEC_SEQ, GB), (1, DEC_SEQ)])

        def halves(ap):
            return ap.rearrange("p (a b) -> p a b", a=2)

        def by_half(ap):
            return ap.rearrange("p (a b) -> p a b", a=2)

        def seqs(ap, lo, hi):
            return ap[:, :, lo:hi].rearrange("p (a b) q -> p a b q", a=2)

        def block_cols(ap, k, i):
            if i < 4:
                return ap[:, k, BLOCK[i]:BLOCK[i] + P]
            return ap[:, k, HALF_P:HALF + HALF_S]

        def head_rows(name, j_step, j0, n):
            return free_dims(bank[name], j0, [(j_step, n), (32, GB), (1, DEC_SEQ)])

        split = {"in": (a_hi, a_lo), "out": (b_hi, b_lo), "mem": (a_hi, a_lo), "cq": (c_hi, c_lo),
                 "co": (a_hi, a_lo), "up": (d_hi, d_lo)}
        for g in range(3):
            split[f"down{g}"] = (a_hi, a_lo)
        IN_LAST, OUT_FIRST = TILE["in", "u", CT - 1], TILE["out", "add", 0]
        MEM_FIRST, CQ_LAST, CO_FIRST = TILE["mem", "mem", 0], TILE["cq", "cq", KT - 1], TILE["co", "add", 0]
        norms = [s[1] for s in SCHEDULE if s[0] == "norm"]
        norm_w = {"in": V_MIX, "mem": V_MEM, "cq": V_CROSS, "up": V_FFN, "final": V_FINAL}
        norm_src = {"in": x, "mem": None, "cq": x, "up": x, "final": x}
        use_of = {step: uses for step, uses, _ in NUMBERED}
        latest_at = {step: latest for step, _, latest in NUMBERED}
        attn_parts = {s: n for n, s in enumerate(s for s in SCHEDULE if s[0] in ("s_out", "p_out"))}
        block = ctx.enter_context(nc.Block())

        @block.sync
        def _(sp):
            def load_weights(n):
                if n >= len(TILES):
                    return
                w = TILES[n]
                if n >= W_STAGE:
                    sp.wait_ge(w_lo_ready, n - W_STAGE + 1)
                src = t[w["weight"]][0, w["row0"]:w["row0"] + w["kt"] * P, w["col"]:w["col"] + P]
                sp.dma_start(w_stage[:, n % W_STAGE, 0:w["kt"], :],
                             src.rearrange("(k p) n -> p k n", p=P)).then_inc(w_loaded[n % W_STAGE], 16)

            def load_self(g, cache, kq):
                src = t["cache_k" if cache == "k" else "cache_v"]
                order = [(b, pg) for b in range(GB) for pg in range(2)]
                if cache == "v":
                    order = [(b, pg) for pg in range(2) for b in range(GB)]
                for b, pg in order:
                    n = self_page(g, cache, kq, b, pg)
                    before = n - PAGE_RING
                    if before < 0:
                        if n == 0:
                            sp.wait_ge(free["T1"], use_of["x_in", 4][1][1] + 1)
                            sp.wait_ge(free["T0"], use_of["x_in", 4][0][1] + 1)
                    else:
                        bg, rest = divmod(before, 2 * 4 * 8)
                        bc, rest = divmod(rest, 4 * 8)
                        bq, rest = divmod(rest, 8)
                        if bc == 0:
                            bb = rest // 2
                            use = use_of["k_turn", bg, bq, 1][bb]
                            sp.wait_ge(full[use[0]], use[1] + 1)
                        else:
                            sp.wait_ge(sem("v_pages_read"), (bg * 4 + bq) * 2 + rest // GB + 1)
                    slot = (4 * g + b) * NPAGES + 2 * kq + pg
                    phys = sp.value_load(page_ids[0:1, slot:slot + 1], min_val=0,
                                         max_val=src.shape[1] - 1)
                    sp.dma_start(page[:, n % PAGE_RING, :],
                                 src[0, bass.ds(phys, 1), :, :, :].rearrange("a r h d -> (a r) (h d)")
                                 ).then_inc(sem(f"page_loaded{n % PAGE_RING}"), 16)

            def load_cross(g, cache, kt):
                src = t["cache_mem_k" if cache == "k" else "cache_mem_v"]
                for b in range(GB):
                    n = cross_page(g, cache, kt, b)
                    before = n - GB
                    if before >= 0:
                        bg, bv, bk = before // 16, before // 8 % 2, before // 4 % 2
                        if not bv:
                            use = use_of["ck_turn", bg, bk, 1][b]
                            sp.wait_ge(full[use[0]], use[1] + 1)
                        elif bk == 0:
                            sp.wait_ge(sem("cv_pages_read"), bg + 1)
                        else:
                            use = use_of["cs_pv", bg, 1][1]
                            sp.wait_ge(full[use[0]], use[1] + 1)
                    sp.dma_start(c_pages[:, b, :],
                                 src[0, 4 * g + b, kt * P:(kt + 1) * P, :, :].rearrange("r h d -> r (h d)")
                                 ).then_inc(sem(f"c_page_loaded{b}"), 16)

            xp = t["x_prompt"][0].rearrange("(i p) c -> p i c", p=P)
            for i in range(4):
                sp.dma_start(x_tok[:, i, :], xp[:, i, :]).then_inc(sem(f"x_loaded{i}"), 16)
            sp.dma_start(x_tok_s[0:32, :], t["x_sample"].rearrange("b q c -> (b q) c")).then_inc(sem("x_loaded4"), 16)
            sp.dma_start(page_ids[:, :], t["page_table"].rearrange("(o b) n -> o (b n)", o=1)).then_inc(sem("ids_loaded"), 16)
            for n in range(4):
                load_weights(n)
            sp.wait_ge(sem("ids_loaded"), 16)
            self_loads = [(g, c, kq) for g in range(GROUPS) for c in ("k", "v") for kq in range(4)]
            cross_loads = [(g, c, kt) for g in range(GROUPS) for c in ("k", "v") for kt in range(2)]
            for step, uses, latest in NUMBERED:
                kind = step[0]
                if kind == "tile":
                    load_weights(step[1] + 4)
                    if step[1] == TILE["in", "q", 1]:
                        load_self(*self_loads.pop(0))
                    if step[1] == MEM_FIRST + 1:
                        sp.wait_ge(tile_done, MEM_FIRST + 1)
                        sp.wait_ge(sem("k_saved"), 128)
                        sp.wait_ge(sem("v_saved"), 32)
                        sp.wait_ge(sem("mix_saved"), 32)
                        load_cross(*cross_loads.pop(0))
                    if step[1] == CO_FIRST + 1:
                        sp.wait_ge(tile_done, CO_FIRST + 1)
                        sp.wait_ge(sem("mv_saved"), 16)
                        sp.wait_ge(sem("mk_saved0"), 16 * 4)
                        sp.wait_ge(sem("mk_saved1"), 16 * 4)
                        sp.dma_start(f_rows[0:16, :], t["state_conv_ffn"][0].rearrange("b w c -> (b w) c")
                                     ).then_inc(sem("f_rows_loaded"), 16)
                if (kind == "k_turn" and step[3] == 0) or kind == "s_pv":
                    if self_loads:
                        load_self(*self_loads.pop(0))
                if kind == "s_norm" and step[1] == 1:
                    use = use_of["k_score", 1, 3, 1][0]
                    sp.wait_ge(full[use[0]], use[1] + 1)
                    sp.dma_start(mem_tok, t["mem_prompt"][0].rearrange("(i p) c -> p i c", p=P)
                                 ).then_inc(sem("mem_loaded"), 16)
                if (kind == "ck_turn" and step[3] == 0) or kind == "cs_pv":
                    if cross_loads:
                        load_cross(*cross_loads.pop(0))

        @block.gpsimd
        def _(pool):
            pool.memset(rel[BUCKETS:BUCKETS + 1, :], NEG).then_inc(sem("rel_set"), 1)
            pool.wait_ge(sem("rel_set"), 1)
            pool.dma_start(ident[:, :], t["const_ident"]).then_inc(sem("ident_loaded"), 16)
            for row, name, n in ((V_MIX, "norm_mix_w", KT), (V_CROSS, "norm_cross_w", KT),
                                 (V_MEM, "norm_mem_w", KT), (V_FFN, "norm_ffn_w", KT)):
                pool.dma_start(packed[row:row + n, 0, :], t[name][0].rearrange("(k p) -> k p", p=P)
                               ).then_inc(sem("packed_loaded"), 16)
            pool.dma_start(packed[V_FINAL:V_FINAL + KT, 0, :], t["norm_final_w"].rearrange("(k p) -> k p", p=P)
                           ).then_inc(sem("packed_loaded"), 16)
            pool.dma_start(packed[V_CW:V_CW + 3 * CT, 0, :], t["conv_mix_w"][0].rearrange("w (k p) -> (w k) p", p=P)
                           ).then_inc(sem("packed_loaded"), 16)
            pool.dma_start(packed[V_CB:V_CB + CT, 0, :], t["conv_mix_b"][0].rearrange("(k p) -> k p", p=P)
                           ).then_inc(sem("packed_loaded"), 16)
            pool.dma_start(packed[V_SUB:V_SUB + 1, 0, :], t["subln_w"]).then_inc(sem("packed_loaded"), 16)
            fw = t["conv_ffn_w"][0].rearrange("w (k p) -> (w k) p", p=P)
            pool.dma_start(packed[0:88, 1, :], fw[0:88, :]).then_inc(sem("packed_loaded"), 16)
            pool.dma_start(packed[0:44, 2, :], fw[88:132, :]).then_inc(sem("packed_loaded"), 16)
            pool.dma_start(packed[44:88, 2, :], t["conv_ffn_b"][0].rearrange("(k p) -> k p", p=P)
                           ).then_inc(sem("packed_loaded"), 16)
            pool.dma_start(mix_in[0:16, :], t["state_conv_mix"][0].rearrange("b w c -> (b w) c")
                           ).then_inc(sem("packed_loaded"), 16)
            pool.memset(ones[:, :], 1.0).then_inc(sem("ones_set"), 1)
            pool.memset(eps[:, :], EPS).then_inc(sem("eps_set"), 1)
            pool.dma_start(onehot[0:BUCKETS + 1, :], t["const_onehot"]).then_inc(sem("bias_loaded"), 16)
            pool.dma_start(rel[0:BUCKETS, :], t["rel_bias"]).then_inc(sem("bias_loaded"), 16)
            pool.dma_start(row_cols[:, :], t["const_rows"]).then_inc(sem("rows_loaded"), 16)
            for j, name in enumerate(("lambda_q1", "lambda_k1", "lambda_q2", "lambda_k2")):
                ap = t[name]
                pool.dma_start(lams[:, j, :], bass.AP(ap.tensor, ap.offset, [[0, P], [1, DK]])
                               ).then_inc(sem("lams_loaded"), 16)
            pool.memset(q_rows[:, :, :, :], 0.0).then_inc(sem("q_rows_zero"), 1)
            pool.memset(new_bias[:, :, :], NEG).then_inc(sem("new_bias_neg"), 1)
            pool.memset(pre[:, 0:2], 0.0).then_inc(sem("pre_zero"), 1)

            kp = t["out_k_prompt"][0, 0].rearrange("(i p) h d -> p i h d", p=P)
            vp = t["out_v_prompt"][0, 0].rearrange("(i p) h d -> p i (h d)", p=P)
            ks = t["out_k_sample"][0].rearrange("b q h d -> (b q) h d")
            vs = t["out_v_sample"][0].rearrange("b q h d -> (b q) (h d)")
            mk = t["out_mem_k"][0, 0].rearrange("(i p) h d -> p i (h d)", p=P)
            mv = t["out_mem_v"][0, 0].rearrange("(i p) h d -> p i (h d)", p=P)
            for step, uses, latest in NUMBERED:
                kind, arg = step[0], step[1] if len(step) > 1 else None
                if kind == "bias":
                    sc = t["scratch_bias"]
                    wait_taken(pool, *uses[0])
                    pool.dma_start(sc, dist_vec[0:HEADS, :]).then_inc(sem("dist_saved"), 16)
                    pool.wait_ge(sem("dist_saved"), 16)
                    pool.dma_start(near_raw, bass.AP(sc.tensor, sc.offset, [[1, P], [DIST, HEADS], [1, 2 * P]])
                                   ).then_inc(sem("near_loaded"), 16)
                    for b in range(GB):
                        for c in range(2):
                            r = 32 * b + 16 * c
                            pool.dma_start(near_s_raw[r:r + 16, :],
                                           bass.AP(sc.tensor, sc.offset + DIST - 4 - 2 * P,
                                                   [[DIST, HEADS], [1, DEC_SEQ], [1, P + DEC_SEQ]])
                                           ).then_inc(sem("near_loaded"), 16)
                    pool.memset(s_keys[:, :, 16:32], 0.0).then_inc(sem("s_keys_zero"), 1)
                    pool.wait_ge(sem("near_ready"), 2)
                    pool.wait_ge(sem("new_bias_neg"), 1)
                    for g in range(GROUPS):
                        for b in range(GB):
                            if g or b:
                                pool.wait_ge(sem("new_bias_ready"), GB * g + b)
                            pool.tensor_copy(new_bias[32 * b:32 * b + 32, g, 16 * g + 4 * b:16 * g + 4 * b + 4],
                                             near_s[32 * b:32 * b + 32, P:P + DEC_SEQ]
                                             ).then_inc(sem("new_bias_ready"), 1)
                if kind == "q_blocks":
                    pool.wait_ge(sem("q_rows_zero"), 1)
                    for h in range(HEADS):
                        wait_tile_out(pool, TILE["in", "q", h])
                        for c in range(2):
                            rows = slice(DK * c, DK * c + DK)
                            lo = 16 * c + 4 * h
                            if h or c:
                                pool.wait_ge(sem("q_rows_ready"), 2 * h + c)
                            pool.tensor_copy(seqs(q_rows[rows, h, :, :], lo, lo + 4), samples(q_t[rows, h, :])
                                             ).then_inc(sem("q_rows_ready"), 1)
                if kind == "k_out":
                    wait_taken(pool, *uses[0])
                    pool.dma_start(kp[:, :, arg, :], k_out.rearrange("p (i d) -> p i d", d=P)
                                   ).then_inc(sem("k_saved"), 16)
                    wait_taken(pool, *uses[1])
                    pool.dma_start(ks[:, arg, :], k_out_s).then_inc(sem("k_saved"), 16)
                if kind == "v_out" and arg == HEADS - 1:
                    wait_taken(pool, *uses[0])
                    pool.dma_start(vp, v_tok[:, 0:4, :]).then_inc(sem("v_saved"), 16)
                    wait_taken(pool, *uses[1])
                    pool.dma_start(vs, v_tok[0:32, 4, :]).then_inc(sem("v_saved"), 16)
                if kind == "mem_in":
                    wait_taken(pool, *uses[4])
                    pool.dma_start(t["out_conv_mix_prompt"][0, 0], mix_out[0:2, :]).then_inc(sem("mix_saved"), 16)
                    pool.dma_start(t["out_conv_mix_sample"][0].rearrange("b w c -> (b w) c"), mix_out[2:18, :]
                                   ).then_inc(sem("mix_saved"), 16)
                if kind == "mem_out":
                    if arg < KT:
                        wait_taken(pool, *uses[0])
                        pool.dma_start(mk[:, :, arg * P:(arg + 1) * P], m_stage[:, arg % 2, :, :]
                                       ).then_inc(sem(f"mk_saved{arg % 2}"), 16)
                    if arg == 2 * KT - 1:
                        wait_taken(pool, *uses[0])
                        pool.dma_start(mv, mv_tok[:, :, :]).then_inc(sem("mv_saved"), 16)
                if kind == "tile" and arg == MEM_FIRST + 1:
                    pool.wait_ge(tile_done, MEM_FIRST + 1)
                    pool.wait_ge(sem("k_saved"), 128)
                    pool.wait_ge(sem("v_saved"), 32)
                    pool.wait_ge(sem("mix_saved"), 32)
                    pool.memset(qc_rows[:, :, :, :], 0.0).then_inc(sem("qc_rows_zero"), 1)
                if kind == "cq_blocks":
                    pool.wait_ge(sem("qc_rows_zero"), 1)
                    for d in range(KT):
                        wait_tile_out(pool, TILE["cq", "cq", d])
                        lo = 4 * (d // 2)
                        pool.tensor_copy(seqs(qc_rows[:, d, :, :], lo, lo + 4), samples(qc_t[:, d, :])
                                         ).then_inc(sem("qc_rows_ready"), 1)
                if kind == "tile" and arg == CO_FIRST + 1:
                    pool.wait_ge(tile_done, CO_FIRST + 1)
                    pool.wait_ge(sem("mv_saved"), 16)
                    pool.wait_ge(sem("mk_saved0"), 16 * 4)
                    pool.wait_ge(sem("mk_saved1"), 16 * 4)
                    pool.memset(up_pad[:, :, :, 0:2], 0.0).then_inc(sem("up_pad_zero"), 1)
                if kind == "ffn":
                    g, i = step[1:]
                    if i == 0:
                        wait_taken(pool, *use_of["state_in",][0])
                        wait_taken(pool, *use_of["state_in",][1])
                    for j in range(2):
                        if j == 0 and i >= 2:
                            pool.wait_ge(sem("conv_ffn_done"), 2 * (i - 2) + 2)
                        pool.tensor_copy(up_pad_s[:, j, i % 2, :, 0:2],
                                         f_prefix[:, j * FT + i, :].rearrange("p (b w) -> p b w", w=2)
                                         ).then_inc(sem("f_prefix_in"), 1)
                    for j, name in enumerate(("gate", "up")):
                        wait_tile_out(pool, TILE["up", name, i])
                        pool.tensor_copy(f_state[:, j * FT + i, 0:2], up_pad[:, j, i % 2, SEQ:SEQ + 2]
                                         ).then_inc(sem("f_state_ready"), 1)
                        pool.tensor_copy(f_state[:, j * FT + i, 2:18].rearrange("p (b w) -> p b w", w=2),
                                         up_pad_s[:, j, i % 2, :, DEC_SEQ:DEC_SEQ + 2]
                                         ).then_inc(sem("f_state_ready"), 1)
                if kind == "state_out" and arg == 2 * FT // 4 - 1:
                    wait_taken(pool, "T0", latest["T0"])
                    wait_taken(pool, "T1", latest["T1"])
                    pool.dma_start(t["out_conv_ffn_prompt"][0, 0], f_rows[0:2, :]).then_inc(sem("f_saved"), 16)
                    pool.dma_start(t["out_conv_ffn_sample"][0].rearrange("b w c -> (b w) c"), f_rows[2:18, :]
                                   ).then_inc(sem("f_saved"), 16)
                if kind == "final":
                    wait_taken(pool, *uses[0])
                    wait_taken(pool, *uses[1])
                    if arg < 4:
                        pool.dma_start(t["out_y_prompt"][0, arg * P:(arg + 1) * P, :], y_out[:, arg % 3, :]
                                       ).then_inc(sem(f"y_saved{arg % 3}"), 16)
                    else:
                        pool.dma_start(t["out_y_sample"].rearrange("b q c -> (b q) c"), y_out[0:32, arg % 3, :]
                                       ).then_inc(sem(f"y_saved{arg % 3}"), 16)
            for name, n in (("k_saved", 128), ("v_saved", 32), ("mix_saved", 32), ("mk_saved0", 64), ("mk_saved1", 64),
                            ("mv_saved", 16), ("f_saved", 32), ("y_saved0", 32), ("y_saved1", 32),
                            ("y_saved2", 16), ("dist_saved", 16)):
                pool.wait_ge(sem(name), n)

        @block.tensor
        def _(pe):
            def tile(n, latest):
                w = TILES[n]
                hi, lo = split[w["phase"]]
                pe.wait_ge(w_lo_ready, n + 1)
                if n >= 2:
                    wait_tile_out(pe, n - 2)
                width = HALF if w["phase"] != "mem" else N_MEM
                halves = 2 if w["phase"] != "mem" else 1
                slot = n % W_SPLIT
                for k in range(w["kt"]):
                    if w["first"]:
                        if w["phase"] in ready:
                            pe.wait_ge(ready[w["phase"]], k + 1)
                        elif w["phase"] == "out" and k < CT:
                            pe.wait_ge(sem("mixer_ready"), k + 1)
                        elif w["phase"] == "out" and k == CT:
                            wait_taken(pe, "T0", latest["T0"])
                        elif w["phase"] == "co" and k == 0:
                            for s in ("S1", "T0", "T1"):
                                wait_taken(pe, s, latest[s])
                        elif w["phase"].startswith("down"):
                            pe.wait_ge(sem("act_ready"), FFN_GROUPS[int(w["phase"][4:])][k] + 1)
                    for a, (wt, act) in enumerate(((w_hi, hi), (w_hi, lo), (w_lo, hi))):
                        for half in range(halves):
                            mm = pe.matmul(proj[n % 2][:, half, 0:width], wt[:, slot, k, :],
                                           act[:, k, half * HALF:half * HALF + width], start=(k == 0 and a == 0),
                                           stop=(k == w["kt"] - 1 and a == 2))
                mm.then_inc(tile_done, 1)

            def turn(use, parts):
                wait_empty(pe, use)
                for src, col in parts:
                    rows = src.shape[0]
                    width = int(np.prod(src.shape[1:]))
                    mm = pe.transpose(bank[use[0]][0:width, col:col + rows], src, ident[0:rows, 0:rows])
                mm.then_inc(full[use[0]], 1)

            for step, uses, latest in NUMBERED:
                kind, arg = step[0], step[1] if len(step) > 1 else None
                if kind == "setup":
                    pe.wait_ge(sem("ident_loaded"), 16)
                    pe.wait_ge(sem("packed_loaded"), 16 * 12)
                    turn(uses[0], [(packed[0:VEC_ROWS, 0, :], 0), (packed[0:88, 1, :], 64), (packed[0:88, 2, :], 152)])
                    turn(uses[1], [(mix_in[0:16, c * P:(c + 1) * P], 16 * c) for c in range(CT)])
                elif kind == "x_in":
                    pe.wait_ge(sem(f"x_loaded{arg}"), 16)
                    src = x_tok[:, arg, :] if arg < 4 else x_tok_s[0:32, :]
                    for j in range(2):
                        turn(uses[j], [(src[:, (4 * j + d) * P:(4 * j + d + 1) * P], d * P) for d in range(4)])
                elif kind == "norm":
                    m = norms.index(arg)
                    pe.wait_ge(sem("ones_set"), 1)
                    pe.wait_ge(sem("sums_added"), KT * (m + 1))
                    for half, use in enumerate(uses):
                        wait_empty(pe, use)
                        width = N_MEM if arg == "mem" else HALF
                        pe.matmul(bank[use[0]][:, 0:width], ones[:, :], sums[:, half * HALF:half * HALF + width],
                                  start=True, stop=True).then_inc(full[use[0]], 1)
                elif kind == "bias":
                    pe.wait_ge(sem("bias_loaded"), 32)
                    pe.wait_ge(sem("rel_set"), 1)
                    wait_empty(pe, uses[0])
                    pe.matmul(bank["S0"][0:HEADS, 0:DIST], rel[0:BUCKETS + 1, :], onehot[0:BUCKETS + 1, :],
                              start=True, stop=True).then_inc(full["S0"], 1)
                elif kind == "tile":
                    tile(arg, latest)
                elif kind in ("k_out", "v_out"):
                    wait_tile_out(pe, TILE["in", kind[0], arg])
                    if kind == "k_out":
                        turn(uses[0], [(block_cols(k_t, arg, i), i * P) for i in range(4)])
                        turn(uses[1], [(block_cols(k_t, arg, 4), 0)])
                    else:
                        turn(uses[0], [(block_cols(gates, arg % 2, i), i * P) for i in range(4)])
                        turn(uses[1], [(block_cols(gates, arg % 2, 4), 0)])
                elif kind == "k_turn":
                    g, kq, hp = step[1:]
                    for b in range(GB):
                        if hp == 0:
                            for pg in range(2):
                                n = self_page(g, "k", kq, b, pg)
                                pe.wait_ge(sem(f"page_loaded{n % PAGE_RING}"), 16 * (n // PAGE_RING + 1))
                        parts = []
                        for h2 in range(2):
                            for pg in range(2):
                                n = self_page(g, "k", kq, b, pg)
                                h = 2 * hp + h2
                                parts.append((page[:, n % PAGE_RING, h * P:(h + 1) * P], (2 * h2 + pg) * P))
                        turn(uses[b], parts)
                elif kind == "k_score":
                    g, kq, hp = step[1:]
                    if hp == 0:
                        pe.wait_ge(sem("q_rows_ready"), 2 * HEADS)
                        wait_empty(pe, uses[0])
                    wait_taken(pe, "T0", latest["T0"])
                    wait_taken(pe, "T1", latest["T1"])
                    for h2 in range(2):
                        h = 2 * hp + h2
                        for b in range(GB):
                            mm = pe.matmul(bank["S0"][32 * b:32 * b + 32, 0:2 * P], q_rows[:, h, GB * g + b, :],
                                           k_turned[:, b, h2 * 2 * P:(h2 + 1) * 2 * P],
                                           start=(h == 0), stop=(h == HEADS - 1), tile_position=(0, 32 * b))
                    if hp == 1:
                        mm.then_inc(full["S0"], 1)
                    if len(uses) > 1:
                        wait_empty(pe, uses[1])
                        for h in range(HEADS):
                            mm = pe.matmul(bank["S1"][:, 0:32],
                                           q_rows[:, h, GB * g:GB * g + GB, :].rearrange("p b r -> p (b r)"),
                                           k_t[:, h, HALF_P:HALF + HALF_S], start=(h == 0), stop=(h == HEADS - 1))
                        mm.then_inc(full["S1"], 1)
                elif kind == "s_turn":
                    pe.wait_ge(sem("s_prob"), arg + 1)
                    turn(uses[0], [(s_sb[:, j * P:(j + 1) * P], j * P) for j in range(4)])
                    turn(uses[1], [(s_sb[:, (4 + j) * P:(5 + j) * P], j * P) for j in range(4)])
                    turn(uses[2], [(s_sb[:, PAST:PAST + 32], 0)])
                elif kind == "s_pv":
                    g, kq = step[1:]
                    if kq == 0:
                        wait_empty(pe, uses[0])
                        wait_taken(pe, *use_of["s_turn", g][1])
                        wait_taken(pe, *use_of["s_turn", g][2])
                        pe.wait_ge(sem("s_keys_zero"), 1)
                    for pg in range(2):
                        for b in range(GB):
                            n = self_page(g, "v", kq, b, pg)
                            pe.wait_ge(sem(f"page_loaded{n % PAGE_RING}"), 16 * (n // PAGE_RING + 1))
                            mm = pe.matmul(bank["S1"][32 * b:32 * b + 32, :], s_keys[:, (2 * kq + pg) * GB + b, :],
                                           page[:, n % PAGE_RING, :], start=(kq == 0 and pg == 0), stop=False,
                                           tile_position=(0, 32 * b))
                        mm.then_inc(sem("v_pages_read"), 1)
                elif kind == "s_new":
                    use = use_of["v_out", HEADS - 1][1]
                    wait_taken(pe, *use)
                    for b in range(GB):
                        mm = pe.matmul(bank["S1"][32 * b:32 * b + 32, :], s_keys[0:32, 8 * GB + b, :],
                                       v_tok[0:32, 4, :], start=False, stop=True, tile_position=(0, 32 * b))
                    mm.then_inc(full["S1"], 1)
                elif kind == "s_out":
                    wait_taken(pe, *use_of["s_norm", arg][0])
                    turn(uses[0], [(o_sb[:, h * P:(h + 1) * P], h * P) for h in range(HEADS)])
                elif kind == "p_score":
                    i, h = step[1:]
                    if h == 0 and i == 0:
                        for hh in range(HEADS):
                            wait_tile_out(pe, TILE["in", "k", hh])
                    for c in range(2):
                        wait_empty(pe, uses[c])
                        rows = slice(DK * c, DK * c + DK)
                        done = 0
                        while done < (i + 1) * P:
                            half = done // HALF_P
                            width = min((i + 1) * P - done, HALF_P)
                            mm = pe.matmul(bank[uses[c][0]][:, done:done + width], block_cols(q_t[rows, :, :], h, i),
                                           k_t[rows, h, BLOCK[2 * half]:BLOCK[2 * half] + width],
                                           start=True, stop=True)
                            done += width
                        mm.then_inc(full[uses[c][0]], 1)
                elif kind == "p_turn":
                    i, h = step[1:]
                    u = i * HEADS + h
                    pe.wait_ge(sem("p_prob"), u + 1)
                    turn(uses[0], [(p_exp[:, u % 2, 0, j * P:(j + 1) * P], j * P) for j in range(i + 1)])
                elif kind == "p_pv":
                    i, h = step[1:]
                    u = i * HEADS + h
                    if h == 0:
                        wait_empty(pe, uses[0])
                    wait_taken(pe, *use_of["p_turn", i, h][0])
                    if u == 0:
                        wait_taken(pe, *use_of["v_out", HEADS - 1][0])
                    for j in range(i + 1):
                        mm = pe.matmul(bank["T1"][:, h * P:(h + 1) * P], p_keys[:, u % 2, j, :],
                                       v_tok[:, j, h * P:(h + 1) * P], start=(j == 0), stop=(j == i))
                    if h == HEADS - 1:
                        mm.then_inc(full["T1"], 1)
                elif kind == "p_out":
                    wait_taken(pe, *use_of["p_norm", arg][0])
                    turn(uses[0], [(o_blk[:, h * P:(h + 1) * P], h * P) for h in range(HEADS)])
                elif kind == "mem_in":
                    pe.wait_ge(sem("mem_loaded"), 16)
                    for i in range(2):
                        for j in range(2):
                            turn(uses[2 * i + j], [(mem_tok[:, i, (4 * j + d) * P:(4 * j + d + 1) * P], d * P)
                                                   for d in range(4)])
                    pe.wait_ge(sem("mixer_ready"), CT)
                    turn(uses[4], [(mix_state[:, c, :], 0 + c * P) for c in range(CT)])
                elif kind == "mem_out":
                    wait_tile_out(pe, TILE["mem", "mem", arg])
                    src = mk_t[:, arg, :] if arg < KT else mv_t[:, arg % 2, :]
                    turn(uses[0], [(src[:, i * P:(i + 1) * P], i * P) for i in range(2)])
                elif kind == "c_score":
                    hp, i = step[1:]
                    if hp == 0 and i == 0:
                        for d in (KT - 2, KT - 1):
                            wait_tile_out(pe, TILE["cq", "cq", d])
                        wait_taken(pe, *use_of["mem_out", 2 * KT - 1][0])
                    wait_empty(pe, uses[0])
                    for h2 in range(2):
                        for d in range(2):
                            mm = pe.matmul(bank["S1"][:, h2 * N_MEM:(h2 + 1) * N_MEM],
                                           block_cols(qc_t, 2 * (2 * hp + h2) + d, i),
                                           mk_t[:, 2 * (2 * hp + h2) + d, :], start=(d == 0), stop=(d == 1))
                    mm.then_inc(full["S1"], 1)
                elif kind == "c_turn":
                    hp, i = step[1:]
                    v = 4 * hp + i
                    pe.wait_ge(sem("c_prob"), v + 1)
                    turn(uses[0], [(c_exp[:, v % 2, h2, kt * P:(kt + 1) * P], (2 * h2 + kt) * P)
                                   for h2 in range(2) for kt in range(2)])
                elif kind == "c_pv":
                    wait_taken(pe, *use_of["c_turn", 1, 3][0])
                    wait_empty(pe, uses[0])
                    for kt in range(2):
                        mm = pe.matmul(bank["S1"], mv_tok[:, kt, arg * P:(arg + 1) * P], c_keys[:, arg // 2 * 2 + kt, :],
                                       start=(kt == 0), stop=(kt == 1))
                    mm.then_inc(full["S1"], 1)
                elif kind == "ck_turn":
                    g, kt, dh = step[1:]
                    for b in range(GB):
                        n = cross_page(g, "k", kt, b)
                        pe.wait_ge(sem(f"c_page_loaded{b}"), 16 * (n // GB + 1))
                        turn(uses[b], [(c_pages[:, b, (4 * dh + d) * P:(4 * dh + d + 1) * P], d * P) for d in range(4)])
                elif kind == "ck_score":
                    g, kt, dh = step[1:]
                    if dh == 0:
                        pe.wait_ge(sem("qc_rows_ready"), KT)
                        wait_empty(pe, uses[0])
                    wait_taken(pe, "T0", latest["T0"])
                    wait_taken(pe, "T1", latest["T1"])
                    for d in range(4):
                        for b in range(GB):
                            mm = pe.matmul(bank["S0"][32 * b:32 * b + 32, 0:P], qc_rows[:, 4 * dh + d, GB * g + b, :],
                                           c_turned[:, b, d * P:(d + 1) * P], start=(dh == 0 and d == 0),
                                           stop=(dh == 1 and d == 3), tile_position=(0, 32 * b))
                    if dh == 1:
                        mm.then_inc(full["S0"], 1)
                elif kind == "cs_turn":
                    pe.wait_ge(sem("cs_prob"), arg + 1)
                    turn(uses[0], [(c_s[:, kt * P:(kt + 1) * P], kt * P) for kt in range(2)])
                elif kind == "cs_pv":
                    g, kt = step[1:]
                    if kt == 0:
                        wait_empty(pe, uses[0])
                        wait_empty(pe, uses[1])
                        wait_taken(pe, *use_of["cs_turn", g][0])
                    for half in range(2):
                        for b in range(GB):
                            n = cross_page(g, "v", kt, b)
                            if half == 0:
                                pe.wait_ge(sem(f"c_page_loaded{b}"), 16 * (n // GB + 1))
                            mm = pe.matmul(bank[uses[half][0]][32 * b:32 * b + 32, :], cs_keys[:, kt, 32 * b:32 * b + 32],
                                           c_pages[:, b, half * 512:(half + 1) * 512], start=(kt == 0), stop=(kt == 1),
                                           tile_position=(0, 32 * b))
                        if kt == 1:
                            mm.then_inc(full[uses[half][0]], 1)
                    if kt == 0:
                        mm.then_inc(sem("cv_pages_read"), 1)
                elif kind == "cs_out":
                    wait_taken(pe, *uses[0])
                    wait_taken(pe, *uses[1])
                    for j in range(2):
                        turn(uses[2 + j], [(o_cross[:, (4 * j + d) * P:(4 * j + d + 1) * P], d * P) for d in range(4)])
                elif kind == "state_in":
                    pe.wait_ge(sem("f_rows_loaded"), 16)
                    for j in range(2):
                        turn(uses[j], [(f_rows[0:16, (FT * j + i) * P:(FT * j + i + 1) * P], 16 * i) for i in range(FT)])
                elif kind == "state_out":
                    pe.wait_ge(sem("f_state_ready"), 4 * FT)
                    turn(uses[0], [(f_state[:, 4 * arg + m, :], m * P) for m in range(4)])
                elif kind == "final":
                    pe.wait_ge(ready["final"], KT)
                    for j in range(2):
                        turn(uses[j], [(block_cols(x, 4 * j + d, arg), d * P) for d in range(4)])

        @block.scalar
        def _(act):
            chain = [0]
            squares = [0]

            def done(ins):
                chain[0] += 1
                ins.then_inc(sem("act_step"), 1)
                act.wait_ge(sem("act_step"), chain[0])

            def split_hi(n):
                if n >= len(TILES):
                    return
                kt = TILES[n]["kt"]
                act.wait_ge(w_loaded[n % W_STAGE], 16 * (n // W_STAGE + 1))
                if n >= W_SPLIT:
                    act.wait_ge(tile_done, n - W_SPLIT + 1)
                act.activation(w_hi[:, n % W_SPLIT, 0:kt, :], w_stage[:, n % W_STAGE, 0:kt, :],
                               ACT.Copy).then_inc(w_hi_ready, 1)

            def rstd_of(out, in_, width_scale):
                done(act.activation(out, in_, ACT.Ln, bias=eps[0:out.shape[0], 0:1], scale=width_scale))
                return act.activation(out, out, ACT.Exp, scale=-0.5)

            for step, uses, latest in NUMBERED:
                kind, arg = step[0], step[1] if len(step) > 1 else None
                if kind == "setup":
                    wait_full(act, uses[0])
                    act.activation(vec[:, :], bank["T0"][:, 0:VEC_ROWS], ACT.Copy).then_inc(sem("vec_ready"), 1)
                    act.activation(fvec[:, :], bank["T0"][:, 64:64 + 8 * FT], ACT.Copy).then_inc(free["T0"], 1)
                    wait_full(act, uses[1])
                    act.activation(mix_prefix[:, :], bank["T1"][:, 0:CT * 16], ACT.Copy).then_inc(free["T1"], 1)
                    act.wait_ge(sem("lam_dots"), 2)
                    act.activation(small[:, 42:44], small[:, 40:42], ACT.Exp).then_inc(sem("lam_exp"), 1)
                    split_hi(0)
                    split_hi(1)
                elif kind == "x_in":
                    wait_full(act, uses[0])
                    if arg < 4:
                        act.activation(x[:, 0:4, BLOCK[arg]:BLOCK[arg] + P], quads["T0"], ACT.Copy
                                       ).then_inc(free["T0"], 1)
                    else:
                        act.activation(x[:, 0:4, HALF_P:HALF + HALF_S],
                                       quads["T0"][:, :, 0:32], ACT.Copy
                                       ).then_inc(free["T0"], 1)
                elif kind == "squares":
                    q = squares[0]
                    squares[0] += 1
                    if q >= 2:
                        act.wait_ge(sem("sums_added"), q - 1)
                    if q // KT == norms.index("in"):
                        wait_taken(act, *use_of["x_in", 4][0])
                        wait_taken(act, *use_of["x_in", 4][1])
                    elif step[2] == "mem":
                        wait_taken(act, *use_of["mem_in",][2])
                        wait_taken(act, *use_of["mem_in",][3])
                        act.wait_ge(sem("mixer_ready"), CT)
                        act.wait_ge(full["T0"], use_of["s_out", 1][0][1] + 1)
                    else:
                        phase = {"cq": "out", "up": "co", "final": "down2"}[norms[q // KT]]
                        wait_tile_out(act, TILE[phase, "add", step[1]])
                    if step[2] == "mem":
                        act.activation(square[:, q % 2, 0:N_MEM], mem_t[:, step[1], :], ACT.Square
                                       ).then_inc(sem("squared"), 1)
                    else:
                        act.activation(square[:, q % 2, :], x[:, step[1], :], ACT.Square
                                       ).then_inc(sem("squared"), 1)
                elif kind == "norm":
                    m = norms.index(arg)
                    act.wait_ge(sem("eps_set"), 1)
                    width = N_MEM if arg == "mem" else HALF
                    for half, use in enumerate(uses):
                        wait_full(act, use)
                        act.activation(rstd[:, half * HALF:half * HALF + width], bank[use[0]][:, 0:width], ACT.Ln,
                                       bias=eps[:, 0:1], scale=1.0 / D_MODEL).then_inc(free[use[0]], 1)
                    for half, use in enumerate(uses):
                        wait_taken(act, *use)
                        act.activation(rstd[:, half * HALF:half * HALF + width],
                                       rstd[:, half * HALF:half * HALF + width], ACT.Exp, scale=-0.5
                                       ).then_inc(sem("rstd_ready"), 1)
                    if arg != "final":
                        hi = split[arg][0]
                        for k in range(KT):
                            act.wait_ge(sem("normed_ready"), KT * m + k + 1)
                            if arg == "mem":
                                act.activation(hi[:, k, 0:N_MEM], normed[:, k % 3, 0:N_MEM], ACT.Copy
                                               ).then_inc(sem("normed_hi"), 1)
                            else:
                                act.activation(hi[:, k, :], normed[:, k % 3, :], ACT.Copy
                                               ).then_inc(sem("normed_hi"), 1)
                elif kind == "bias":
                    wait_full(act, uses[0])
                    act.wait_ge(ready["in"], KT)
                    act.activation(dist_vec[0:HEADS, :], bank["S0"][0:HEADS, 0:DIST], ACT.Copy).then_inc(free["S0"], 1)
                elif kind == "tile":
                    split_hi(arg + 2)
                    w = TILES[arg]
                    out = proj[arg % 2][:, :, :]
                    if w["kind"] in ("add", "u"):
                        continue
                    act.wait_ge(tile_done, arg + 1)
                    if w["kind"] == "q":
                        act.activation(halves(q_t[:, w["i"], :]), out[:, :, 0:HALF], ACT.Copy, scale=DK ** -0.5
                                       ).then_inc(tile_out[arg % 2], 1)
                    elif w["kind"] == "k":
                        act.activation(halves(k_t[:, w["i"], :]), out[:, :, 0:HALF], ACT.Copy).then_inc(tile_out[arg % 2], 1)
                    elif w["kind"] == "v":
                        act.activation(halves(gates[:, w["i"] % 2, :]), out[:, :, 0:HALF], ACT.Copy
                                       ).then_inc(tile_out[arg % 2], 1)
                    elif w["kind"] in ("gb", "gc"):
                        if w["i"]:
                            act.wait_ge(sem("mixer_ready"), w["i"])
                        act.activation(halves(gates[:, int(w["kind"] == "gc"), :]), out[:, :, 0:HALF], ACT.Copy
                                       ).then_inc(tile_out[arg % 2], 1)
                    elif w["kind"] == "mem":
                        if w["i"] == 0:
                            act.wait_ge(sem("k_saved"), 128)
                            act.wait_ge(sem("v_saved"), 32)
                            act.wait_ge(sem("mix_saved"), 32)
                        dst = mk_t[:, w["i"], :] if w["i"] < KT else mv_t[:, w["i"] % 2, :]
                        act.activation(dst, out[:, 0, 0:N_MEM], ACT.Copy).then_inc(tile_out[arg % 2], 1)
                    elif w["kind"] == "cq":
                        act.activation(halves(qc_t[:, w["i"], :]), out[:, :, 0:HALF], ACT.Copy, scale=MEM_DH ** -0.5
                                       ).then_inc(tile_out[arg % 2], 1)
                    elif w["kind"] in ("gate", "up"):
                        j, i = int(w["kind"] == "up"), w["i"]
                        if i >= 2:
                            act.wait_ge(sem("conv_ffn_done"), 2 * (i - 2) + 1 + j)
                            act.wait_ge(sem("f_state_ready"), 4 * (i - 2) + 2 * j + 2)
                        if i < 2:
                            act.wait_ge(sem("f_rows_loaded"), 16)
                        act.activation(by_half(up_pad[:, j, i % 2, 2:2 + SEQ]), prompt_of(out), ACT.Copy
                                       ).then_inc(sem("act_side"), 1)
                        act.activation(seqs(up_pad_s[:, j, i % 2, :, :], 2, 6), samples_of(out), ACT.Copy
                                       ).then_inc(tile_out[arg % 2], 1)
                elif kind == "k_out":
                    wait_full(act, uses[1])
                    if arg:
                        act.wait_ge(sem("k_saved"), 32 * arg)
                    act.activation(k_out_s, bank["T1"][0:32, 0:P], ACT.Copy).then_inc(free["T1"], 1)
                elif kind == "v_out":
                    wait_full(act, uses[1])
                    act.activation(v_tok[0:32, 4, arg * P:(arg + 1) * P], bank["T1"][0:32, 0:P], ACT.Copy
                                   ).then_inc(free["T1"], 1)
                elif kind == "k_turn":
                    for b in (0, 2):
                        wait_full(act, uses[b])
                        act.activation(k_turned[:, b, :], bank["T0"], ACT.Copy).then_inc(free["T0"], 1)
                elif kind == "s_soft":
                    act.wait_ge(sem("s_max"), arg + 1)
                    act.activation(s_sb, s_sb, ACT.Exp, bias=small[:, 0:1], accum_out=small[:, 1:2]
                                   ).then_inc(sem("s_exp"), 1)
                elif kind == "s_norm":
                    wait_full(act, uses[0])
                    act.wait_ge(sem("k_saved"), 128)
                    for h in range(HEADS):
                        cols = slice(h * P, (h + 1) * P)
                        ins = act.activation(o_sb[:, cols], bank["S1"][:, cols], ACT.Square,
                                             scale=row_cols[:, h:h + 1], accum_out=small[:, 4 + h:5 + h])
                        ins.then_inc(sem("s_squares"), 1)
                    act.wait_ge(sem("s_sum"), arg + 1)
                    rstd_of(small[:, 9:10], small[:, 8:9], 1.0 / DV).then_inc(sem("s_rstd"), 1)
                    act.wait_ge(sem("s_row_scale"), arg + 1)
                    for h in range(HEADS):
                        cols = slice(h * P, (h + 1) * P)
                        ins = act.activation(o_sb[:, cols], bank["S1"][:, cols], ACT.Copy, scale=small[:, 10 + h:11 + h])
                        ins.then_inc(sem("act_side") if h < HEADS - 1 else free["S1"], 1)
                elif kind in ("s_out", "p_out"):
                    wait_full(act, uses[0])
                    if kind == "s_out":
                        act.activation(b_hi[:, 4:8, HALF_P + HALF_S * arg:HALF + HALF_S * arg].rearrange("p h (b q) -> p h b q", q=DEC_SEQ),
                                       head_rows("T0", P + 4, 0, HEADS), ACT.Copy, scale=sub_w[:, 0:1]
                                       ).then_inc(sem("attn_hi"), 1)
                    else:
                        act.activation(b_hi[:, 4:8, BLOCK[arg]:BLOCK[arg] + P], quads["T0"],
                                       ACT.Copy, scale=sub_w[:, 0:1]).then_inc(sem("attn_hi"), 1)
                elif kind == "p_score":
                    i, h = step[1:]
                    u = i * HEADS + h
                    act.wait_ge(sem("p_max"), u + 1)
                    for c in range(2):
                        act.activation(p_exp[:, u % 2, c, 0:(i + 1) * P], bank[uses[c][0]][:, 0:(i + 1) * P], ACT.Exp,
                                       bias=small[:, 16 + 2 * (u % 2) + c:17 + 2 * (u % 2) + c],
                                       accum_out=small[:, 20 + 2 * (u % 2) + c:21 + 2 * (u % 2) + c]
                                       ).then_inc(free[uses[c][0]], 1)
                elif kind == "p_turn":
                    i, h = step[1:]
                    u = i * HEADS + h
                    wait_full(act, uses[0])
                    act.activation(p_keys[:, u % 2, 0:i + 1, :], quads["T0"][:, 0:i + 1, :], ACT.Copy
                                   ).then_inc(free["T0"], 1)
                elif kind == "p_norm":
                    wait_full(act, uses[0])
                    for h in range(HEADS):
                        cols = slice(h * P, (h + 1) * P)
                        ins = act.activation(o_sq[:, cols], bank["T1"][:, cols], ACT.Square,
                                             accum_out=small[:, 28 + h:29 + h])
                        if h < HEADS - 1:
                            ins.then_inc(sem("act_side"), 1)
                        else:
                            done(ins)
                    done(rstd_of(small[:, 32:36], small[:, 28:32], 1.0 / DV))
                    for h in range(HEADS):
                        cols = slice(h * P, (h + 1) * P)
                        act.activation(o_blk[:, cols], bank["T1"][:, cols], ACT.Copy, scale=small[:, 32 + h:33 + h]
                                       ).then_inc(sem("act_side") if h < HEADS - 1 else free["T1"], 1)
                elif kind == "conv":
                    act.wait_ge(sem("mixed"), arg + 1)
                    act.activation(b_hi[:, arg, :], gates[:, 1, :], ACT.Copy).then_inc(sem("mixed_hi"), 1)
                elif kind == "mem_in":
                    for i in range(2):
                        wait_full(act, uses[2 * i])
                        act.activation(mem_t[:, 0:4, i * P:(i + 1) * P], quads["T0"], ACT.Copy).then_inc(free["T0"], 1)
                    wait_full(act, uses[4])
                    act.activation(mix_out[0:18, :], bank["S0"][0:18, :], ACT.Copy).then_inc(free["S0"], 1)
                elif kind == "mem_out":
                    wait_full(act, uses[0])
                    src = bank["T0"][:, 0:N_MEM].rearrange("p (i c) -> p i c", c=P)
                    if arg < KT:
                        if arg >= 2:
                            act.wait_ge(sem(f"mk_saved{arg % 2}"), 16 * (arg // 2))
                        act.activation(m_stage[:, arg % 2, :, :], src, ACT.Copy).then_inc(free["T0"], 1)
                    else:
                        act.activation(mv_tok[:, :, (arg - KT) * P:(arg - KT + 1) * P], src, ACT.Copy
                                       ).then_inc(free["T0"], 1)
                elif kind == "c_score":
                    v = 4 * step[1] + step[2]
                    act.wait_ge(sem("c_max"), v + 1)
                    for h2 in range(2):
                        col = 2 * (v % 2) + h2
                        act.activation(c_exp[:, v % 2, h2, :], bank["S1"][:, h2 * N_MEM:(h2 + 1) * N_MEM], ACT.Exp,
                                       bias=c_small[:, col:col + 1], accum_out=c_small[:, 4 + col:5 + col]
                                       ).then_inc(sem("act_side") if h2 == 0 else free["S1"], 1)
                elif kind == "c_pv":
                    wait_full(act, uses[0])
                    act.activation(prompt(a_hi[:, arg, :]), by_half(bank["S1"]), ACT.Copy).then_inc(sem("cross_hi"), 1)
                elif kind == "ck_turn":
                    for b in (0, 2):
                        wait_full(act, uses[b])
                        act.activation(c_turned[:, b, :], bank["T0"], ACT.Copy).then_inc(free["T0"], 1)
                elif kind == "cs_soft":
                    act.wait_ge(sem("cs_max"), arg + 1)
                    act.activation(c_s, c_s, ACT.Exp, bias=c_small[:, 16:17], accum_out=c_small[:, 17:18]
                                   ).then_inc(sem("cs_exp"), 1)
                elif kind == "cs_turn":
                    wait_full(act, uses[0])
                    act.activation(cs_keys, bank["T0"][:, 0:N_MEM].rearrange("p (i c) -> p i c", c=P), ACT.Copy
                                   ).then_inc(free["T0"], 1)
                elif kind == "cs_out":
                    wait_full(act, uses[0])
                    ins = act.activation(o_cross[:, 0:512], bank["S0"], ACT.Copy)
                    ins.then_inc(free["S0"], 1)
                    for j in range(2):
                        wait_full(act, uses[2 + j])
                        for h2 in range(2):
                            h = 2 * j + h2
                            act.activation(a_hi[:, 2 * h:2 * h + 2, HALF_P + HALF_S * arg:HALF + HALF_S * arg].rearrange("p d (b q) -> p d b q", q=DEC_SEQ),
                                           head_rows(uses[2 + j][0], P, h2 * 2 * P + 4 * h, 2), ACT.Copy
                                           ).then_inc(sem("cs_hi"), 1)
                elif kind == "state_in":
                    wait_full(act, uses[0])
                    act.activation(f_prefix[:, 0:FT, :], bank["T0"][:, 0:FT * 16].rearrange("p (i c) -> p i c", c=16),
                                   ACT.Copy).then_inc(free["T0"], 1)
                elif kind == "ffn":
                    g, i = step[1:]
                    act.wait_ge(sem("conv_ffn_done"), 2 * i + 1)
                    act.activation(conv[:, 0, :], conv[:, 0, :], ACT.Silu).then_inc(sem("silu_done"), 1)
                    act.wait_ge(sem("gated"), i + 1)
                    if i == FFN_GROUPS[g][0]:
                        last = TILE["co", "add", KT - 1] if g == 0 else TILE[f"down{g - 1}", "add", KT - 1]
                        act.wait_ge(tile_done, last + 1)
                    act.activation(a_hi[:, i - FFN_GROUPS[g][0], :], conv[:, 1, :], ACT.Copy
                                   ).then_inc(sem("act_hi"), 1)
                elif kind == "state_out":
                    if arg % 2 == 0:
                        wait_full(act, uses[0])
                        act.activation(f_rows[0:18, arg * 512:(arg + 1) * 512], bank["T0"][0:18, :], ACT.Copy
                                       ).then_inc(free["T0"], 1)
                elif kind == "final":
                    wait_full(act, uses[0])
                    if arg >= 3:
                        act.wait_ge(sem(f"y_saved{arg % 3}"), 16)
                    rows = P if arg < 4 else 32
                    act.activation(y_out[0:rows, arg % 3, 0:512], bank["T0"][0:rows, :], ACT.Copy).then_inc(free["T0"], 1)

        @block.vector
        def _(dve):
            chain = [0]
            squares = [0]

            def done(ins):
                chain[0] += 1
                ins.then_inc(sem("dve_step"), 1)
                dve.wait_ge(sem("dve_step"), chain[0])

            def side(ins):
                chain[0] += 1
                ins.then_inc(sem("dve_step"), 1)

            def settle():
                dve.wait_ge(sem("dve_step"), chain[0])

            def split_lo(n):
                if n >= len(TILES):
                    return
                kt = TILES[n]["kt"]
                dve.wait_ge(w_hi_ready, n + 1)
                dve.tensor_tensor(w_lo[:, n % W_SPLIT, 0:kt, :], w_stage[:, n % W_STAGE, 0:kt, :],
                                  w_hi[:, n % W_SPLIT, 0:kt, :].bitcast(F32), ALU.subtract).then_inc(w_lo_ready, 1)

            def conv3(pads, outs, cols):
                w, b = cols[0:3], cols[3]
                (pp, ps), (op, os) = pads, outs
                side(dve.tensor_scalar(op, by_half(pp[:, 0:SEQ]), w[0], b, ALU.mult, ALU.add))
                done(dve.tensor_scalar(os, seqs(ps, 0, 4), w[0], b, ALU.mult, ALU.add))
                side(dve.scalar_tensor_tensor(out=op, in0=by_half(pp[:, 1:1 + SEQ]), scalar=w[1], in1=op,
                                              op0=ALU.mult, op1=ALU.add))
                done(dve.scalar_tensor_tensor(out=os, in0=seqs(ps, 1, 5), scalar=w[1], in1=os,
                                              op0=ALU.mult, op1=ALU.add))
                side(dve.scalar_tensor_tensor(out=op, in0=by_half(pp[:, 2:2 + SEQ]), scalar=w[2], in1=op,
                                              op0=ALU.mult, op1=ALU.add))
                return dve.scalar_tensor_tensor(out=os, in0=seqs(ps, 2, 6), scalar=w[2], in1=os,
                                                op0=ALU.mult, op1=ALU.add)

            for step, uses, latest in NUMBERED:
                kind, arg = step[0], step[1] if len(step) > 1 else None
                if kind == "setup":
                    dve.wait_ge(sem("lams_loaded"), 64)
                    for j in range(2):
                        dve.tensor_tensor_reduce(lams[:, 2 * j, :], lams[:, 2 * j, :], lams[:, 2 * j + 1, :], 1.0, 0.0,
                                                 ALU.mult, ALU.add, small[:, 40 + j:41 + j]).then_inc(sem("lam_dots"), 1)
                    dve.wait_ge(sem("lam_exp"), 1)
                    done(dve.tensor_tensor(small[:, 44:45], small[:, 43:44], small[:, 42:43], ALU.subtract))
                    done(dve.tensor_scalar(neg_lam[:, :], small[:, 44:45], -LAM_INIT, None, ALU.add))
                    dve.wait_ge(sem("rows_loaded"), 16)
                    done(dve.tensor_scalar(lam_row[:, :], neg_lam[:, :], -1.0, None, ALU.add))
                    done(dve.tensor_scalar(lam_row[:, :], lam_row[:, :], row_cols[:, 4:5], 1.0, ALU.mult, ALU.add))
                    dve.wait_ge(sem("vec_ready"), 1)
                    done(dve.tensor_scalar(sub_w[:, :], vec[:, V_SUB:V_SUB + 1], 1.0 - LAM_INIT, None, ALU.mult))
                    split_lo(0)
                    split_lo(1)
                elif kind == "x_in":
                    wait_full(dve, uses[1])
                    if arg < 4:
                        dve.tensor_copy(x[:, 4:8, BLOCK[arg]:BLOCK[arg] + P], quads["T1"]
                                        ).then_inc(free["T1"], 1)
                    else:
                        dve.tensor_copy(x[:, 4:8, HALF_P:HALF + HALF_S],
                                        quads["T1"][:, :, 0:32]
                                        ).then_inc(free["T1"], 1)
                elif kind == "squares":
                    q = squares[0]
                    squares[0] += 1
                    dve.wait_ge(sem("squared"), q + 1)
                    mem = step[2] == "mem"
                    total = sums[:, 0:N_MEM] if mem else sums
                    new = square[:, q % 2, 0:N_MEM] if mem else square[:, q % 2, :]
                    if q % KT == 0:
                        if q:
                            use = use_of["norm", norms[q // KT - 1]][-1]
                            dve.wait_ge(full[use[0]], use[1] + 1)
                        dve.tensor_copy(total, new).then_inc(sem("sums_added"), 1)
                    else:
                        dve.wait_ge(sem("sums_added"), q)
                        dve.tensor_tensor(total, total, new, ALU.add).then_inc(sem("sums_added"), 1)
                elif kind == "norm":
                    m = norms.index(arg)
                    mem = arg == "mem"
                    n_rstd = sum(1 if s == "mem" else 2 for s in norms[:m + 1])
                    dve.wait_ge(sem("rstd_ready"), n_rstd)
                    dve.wait_ge(sem("vec_ready"), 1)
                    if arg in ("mem", "up"):
                        dve.wait_ge(tile_done, {"mem": IN_LAST, "up": CO_FIRST}[arg] + 1)
                    if arg == "cq":
                        dve.wait_ge(tile_done, MEM_FIRST)

                    def scaled(k):
                        w = vec[:, norm_w[arg] + k:norm_w[arg] + k + 1]
                        src = mem_t[:, k, :] if mem else x[:, k, :]
                        dst = normed[:, k % 3, 0:N_MEM] if mem else normed[:, k % 3, :]
                        r = rstd[:, 0:N_MEM] if mem else rstd
                        if arg == "final":
                            dst = src
                        return dve.scalar_tensor_tensor(out=dst, in0=src, scalar=w, in1=r, op0=ALU.mult, op1=ALU.mult)

                    def low(k):
                        dve.wait_ge(sem("normed_hi"), KT * m + k + 1)
                        hi, lo = split[arg]
                        if mem:
                            dve.tensor_tensor(lo[:, k, 0:N_MEM], normed[:, k % 3, 0:N_MEM],
                                              hi[:, k, 0:N_MEM].bitcast(F32), ALU.subtract).then_inc(ready[arg], 1)
                        else:
                            dve.tensor_tensor(lo[:, k, :], normed[:, k % 3, :], hi[:, k, :].bitcast(F32),
                                              ALU.subtract).then_inc(ready[arg], 1)

                    for k in range(KT):
                        if arg == "final":
                            scaled(k).then_inc(ready["final"], 1)
                            continue
                        if k >= 3:
                            dve.wait_ge(ready[arg], k - 2)
                        scaled(k).then_inc(sem("normed_ready"), 1)
                        if k:
                            low(k - 1)
                    if arg != "final":
                        low(KT - 1)
                elif kind == "bias":
                    dve.wait_ge(sem("near_loaded"), 16 * 9)
                    dve.tensor_copy(near[:, :, :], near_raw[:, :, ::-1]).then_inc(sem("near_ready"), 1)
                    dve.tensor_copy(near_s[:, :], near_s_raw[:, ::-1]).then_inc(sem("near_ready"), 1)
                elif kind == "tile":
                    split_lo(arg + 2)
                    w = TILES[arg]
                    out = proj[arg % 2][:, :, :]
                    if w["kind"] == "add":
                        dve.wait_ge(tile_done, arg + 1)
                        dve.tensor_tensor(halves(x[:, w["i"], :]), out[:, :, 0:HALF], halves(x[:, w["i"], :]), ALU.add
                                          ).then_inc(tile_out[arg % 2], 1)
                    if w["kind"] == "u":
                        dve.wait_ge(tile_done, arg + 1)
                        wait_tile_out(dve, arg - 1)
                        if w["i"]:
                            dve.wait_ge(sem("mixer_ready"), w["i"])
                        else:
                            dve.wait_ge(sem("k_saved"), 128)
                        side(dve.tensor_tensor(by_half(pre[:, 2:2 + SEQ]), prompt_of(out), prompt(gates[:, 1, :]), ALU.mult))
                        dve.tensor_tensor(seqs(pre_s, 2, 6), samples_of(out), samples(gates[:, 1, :]), ALU.mult
                                          ).then_inc(tile_out[arg % 2], 1)
                elif kind == "conv":
                    settle()
                    wait_tile_out(dve, TILE["in", "u", arg])
                    dve.wait_ge(sem("pre_zero"), 1)
                    wait_taken(dve, *use_of["setup",][1])
                    side(dve.tensor_copy(pre_s[:, :, 0:2],
                                         mix_prefix[:, arg * 16:(arg + 1) * 16].rearrange("p (b w) -> p b w", w=2)))
                    side(dve.tensor_copy(mix_state[:, arg, 0:2], pre[:, SEQ:SEQ + 2]))
                    done(dve.tensor_copy(mix_state[:, arg, 2:18].rearrange("p (b w) -> p b w", w=2), pre_s[:, :, 4:6]))
                    cols = [vec[:, c:c + 1] for c in (V_CW + arg, V_CW + CT + arg, V_CW + 2 * CT + arg, V_CB + arg)]
                    y = gates[:, 1, :]
                    done(conv3((pre, pre_s), (prompt(y), samples(y)), cols))
                    dve.tensor_tensor(y, y, gates[:, 0, :], ALU.mult).then_inc(sem("mixed"), 1)
                    dve.wait_ge(sem("mixed_hi"), arg + 1)
                    dve.tensor_tensor(b_lo[:, arg, :], y, b_hi[:, arg, :].bitcast(F32), ALU.subtract
                                      ).then_inc(sem("mixer_ready"), 1)
                elif kind == "k_out":
                    wait_full(dve, uses[0])
                    if arg:
                        dve.wait_ge(sem("k_saved"), 32 * arg)
                    dve.tensor_copy(k_out, bank["T0"]).then_inc(free["T0"], 1)
                elif kind == "v_out":
                    wait_full(dve, uses[0])
                    dve.tensor_copy(v_tok[:, 0:4, arg * P:(arg + 1) * P], quads["T0"]).then_inc(free["T0"], 1)
                elif kind == "k_turn":
                    for b in (1, 3):
                        wait_full(dve, uses[b])
                        dve.tensor_copy(k_turned[:, b, :], bank["T1"]).then_inc(free["T1"], 1)
                elif kind == "k_score":
                    g, kq, hp = step[1:]
                    if hp == 0:
                        continue
                    wait_full(dve, uses[0])
                    if g == 0 and kq == 0:
                        dve.wait_ge(sem("near_ready"), 2)
                    far = near_s[:, 0:1]
                    if kq < 3:
                        dve.tensor_scalar(s_sb[:, kq * 256:kq * 256 + 256], bank["S0"][:, 0:256], far, None, ALU.add
                                          ).then_inc(free["S0"], 1)
                    else:
                        side(dve.tensor_scalar(s_sb[:, 768:896], bank["S0"][:, 0:P], far, None, ALU.add))
                        dve.tensor_tensor(s_sb[:, 896:1024], bank["S0"][:, P:2 * P], near_s[:, 0:P], ALU.add
                                          ).then_inc(free["S0"], 1)
                        wait_full(dve, uses[1])
                        dve.wait_ge(sem("new_bias_ready"), 8)
                        dve.tensor_tensor(s_sb[:, PAST:PAST + 32], bank["S1"][:, 0:32], new_bias[:, g, :], ALU.add
                                          ).then_inc(free["S1"], 1)
                elif kind == "s_soft":
                    settle()
                    wait_taken(dve, *use_of["k_score", arg, 3, 1][0])
                    wait_taken(dve, *use_of["k_score", arg, 3, 1][1])
                    dve.tensor_reduce(small[:, 0:1], s_sb, AX.X, ALU.max, negate=True).then_inc(sem("s_max"), 1)
                    dve.wait_ge(sem("s_exp"), arg + 1)
                    done(dve.reciprocal(small[:, 2:3], small[:, 1:2]))
                    done(dve.tensor_tensor(small[:, 3:4], small[:, 2:3], lam_row[:, :], ALU.mult))
                    dve.tensor_scalar(s_sb, s_sb, small[:, 3:4], None, ALU.mult).then_inc(sem("s_prob"), 1)
                elif kind == "s_turn":
                    for j, use in enumerate(uses[:2]):
                        wait_full(dve, use)
                        src = bank[use[0]].rearrange("p (a r) -> p a r", r=32)
                        side(dve.tensor_copy(s_keys[:, 16 * j:16 * j + 16, 0:16], src[:, :, 0:16]))
                        settle()
                        dve.tensor_tensor(s_keys[:, 16 * j:16 * j + 16, 0:16], src[:, :, 16:32],
                                          s_keys[:, 16 * j:16 * j + 16, 0:16], ALU.add).then_inc(free[use[0]], 1)
                    wait_full(dve, uses[2])
                    src = bank["T0"][0:32, 0:P].rearrange("p (a r) -> p a r", r=32)
                    done(dve.tensor_copy(s_keys[0:32, 32:36, 0:16], src[:, :, 0:16]))
                    dve.tensor_tensor(s_keys[0:32, 32:36, 0:16], src[:, :, 16:32], s_keys[0:32, 32:36, 0:16], ALU.add
                                      ).then_inc(free["T0"], 1)
                elif kind == "s_norm":
                    dve.wait_ge(sem("s_squares"), HEADS * (arg + 1))
                    dve.tensor_reduce(small[:, 8:9], small[:, 4:8], AX.X, ALU.add).then_inc(sem("s_sum"), 1)
                    dve.wait_ge(sem("s_rstd"), arg + 1)
                    dve.tensor_scalar(small[:, 10:14], row_cols[:, 0:4], small[:, 9:10], None, ALU.mult
                                      ).then_inc(sem("s_row_scale"), 1)
                elif kind in ("s_out", "p_out"):
                    wait_full(dve, uses[0])
                    dve.wait_ge(sem("attn_hi"), attn_parts[step] + 1)
                    if kind == "s_out":
                        cols = slice(HALF_P + HALF_S * arg, HALF + HALF_S * arg)
                        for h in range(HEADS):
                            dve.scalar_tensor_tensor(
                                out=b_lo[:, CT + h, cols].rearrange("p (b q) -> p b q", q=DEC_SEQ),
                                in0=free_dims(bank["T0"], h * (P + DEC_SEQ), [(32, GB), (1, DEC_SEQ)]), scalar=sub_w[:, 0:1],
                                in1=b_hi[:, CT + h, cols].bitcast(F32).rearrange("p (b q) -> p b q", q=DEC_SEQ),
                                op0=ALU.mult, op1=ALU.subtract
                            ).then_inc(sem("dve_side") if h < HEADS - 1 else free["T0"], 1)
                        continue
                    cols = slice(BLOCK[arg], BLOCK[arg] + P)
                    dve.scalar_tensor_tensor(out=b_lo[:, CT:KT, cols], in0=quads["T0"], scalar=sub_w[:, 0:1],
                                             in1=b_hi[:, CT:KT, cols].bitcast(F32), op0=ALU.mult,
                                             op1=ALU.subtract).then_inc(free["T0"], 1)
                elif kind == "p_score":
                    i, h = step[1:]
                    u = i * HEADS + h
                    w = min(2, i + 1) * P
                    wait_full(dve, uses[0])
                    wait_full(dve, uses[1])
                    if i >= 2:
                        side(dve.tensor_scalar(score[:, :, 0:(i - 1) * P], score[:, :, 0:(i - 1) * P], near[:, h, 0:1],
                                               None, ALU.add))
                    for c in range(2):
                        lo = (i + 1) * P - w
                        side(dve.tensor_tensor(score[:, c, lo:lo + w], score[:, c, lo:lo + w],
                                               near[:, h, 2 * P - w:2 * P], ALU.add))
                    settle()
                    if u == 0:
                        dve.wait_ge(sem("near_ready"), 2)
                    dve.tensor_reduce(small[:, 16 + 2 * (u % 2):18 + 2 * (u % 2)], score[:, :, 0:(i + 1) * P], AX.X,
                                      ALU.max, negate=True).then_inc(sem("p_max"), 1)
                elif kind == "p_turn":
                    i, h = step[1:]
                    u = i * HEADS + h
                    for use in use_of["p_score", i, h]:
                        wait_taken(dve, *use)
                    z, r = small[:, 20 + 2 * (u % 2):22 + 2 * (u % 2)], small[:, 24 + 2 * (u % 2):26 + 2 * (u % 2)]
                    done(dve.reciprocal(r, z))
                    done(dve.tensor_tensor(r[:, 1:2], r[:, 1:2], neg_lam[:, :], ALU.mult))
                    e = [p_exp[:, u % 2, c, 0:(i + 1) * P] for c in range(2)]
                    done(dve.tensor_scalar(e[0], e[0], r[:, 0:1], None, ALU.mult))
                    dve.scalar_tensor_tensor(out=e[0], in0=e[1], scalar=r[:, 1:2], in1=e[0], op0=ALU.mult,
                                             op1=ALU.add).then_inc(sem("p_prob"), 1)
                elif kind == "mem_in":
                    for i in range(2):
                        wait_full(dve, uses[2 * i + 1])
                        dve.tensor_copy(mem_t[:, 4:8, i * P:(i + 1) * P], quads["T1"]).then_inc(free["T1"], 1)
                elif kind == "c_score":
                    v = 4 * step[1] + step[2]
                    wait_full(dve, uses[0])
                    dve.tensor_reduce(c_small[:, 2 * (v % 2):2 * (v % 2) + 2],
                                      bank["S1"].rearrange("p (h k) -> p h k", h=2), AX.X, ALU.max, negate=True
                                      ).then_inc(sem("c_max"), 1)
                elif kind == "c_turn":
                    v = 4 * step[1] + step[2]
                    wait_taken(dve, *use_of["c_score", step[1], step[2]][0])
                    r = c_small[:, 8 + 2 * (v % 2):10 + 2 * (v % 2)]
                    done(dve.reciprocal(r, c_small[:, 4 + 2 * (v % 2):6 + 2 * (v % 2)]))
                    for h2 in range(2):
                        e = c_exp[:, v % 2, h2, :]
                        ins = dve.tensor_scalar(e, e, r[:, h2:h2 + 1], None, ALU.mult)
                        side(ins) if h2 == 0 else ins.then_inc(sem("c_prob"), 1)
                    wait_full(dve, uses[0])
                    hp, i = step[1:]
                    dve.tensor_copy(c_keys[:, 4 * hp:4 * hp + 4, i * P:(i + 1) * P], quads["T0"]).then_inc(free["T0"], 1)
                elif kind == "c_pv":
                    dve.wait_ge(sem("cross_hi"), arg + 1)
                    dve.tensor_tensor(prompt(a_lo[:, arg, :]), by_half(bank["S1"]),
                                      prompt(a_hi[:, arg, :]).bitcast(F32), ALU.subtract).then_inc(free["S1"], 1)
                elif kind == "ck_turn":
                    for b in (1, 3):
                        wait_full(dve, uses[b])
                        dve.tensor_copy(c_turned[:, b, :], bank["T1"]).then_inc(free["T1"], 1)
                elif kind == "ck_score":
                    g, kt, dh = step[1:]
                    if dh == 1:
                        wait_full(dve, uses[0])
                        dve.tensor_copy(c_s[:, kt * P:(kt + 1) * P], bank["S0"][:, 0:P]).then_inc(free["S0"], 1)
                elif kind == "cs_soft":
                    wait_taken(dve, *use_of["ck_score", arg, 1, 1][0])
                    dve.tensor_reduce(c_small[:, 16:17], c_s, AX.X, ALU.max, negate=True).then_inc(sem("cs_max"), 1)
                    dve.wait_ge(sem("cs_exp"), arg + 1)
                    done(dve.reciprocal(c_small[:, 18:19], c_small[:, 17:18]))
                    dve.tensor_scalar(c_s, c_s, c_small[:, 18:19], None, ALU.mult).then_inc(sem("cs_prob"), 1)
                elif kind == "cs_out":
                    wait_full(dve, uses[1])
                    dve.tensor_copy(o_cross[:, 512:1024], bank["T1"]).then_inc(free["T1"], 1)
                    for j in range(2):
                        for h2 in range(2):
                            h = 2 * j + h2
                            dve.wait_ge(sem("cs_hi"), 4 * arg + 2 * j + 2)
                            cols = (slice(None), slice(2 * h, 2 * h + 2),
                                    slice(HALF_P + HALF_S * arg, HALF + HALF_S * arg))
                            ins = dve.tensor_tensor(
                                a_lo[cols].rearrange("p d (b q) -> p d b q", q=DEC_SEQ),
                                head_rows(uses[2 + j][0], P, h2 * 2 * P + 4 * h, 2),
                                a_hi[cols].bitcast(F32).rearrange("p d (b q) -> p d b q", q=DEC_SEQ), ALU.subtract)
                            ins.then_inc(sem("dve_side") if h2 == 0 else free[uses[2 + j][0]], 1)
                elif kind == "state_in":
                    wait_full(dve, uses[1])
                    dve.tensor_copy(f_prefix[:, FT:2 * FT, :], bank["T1"][:, 0:FT * 16].rearrange("p (i c) -> p i c", c=16)
                                    ).then_inc(free["T1"], 1)
                elif kind == "ffn":
                    g, i = step[1:]
                    if i:
                        dve.wait_ge(sem("act_ready"), i)
                    dve.wait_ge(sem("up_pad_zero"), 1)
                    for j, name in enumerate(("gate", "up")):
                        wait_tile_out(dve, TILE["up", name, i])
                        dve.wait_ge(sem("f_prefix_in"), 2 * i + 1 + j)
                        n = j * FT + i
                        cols = [fvec[:, c * 2 * FT + n:c * 2 * FT + n + 1] for c in range(4)]
                        out = conv[:, j, :]
                        ins = conv3((up_pad[:, j, i % 2, :], up_pad_s[:, j, i % 2, :, :]), (prompt(out), samples(out)), cols)
                        ins.then_inc(sem("conv_ffn_done"), 1)
                    dve.wait_ge(sem("silu_done"), i + 1)
                    dve.wait_ge(sem("conv_ffn_done"), 2 * i + 2)
                    dve.tensor_tensor(conv[:, 1, :], conv[:, 0, :], conv[:, 1, :], ALU.mult
                                      ).then_inc(sem("gated"), 1)
                    dve.wait_ge(sem("act_hi"), i + 1)
                    k = i - FFN_GROUPS[g][0]
                    dve.tensor_tensor(a_lo[:, k, :], conv[:, 1, :], a_hi[:, k, :].bitcast(F32), ALU.subtract
                                      ).then_inc(sem("act_ready"), 1)
                elif kind == "state_out":
                    if arg % 2:
                        wait_full(dve, uses[0])
                        dve.tensor_copy(f_rows[0:18, arg * 512:(arg + 1) * 512], bank["T1"][0:18, :]).then_inc(free["T1"], 1)
                elif kind == "final":
                    wait_full(dve, uses[1])
                    if arg >= 3:
                        dve.wait_ge(sem(f"y_saved{arg % 3}"), 16)
                    rows = P if arg < 4 else 32
                    dve.tensor_copy(y_out[0:rows, arg % 3, 512:1024], bank["T1"][0:rows, :]).then_inc(free["T1"], 1)


_OUTS = [("y_prompt", (1, SEQ, D_MODEL)), ("y_sample", (DEC_BATCH, DEC_SEQ, D_MODEL)),
         ("k_prompt", (1, 1, SEQ, HEADS, 2 * DK)), ("v_prompt", (1, 1, SEQ, HEADS, DV)),
         ("k_sample", (1, DEC_BATCH, DEC_SEQ, HEADS, 2 * DK)), ("v_sample", (1, DEC_BATCH, DEC_SEQ, HEADS, DV)),
         ("conv_mix_prompt", (1, 1, 2, D_CONV)), ("conv_mix_sample", (1, DEC_BATCH, 2, D_CONV)),
         ("conv_ffn_prompt", (1, 1, 2, 2 * D_FF)), ("conv_ffn_sample", (1, DEC_BATCH, 2, 2 * D_FF)),
         ("mem_k", (1, 1, N_MEM, HEADS, MEM_DH)), ("mem_v", (1, 1, N_MEM, HEADS, MEM_DH))]


def kernel(**inputs):
    import concourse.bacc as bacc
    from concourse.bass_utils import run_bass_kernel_spmd

    nc = bacc.Bacc("TRN2", target_bir_lowering=False, num_devices=1)
    arrays, t = {}, {}
    given = {name: np.ascontiguousarray(a) for name, a in inputs.items()}
    given["const_ident"] = np.eye(P, dtype=np.float32)
    given["const_onehot"] = bucket_onehot()
    given["const_rows"] = row_columns()
    for name, a in given.items():
        arrays[f"in_{name}"] = a
        t[name] = nc.dram_tensor(f"in_{name}", a.shape, mybir.dt.from_np(a.dtype), kind="ExternalInput").ap()
    for name, shape in _OUTS:
        t[f"out_{name}"] = nc.dram_tensor(f"out_{name}", shape, F32, kind="ExternalOutput").ap()
    t["scratch_bias"] = nc.dram_tensor("scratch_bias", (HEADS, DIST), F32, kind="Internal").ap()
    build(nc, t)
    result = run_bass_kernel_spmd(nc, [arrays], core_ids=[0]).results[0]
    return tuple(result[f"out_{name}"] for name, _ in _OUTS)
```

```python
from contextlib import ExitStack

import numpy as np

import concourse.bass as bass
from concourse import mybir

F32 = mybir.dt.float32
F32R = mybir.dt.float32r
I32 = mybir.dt.int32
ALU = mybir.AluOpType
ACT = mybir.ActivationFunctionType
AX = mybir.AxisListType

P = 128
D_MODEL, SEQ, DEC_BATCH, DEC_SEQ, PAST, PAGE = 1024, 512, 8, 4, 1024, 128
D_CONV, HEADS, DK, DV, N_MEM, D_FF, BUCKETS = 512, 4, 64, 128, 256, 2816, 32
MEM_DH = D_MODEL // HEADS
EPS, NEG = 1e-6, -1e30
LAM_INIT = 0.2
KT = D_MODEL // P
CT = D_CONV // P
FT = D_FF // P
HALF_P, HALF_S = SEQ // 2, DEC_BATCH * DEC_SEQ // 2
HALF = HALF_P + HALF_S
TOK = 2 * HALF
BLOCK = [0, P, HALF + HALF_S, HALF + HALF_S + P]
NPAGES = PAST // PAGE
GROUPS, GB = 2, 4
FFN_GROUPS = [range(0, 8), range(8, 15), range(15, 22)]
DIST = 384
W_RING, W_HI_RING = 4, 3
PAGE_RING, C_PAGE_RING = 16, 8
VEC_ROWS = 5 * KT + 3 * CT + CT + 1
V_MIX, V_CROSS, V_MEM, V_FFN, V_FINAL = 0, KT, 2 * KT, 3 * KT, 4 * KT
V_CW, V_CB, V_SUB = 5 * KT, 5 * KT + 3 * CT, 5 * KT + 4 * CT


def bucket_onehot():
    import math
    m = np.zeros((BUCKETS + 1, DIST), np.float32)
    for col in range(DIST):
        n = col - (P - 1)
        if n < 0:
            m[BUCKETS, col] = 1.0
            continue
        big = 16 + int(np.float32(np.log(np.float32(max(n, 1) / 16.0))) / np.float32(math.log(8.0)) * 16) if n >= 16 else n
        m[min(big, BUCKETS - 1), col] = 1.0
    return m


def row_columns():
    m = np.zeros((P, 5), np.float32)
    for r in range(P):
        if r % 32 < 16:
            m[r, (r % 32) // DEC_SEQ] = 1.0
        else:
            m[r, 4] = 1.0
    return m


OUT_AND_KEYS = [("out", n) for n in range(5)]
OUT_AND_KEYS += [("mem", 0), ("out", 5), ("mem", 1), ("out", 6), ("mem", 2), ("out", 7)]
OUT_AND_KEYS += [("mem", n) for n in range(3, KT)]


FFN_ORDER = []
for _g, _group in enumerate(FFN_GROUPS):
    for _i in _group:
        if _g == 0 or _i != _group[0]:
            FFN_ORDER.append(("up", "gate", _i))
        FFN_ORDER.append(("up", "up", _i))
        if _i == _group[-1]:
            if _g + 1 < len(FFN_GROUPS):
                FFN_ORDER.append(("up", "gate", _i + 1))
            FFN_ORDER += [(f"down{_g}", "add", _n) for _n in range(KT)]


def make_tiles():
    tiles = []

    def add(phase, kind, i, weight, row0, rows, col):
        tiles.append(dict(phase=phase, kind=kind, i=i, weight=weight, row0=row0, kt=rows // P,
                          col=col, first=all(w["phase"] != phase for w in tiles), n=len(tiles)))

    for h in range(HEADS):
        add("in", "q", h, "w_in", 0, D_MODEL, 3 * D_CONV + h * P)
    for h in range(HEADS):
        add("in", "k", h, "w_in", 0, D_MODEL, 3 * D_CONV + 512 + h * P)
    for h in range(HEADS):
        add("in", "v", h, "w_in", 0, D_MODEL, 3 * D_CONV + 1024 + h * P)
    for c in range(CT):
        for j, kind in enumerate(("gb", "gc", "u")):
            add("in", kind, c, "w_in", 0, D_MODEL, j * D_CONV + c * P)
    for phase, n in OUT_AND_KEYS:
        add(phase, "add" if phase == "out" else "mem", n, "w_out" if phase == "out" else "w_ckv", 0, D_MODEL, n * P)
    for n in range(KT):
        add("cq", "cq", n, "w_cq", 0, D_MODEL, n * P)
    for n in range(KT, 2 * KT):
        add("mem", "mem", n, "w_ckv", 0, D_MODEL, n * P)
    for n in range(KT):
        add("co", "add", n, "w_co", 0, D_MODEL, n * P)
    for phase, kind, i in FFN_ORDER:
        if phase == "up":
            add("up", kind, i, "w_up", 0, D_MODEL, i * P + (D_FF if kind == "up" else 0))
        else:
            group = FFN_GROUPS[int(phase[4:])]
            add(phase, "add", i, "w_down", group[0] * P, len(group) * P, i * P)
    return tiles


TILES = make_tiles()
TILE = {(t["phase"], t["kind"], t["i"]): t["n"] for t in TILES}


def make_schedule():
    s = []

    def tile(phase, kind, i):
        s.append(("tile", TILE[phase, kind, i]))

    s += [("x_in", i) for i in range(4)]
    s += [("first_split", 0), ("x_in", 4), ("setup",)]
    s += [("apply", "in", k) for k in range(KT)]
    s.append(("first_split", 1))
    s += [("squares", k, "x") for k in range(KT)]
    tile("in", "q", 0)
    s += [("half_tile", TILE["in", "q", 1]), ("norm", "in")]
    tile("in", "q", 1)
    s += [("setup_2",), ("bias",)]
    tile("in", "q", 2)
    tile("in", "q", 3)
    s += [("near",), ("q_blocks",)]
    fill = [("in", "k", h) for h in range(HEADS)] + [("in", "v", h) for h in range(HEADS)]
    fill += [("in", kind, c) for c in range(CT) for kind in ("gb", "gc", "u")]
    after = {("in", "k", h): [("k_out", h)] for h in range(HEADS)}
    after |= {("in", "v", h): [("v_out", h)] for h in range(HEADS)}

    def turns(g, kq, hp, behind=None):
        steps = []
        for j in range(2):
            steps.append(("k_turn", g, kq, hp, j))
            if behind:
                steps.append(("k_score", g, *behind, j))
        return steps

    def keys(g, kq):
        return turns(g, kq, 0, (kq - 1, 1) if kq else None) + turns(g, kq, 1, (kq, 0))

    def scores(g, kq, hp):
        return [("k_score", g, kq, hp, j) for j in range(2)]

    plan = [keys(0, kq) for kq in range(4)]
    plan.append(scores(0, 3, 1) + turns(1, 0, 0) + turns(1, 0, 1) + [("s_soft", 0)])
    plan.append([("s_turn", 0)] + scores(1, 0, 0) + [("s_pv", 0, 0)])
    plan.append([("s_pv", 0, 1)] + keys(1, 1))
    plan.append([("s_pv", 0, 2)] + keys(1, 2))
    plan.append([("s_pv", 0, 3), ("s_new", 0)] + keys(1, 3) + [("s_norm", 0)])
    plan.append(scores(1, 3, 1) + [("s_soft", 1)])
    plan.append([("s_turn", 1), ("s_pv", 1, 0), ("s_pv", 1, 1)])
    plan.append([("s_pv", 1, 2), ("s_out", 0), ("s_pv", 1, 3), ("s_new", 1), ("s_norm", 1)])
    units = [(i, h) for i in range(SEQ // P) for h in range(HEADS)]
    half_at, fill_at = range(3, 17, 2), range(4, 18, 2)
    ticks = []
    for u in range(len(units) + 4):
        tick = []
        if 0 <= u - 1 < len(units):
            tick.append(("p_mix", *units[u - 1]))
        if u >= 4 and units[u - 4][1] == HEADS - 1:
            tick.append(("p_out", units[u - 4][0]))
        if u < len(units):
            tick.append(("p_score", *units[u]))
        if 3 <= u < len(units) + 3 and units[u - 3][1] == HEADS - 1:
            tick.append(("p_scale", units[u - 3][0]))
        if u in half_at:
            tick.append("half")
        if u in fill_at:
            tick.append("fill")
        if 0 <= u - 1 < len(units):
            tick.append(("p_turn", *units[u - 1]))
        if 0 <= u - 2 < len(units):
            tick.append(("p_pv", *units[u - 2]))
            if units[u - 2][1] == HEADS - 1:
                tick.append(("p_norm", units[u - 2][0]))
        ticks += tick
    assert len(plan) + len(fill_at) + 1 == len(fill)
    late = []
    for part in plan:
        f = fill.pop(0)
        tile(*f)
        if f[1] == "u":
            part = part + [("conv", f[2]), ("mix", f[2])]
        if ("s_new", 0) in part:
            part = late + part
        else:
            at = len(part) - 1 if part[-1][0] == "k_score" else 0
            part = part[:at] + late + part[at:]
        late = list(after.get(f, []))
        s.extend(part)
    ticks.insert(0, "fill")
    for n, step in enumerate(ticks):
        if n == 3:
            s.append(("s_out", 1))
        if step == ("p_pv", 3, 3):
            s.append(("mem_in",))
        if step == ("p_out", 3):
            s += [("half_tile", TILE["out", "add", 0]), step]
            s += [("squares", k, "mem") for k in range(KT)]
            continue
        if step == "half":
            s.append(("half_tile", TILE[fill[0]]))
            continue
        if step == "fill":
            f = fill.pop(0)
            tile(*f)
            if f[1] == "u":
                late += [("conv", f[2]), ("mix", f[2])]
            continue
        s.append(step)
        if step[0] == "p_score":
            s.extend(late[:1])
            late = late[1:]
        if step == ("p_turn", 3, 3):
            s.extend(late)
    for phase, n in OUT_AND_KEYS:
        tile(phase, "add" if phase == "out" else "mem", n)
        if phase == "out":
            s.append(("squares", n - 1, "x") if n else ("norm", "mem"))
            if n == 1:
                s.append(("mix_out",))
            if n < 4:
                s += [("apply", "mem", 2 * n), ("apply", "mem", 2 * n + 1)]
            if n == KT - 1:
                s.append(("squares", n, "x"))
        else:
            if n:
                s.append(("mem_out", n - 1))
            if 3 <= n < 7:
                s += [("apply", "cq", 2 * n - 6), ("apply", "cq", 2 * n - 5)]
            if n == 5:
                s.append(("norm", "cq"))
    for n in range(KT):
        tile("cq", "cq", n)
        if n == 0:
            s.append(("mem_out", KT - 1))
    s.append(("cq_blocks",))
    units = [(hp, i) for hp in range(2) for i in range(4)]
    parts = []
    for g in range(GROUPS):
        for kt in range(2):
            parts += [[("ck_turn", g, kt, 0)], [("ck_score", g, kt, 0), ("ck_turn", g, kt, 1)],
                      [("ck_score", g, kt, 1)]]
        parts[-1].append(("cs_soft", g))
        parts += [[("cs_turn", g), ("cs_pv", g, 0)], [("cs_pv", g, 1), ("cs_out", g)]]
    for j, part in enumerate(parts):
        if 1 <= j < 9:
            s.append(("c_mix", *units[j - 1]))
        if j < 8:
            s.append(("c_score", *units[j]))
        if 1 <= j < 9:
            s.append(("c_turn", *units[j - 1]))
        scores = [step for step in part if step[0] == "ck_score"]
        s += scores
        if 1 <= j < 9:
            s.append(("mem_out", KT + j - 1))
        if j < 8:
            tile("mem", "mem", KT + j)
        s += [step for step in part if step not in scores]
        if 8 <= j < 15:
            s.append(("c_pv", j - 8))
    s.append(("c_pv", KT - 1))
    for n in range(KT):
        tile("co", "add", n)
        if n:
            s += [("apply", "up", n - 1), ("squares", n - 1, "x")]
        if n == 5:
            s.append(("state_in",))
    s += [("apply", "up", KT - 1), ("squares", KT - 1, "x")]
    for phase, kind, n in FFN_ORDER:
        tile(phase, kind, n)
        if phase == "up":
            if (kind, n) == ("gate", 0):
                s.append(("norm", "up"))
            s.append(("ffn", next(g for g, group in enumerate(FFN_GROUPS) if n in group), n, int(kind == "up")))
        if phase == "down2" and n:
            s += [("squares", n - 1, "x"), ("apply", "final", n - 1)]
        if phase == "down2" and n >= 2:
            s += [("state_out", j) for j in range(2 * n - 4, 2 * n - 2) if j < 2 * FT // 4]
    s += [("squares", KT - 1, "x"), ("apply", "final", KT - 1), ("norm", "final")]
    s += [("final", i) for i in range(5)]
    return s


SCHEDULE = make_schedule()
HALVED = {step[1] for step in SCHEDULE if step[0] == "half_tile"}
FILLS = {
    "setup": ["T0"], "setup_2": ["T0", "T1"], "x_in": ["T0", "T1"], "norm": ["S0", "S1"], "bias": ["S0"],
    "k_out": ["T0", "T1"], "v_out": ["T0", "T1"], "k_turn": ["T0", "T1"],
    "s_turn": ["T0", "T1", "T0"], "p_score": ["S0", "S1"], "p_turn": ["T0"],
    "s_out": ["T0"], "p_out": ["T0"],
    "mem_in": ["S0", "S1", "S0", "S1"], "mix_out": ["S0"], "mem_out": ["T0"], "c_score": ["S1"],
    "c_turn": ["T0"], "c_pv": ["S1"], "ck_turn": ["T0", "T1"] * 2,
    "cs_turn": ["T0"], "state_in": ["T0", "T1"], "final": ["T0", "T1"],
}


def number_fills():
    count = dict(S0=0, S1=0, T0=0, T1=0)
    out, held = [], {}

    def use(slot):
        count[slot] += 1
        return slot, count[slot] - 1

    for step in SCHEDULE:
        kind = step[0]
        uses = [use(slot) for slot in FILLS.get(kind, [])]
        if kind == "k_score":
            if step[3:] == (0, 0):
                held["k"] = use("S0")
            uses = [held["k"]]
            if step[2:] == (3, 1, 1):
                uses.append(use("S1"))
        if kind == "norm" and step[1] in ("mem", "final"):
            count["S1"] -= 1
            uses = uses[:1]
        if kind == "s_pv":
            if step[2] == 0:
                held["s", step[1]] = use("S1")
            uses = [held["s", step[1]]]
        if kind in ("s_new", "s_norm"):
            uses = [held["s", step[1]]]
        if kind == "p_pv":
            if step[2] == 0:
                held["p", step[1]] = use("T1")
            uses = [held["p", step[1]]]
        if kind in ("p_norm", "p_scale"):
            uses = [held["p", step[1]]]
        if kind == "ck_score":
            if step[3] == 0:
                held["ck"] = use("S0")
            uses = [held["ck"]]
        if kind == "cs_pv":
            if step[2] == 0:
                held["cs"] = [use("S0"), use("T1")]
            uses = list(held["cs"])
        if kind == "cs_out":
            uses = [*held["cs"], use("T0"), use("T1")]
        if kind == "state_out":
            uses = [use("T0" if step[1] % 2 == 0 else "T1")]
        latest = {slot: n - 1 for slot, n in count.items()}
        out.append((step, uses, latest))
    return out


NUMBERED = number_fills()


PAGE_GROUPS = [(step[1], "k" if step[0] == "k_turn" else "v", step[2]) for step in SCHEDULE
               if (step[0] == "k_turn" and step[3:] == (0, 0)) or step[0] == "s_pv"]


def self_page(g, cache, kq, b, pg):
    first = PAGE_GROUPS.index((g, cache, kq)) * 2 * GB
    return first + (pg * GB + b if cache == "v" else 2 * b + pg)


def cross_page(g, cache, kt, b):
    return ((g * 2 + (cache == "v")) * 2 + kt) * GB + b


def build(nc, t):
    ctx = ExitStack()
    with ctx:
        sems = {}

        def sem(name):
            if name not in sems:
                sems[name] = ctx.enter_context(nc.semaphore(name))
            return sems[name]

        def sb(name, shape, dtype=F32, stack=ctx, side=None):
            return stack.enter_context(nc.sbuf_tensor(name, shape, dtype, side=side))

        early = ExitStack()
        w_raw = sb("w_raw", [P, W_RING, KT, P], F32, early)
        early.close()
        w_lo = sb("w_lo", [P, W_RING, KT, P], F32R)
        w_hi = sb("w_hi", [P, W_HI_RING, KT, P], F32R)
        x = sb("x", [P, KT, TOK])
        a_hi = sb("a_hi", [P, KT, TOK], F32R)
        a_lo = sb("a_lo", [P, KT, TOK], F32R)
        ident = sb("ident", [P, P])
        ones = sb("ones", [P, P])
        vec = sb("vec", [P, VEC_ROWS])
        fvec = sb("fvec", [P, 8 * FT])
        eps = sb("eps", [P, 1])
        neg_lam = sb("neg_lam", [P, 1])
        sub_w = sb("sub_w", [P, 1])
        rstd = sb("rstd", [P, TOK])[:, :]
        rstd_tok = sb("rstd_tok", [P, 5])
        norm_area = sb("norm_area", [P, 7 * TOK])

        def lend(area, start, shape):
            n = int(np.prod(shape))
            v = area[:, start:start + n]
            if len(shape) == 1:
                return v
            names = " ".join(f"d{i}" for i in range(len(shape)))
            return v.rearrange(f"p ({names}) -> p {names}", **{f"d{i}": m for i, m in enumerate(shape)})

        normed = lend(norm_area, 0, (3, TOK))
        square = lend(norm_area, 3 * TOK, (2, TOK))
        sums = lend(norm_area, 5 * TOK, (TOK,))

        right = ExitStack()
        early_pages = [sb(f"early_pages{i}", [P, KT, TOK], F32, right, "right") for i in range(2)]
        right.close()
        right = ExitStack()
        b_hi = sb("b_hi", [P, KT, TOK], F32R, right, "right")
        b_lo = sb("b_lo", [P, KT, TOK], F32R, right, "right")
        right.close()
        right = ExitStack()
        c_hi = sb("c_hi", [P, KT, TOK], F32R, right, "right")
        c_lo = sb("c_lo", [P, KT, TOK], F32R, right, "right")
        right.close()
        right = ExitStack()
        c_keys = sb("c_keys", [P, HEADS * 2, SEQ], F32, right, "right")
        c_turned = sb("c_turned", [P, GB, 4 * P], F32, right, "right")
        right.close()
        d_hi = sb("d_hi", [P, KT, TOK], F32R, ctx, "right")
        d_lo = sb("d_lo", [P, KT, TOK], F32R, ctx, "right")

        one = ExitStack()
        q_t = sb("q_t", [P, HEADS, TOK], F32, one)
        k_t = sb("k_t", [P, HEADS, TOK], F32, one)
        v_tok = sb("v_tok", [P, 5, HEADS * DV], F32, one)
        near = sb("near", [P, HEADS, 2 * P], F32, one)
        near_s = sb("near_s", [P, P + DEC_SEQ], F32, one)
        new_bias = sb("new_bias", [P, GROUPS, 32], F32, one)
        q_rows = sb("q_rows", [P, HEADS, DEC_BATCH, 32], F32, one)
        row_cols = sb("row_cols", [P, 5], F32, one)
        lam_row = sb("lam_row", [P, 1], F32, one)
        small = sb("small", [P, 64], F32, one)
        pages = sb("pages", [P, PAGE_RING // 2 * HEADS * DV], F32, one)
        turned = sb("turned", [P, 2 * GB * 4 * P], F32, one)
        pre = sb("pre", [P, 2 + SEQ], F32, one)
        pre_s = sb("pre_s", [P, DEC_BATCH, 2 + DEC_SEQ], F32, one)
        mix_prefix = sb("mix_prefix", [P, CT * 16], F32, one)
        mix_state = sb("mix_state", [P, CT, 18], F32, one)
        page_ids = sb("page_ids", [1, DEC_BATCH * NPAGES], I32, one)
        one.close()
        x_tok = lend(pages, 0, (4, D_MODEL))
        p_exp = lend(pages, 0, (2, 2, SEQ))
        p_keys = lend(pages, 2048, (2, 4, P))
        o_blk = lend(pages, 3072, (HEADS * DV,))
        o_sq = lend(pages, 3584, (HEADS * DV,))
        k_turned = lend(turned, 0, (2, GB, 4 * P))
        x_tok_s = lend(turned, 0, (D_MODEL,))
        packed = lend(turned, D_MODEL, (3, P))
        onehot = lend(turned, 1536, (DIST,))
        rel = turned[:, 1536 + DIST:1536 + DIST + HEADS]
        mem_tok = lend(turned, 0, (2, D_MODEL))
        mem_t = lend(turned, 2 * D_MODEL, (KT, N_MEM))
        mix_in = v_tok[:, 0, :]
        lams = lend(v_tok[:, 1, :], 0, (4, DK))
        gates = lend(norm_area, 0, (2, TOK))
        s_sb = lend(norm_area, 2 * TOK, (PAST + 32,))
        s_keys = lend(norm_area, 2 * TOK + PAST + 32, (9 * GB, 32))
        o_sb = lend(norm_area, 2 * TOK + PAST + 32 + 9 * GB * 32, (HEADS * DV,))
        near_raw = lend(norm_area, 2 * TOK, (HEADS, 2 * P))
        near_s_raw = o_sb[:, 0:P + DEC_SEQ]
        dist_vec = s_keys[:, 0:12, :].rearrange("p a b -> p (a b)")
        k_out = o_sb
        k_out_s = pre[0:32, 2:2 + P]
        mix_out = lend(k_t[:, :, :].rearrange("p a b -> p (a b)"), 0, (HEADS * DV,))

        two = ExitStack()
        qc_t = sb("qc_t", [P, KT, TOK], F32, two)
        mk_t = sb("mk_t", [P, KT, N_MEM], F32, two)
        mv_tok = sb("mv_tok", [P, 2, D_MODEL], F32, two)
        mv_t = sb("mv_t", [P, 2, N_MEM], F32, two)
        qc_rows = sb("qc_rows", [P, KT, DEC_BATCH, 32], F32, two)
        c_pages = sb("c_pages", [P, C_PAGE_RING, D_MODEL], F32, two)
        c_small = sb("c_small", [P, 32], F32, two)
        two.close()
        m_stage = lend(norm_area, 6 * TOK, (2, 2, P))
        c_exp = lend(norm_area, 0, (2, 2, N_MEM))
        c_s = lend(norm_area, 1024, (N_MEM,))
        cs_keys = lend(norm_area, 1280, (2, P))
        o_cross = lend(norm_area, 1536, (D_MODEL,))

        three = ExitStack()
        f_rows = sb("f_rows", [18, 2 * D_FF], F32, three)
        f_prefix = sb("f_prefix", [P, 2 * FT, 16], F32, three)
        f_state = sb("f_state", [P, 2 * FT, 18], F32, three)
        up_pad = sb("up_pad", [P, 2, 2, 2 + SEQ], F32, three)
        up_pad_s = sb("up_pad_s", [P, 2, 2, DEC_BATCH, 2 + DEC_SEQ], F32, three)
        conv = sb("conv", [P, 2, TOK], F32, three)
        three.close()
        y_out = lend(norm_area, 0, (3, D_MODEL))

        proj = [ctx.enter_context(nc.psum_tensor(f"proj{i}", [P, 2, 512], F32)) for i in range(2)]
        score = ctx.enter_context(nc.psum_tensor("score", [P, 2, 512], F32))
        bank = {"S0": score[:, 0, :], "S1": score[:, 1, :]}
        for name in ("T0", "T1"):
            bank[name] = ctx.enter_context(nc.psum_tensor(name, [P, 512], F32))[:, :]
        quads = {name: ap.rearrange("p (j c) -> p j c", c=P) for name, ap in bank.items()}

        w_loaded = [sem(f"w_loaded{i}") for i in range(W_RING)]
        w_hi_ready, w_lo_ready = sem("w_hi_ready"), sem("w_lo_ready")
        tile_done = sem("tile_done")
        tile_out = [sem("tile_out0"), sem("tile_out1")]
        full = {s: sem(f"full_{s}") for s in ("S0", "S1", "T0", "T1")}
        free = {s: sem(f"free_{s}") for s in ("S0", "S1", "T0", "T1")}
        ready = {ph: sem(f"ready_{ph}") for ph in ("in", "mem", "cq", "up", "final")}

        def page(n):
            slot = n % PAGE_RING
            if slot >= 2 * GB:
                return pages[:, (slot - 2 * GB) * HEADS * DV:(slot - 2 * GB + 1) * HEADS * DV]
            area = early_pages[slot // GB][:, CT:KT, :].rearrange("p a b -> p (a b)")
            return area[:, slot % GB * HEADS * DV:(slot % GB + 1) * HEADS * DV]

        def wait_full(eng, use):
            eng.wait_ge(full[use[0]], use[1] + 1)

        def wait_empty(eng, use):
            if use[1] > 0:
                eng.wait_ge(free[use[0]], use[1])

        def wait_taken(eng, slot, n):
            eng.wait_ge(free[slot], n + 1)

        def wait_tile_out(eng, n):
            eng.wait_ge(tile_out[n % 2], n // 2 + 1)

        def free_dims(ap, start, dims):
            return bass.AP(ap.tensor, ap.offset + start, [list(ap.ap[0])] + [list(d) for d in dims])

        def prompt(ap):
            return free_dims(ap, 0, [(HALF + HALF_S, 2), (1, HALF_P)])

        def samples(ap):
            return ap[:, HALF_P:HALF + HALF_S].rearrange("p (a b q) -> p a b q", a=2, q=DEC_SEQ)

        def prompt_of(banks):
            return free_dims(banks, 0, [(512 + HALF_S, 2), (1, HALF_P)])

        def samples_of(banks):
            return free_dims(banks, HALF_P, [(512 - HALF_P, 2), (DEC_SEQ, GB), (1, DEC_SEQ)])

        def halves(ap):
            return ap.rearrange("p (a b) -> p a b", a=2)

        def by_half(ap):
            return ap.rearrange("p (a b) -> p a b", a=2)

        def seqs(ap, lo, hi):
            return ap[:, :, lo:hi].rearrange("p (a b) q -> p a b q", a=2)

        def block_cols(ap, k, i):
            if i < 4:
                return ap[:, k, BLOCK[i]:BLOCK[i] + P]
            return ap[:, k, HALF_P:HALF + HALF_S]

        def head_rows(name, j_step, j0, n):
            return free_dims(bank[name], j0, [(j_step, n), (32, GB), (1, DEC_SEQ)])

        split = {"in": (a_hi, a_lo), "out": (b_hi, b_lo), "mem": (a_hi, a_lo), "cq": (c_hi, c_lo),
                 "co": (a_hi, a_lo), "up": (d_hi, d_lo)}
        for g in range(3):
            split[f"down{g}"] = (a_hi, a_lo)
        IN_LAST, OUT_LAST = TILE["in", "u", CT - 1], TILE["out", "add", KT - 1]
        MEM_FIRST, CQ_LAST, CO_FIRST = TILE["mem", "mem", 0], TILE["cq", "cq", KT - 1], TILE["co", "add", 0]
        norms = [s[1] for s in SCHEDULE if s[0] == "norm"]
        norm_w = {"in": V_MIX, "mem": V_MEM, "cq": V_CROSS, "up": V_FFN, "final": V_FINAL}
        LATE_NORMS = ["mem"]
        use_of = {step: uses for step, uses, _ in NUMBERED}
        latest_at = {step: latest for step, _, latest in NUMBERED}
        attn_parts = {s: n for n, s in enumerate(s for s in SCHEDULE if s[0] in ("s_out", "p_out"))}
        block = ctx.enter_context(nc.Block())

        @block.sync
        def _(sp):
            def load_weights(n):
                if n >= len(TILES):
                    return
                w = TILES[n]
                if n >= W_RING:
                    sp.wait_ge(tile_done, n - W_RING + 1)
                src = t[w["weight"]][0, w["row0"]:w["row0"] + w["kt"] * P, w["col"]:w["col"] + P]
                sp.dma_start(w_raw[:, n % W_RING, 0:w["kt"], :],
                             src.rearrange("(k p) n -> p k n", p=P)).then_inc(w_loaded[n % W_RING], 16)

            def load_self(g, cache, kq):
                src = t["cache_k" if cache == "k" else "cache_v"]
                order = [(b, pg) for b in range(GB) for pg in range(2)]
                if cache == "v":
                    order = [(b, pg) for pg in range(2) for b in range(GB)]
                physical = []
                for b, pg in order:
                    slot = (4 * g + b) * NPAGES + 2 * kq + pg
                    physical.append(sp.value_load(page_ids[0:1, slot:slot + 1], min_val=0,
                                                  max_val=src.shape[1] - 1))
                for (b, pg), phys in zip(order, physical):
                    n = self_page(g, cache, kq, b, pg)
                    before = n - PAGE_RING
                    if before < 0:
                        if n == 2 * GB:
                            sp.wait_ge(free["T1"], use_of["x_in", 4][1][1] + 1)
                            sp.wait_ge(free["T0"], use_of["x_in", 4][0][1] + 1)
                    else:
                        j, rest = divmod(before, 2 * GB)
                        bg, bc, bq = PAGE_GROUPS[j]
                        if bc == "k":
                            use = use_of["k_turn", bg, bq, 1, rest // 4][rest // 2 % 2]
                            sp.wait_ge(full[use[0]], use[1] + 1)
                        else:
                            sp.wait_ge(sem("v_pages_read"), (bg * 4 + bq) * 2 + rest // GB + 1)
                    sp.dma_start(page(n),
                                 src[0, bass.ds(phys, 1), :, :, :].rearrange("a r h d -> (a r) (h d)")
                                 ).then_inc(sem(f"page_loaded{n % PAGE_RING}"), 16)

            def load_cross(g, cache, kt):
                src = t["cache_mem_k" if cache == "k" else "cache_mem_v"]
                for b in range(GB):
                    n = cross_page(g, cache, kt, b)
                    before = n - C_PAGE_RING
                    if before >= 0:
                        bg, bv, bk = before // 16, before // 8 % 2, before // 4 % 2
                        if not bv:
                            use = use_of["ck_turn", bg, bk, 1][b]
                            sp.wait_ge(full[use[0]], use[1] + 1)
                        elif bk == 0:
                            sp.wait_ge(sem("cv_pages_read"), bg + 1)
                        else:
                            use = use_of["cs_pv", bg, 1][1]
                            sp.wait_ge(full[use[0]], use[1] + 1)
                    sp.dma_start(c_pages[:, n % C_PAGE_RING, :],
                                 src[0, 4 * g + b, kt * P:(kt + 1) * P, :, :].rearrange("r h d -> r (h d)")
                                 ).then_inc(sem(f"c_page_loaded{n % C_PAGE_RING}"), 16)

            xp = t["x_prompt"][0].rearrange("(i p) c -> p i c", p=P)
            for i in range(4):
                sp.dma_start(x_tok[:, i, :], xp[:, i, :]).then_inc(sem(f"x_loaded{i}"), 16)
            sp.dma_start(x_tok_s[0:32, :], t["x_sample"].rearrange("b q c -> (b q) c")).then_inc(sem("x_loaded4"), 16)
            for row, name, n in ((V_MIX, "norm_mix_w", KT), (V_CROSS, "norm_cross_w", KT),
                                 (V_MEM, "norm_mem_w", KT), (V_FFN, "norm_ffn_w", KT)):
                sp.dma_start(packed[row:row + n, 0, :], t[name][0].rearrange("(k p) -> k p", p=P)
                               ).then_inc(sem("packed_loaded"), 16)
            sp.dma_start(packed[V_FINAL:V_FINAL + KT, 0, :], t["norm_final_w"].rearrange("(k p) -> k p", p=P)
                           ).then_inc(sem("packed_loaded"), 16)
            sp.dma_start(packed[V_CW:V_CW + 3 * CT, 0, :], t["conv_mix_w"][0].rearrange("w (k p) -> (w k) p", p=P)
                           ).then_inc(sem("packed_loaded"), 16)
            sp.dma_start(packed[V_CB:V_CB + CT, 0, :], t["conv_mix_b"][0].rearrange("(k p) -> k p", p=P)
                           ).then_inc(sem("packed_loaded"), 16)
            sp.dma_start(packed[V_SUB:V_SUB + 1, 0, :], t["subln_w"]).then_inc(sem("packed_loaded"), 16)
            sp.dma_start(page_ids[:, :], t["page_table"].rearrange("(o b) n -> o (b n)", o=1)).then_inc(sem("ids_loaded"), 16)
            for n in range(4):
                load_weights(n)
            sp.wait_ge(sem("ids_loaded"), 16)
            self_loads = list(PAGE_GROUPS)
            load_self(*self_loads.pop(0))
            load_self(*self_loads.pop(0))
            cross_loads = [(g, c, kt) for g in range(GROUPS) for c in ("k", "v") for kt in range(2)]
            for step, uses, latest in NUMBERED:
                kind, arg = step[0], step[1] if len(step) > 1 else None
                if kind == "tile":
                    load_weights(step[1] + 4)
                    if step[1] == TILE["cq", "cq", 0]:
                        sp.wait_ge(tile_done, MEM_FIRST + 1)
                        sp.wait_ge(sem("k_saved"), 128)
                        sp.wait_ge(sem("v_saved"), 32)
                        sp.wait_ge(sem("mix_saved"), 32)
                        load_cross(*cross_loads.pop(0))
                    if step[1] == TILE["cq", "cq", 3]:
                        load_cross(*cross_loads.pop(0))
                    if step[1] == CO_FIRST + 1:
                        sp.wait_ge(tile_done, CO_FIRST + 1)
                        sp.wait_ge(sem("mv_saved"), 16)
                        sp.wait_ge(sem("mk_saved0"), 16 * 4)
                        sp.wait_ge(sem("mk_saved1"), 16 * 4)
                        sp.dma_start(f_rows[0:16, :], t["state_conv_ffn"][0].rearrange("b w c -> (b w) c")
                                     ).then_inc(sem("f_rows_loaded"), 16)
                if (kind == "k_turn" and step[3:] == (0, 0)) or kind == "s_pv":
                    if self_loads:
                        load_self(*self_loads.pop(0))
                if step == ("k_score", 1, 3, 1, 1):
                    use = uses[0]
                    sp.wait_ge(full[use[0]], use[1] + 1)
                    sp.dma_start(mem_tok, t["mem_prompt"][0].rearrange("(i p) c -> p i c", p=P)
                                 ).then_inc(sem("mem_loaded"), 16)
                if (kind == "ck_turn" and step[3] == 0) or kind == "cs_pv":
                    if cross_loads:
                        load_cross(*cross_loads.pop(0))
                if kind == "final":
                    wait_taken(sp, *uses[0])
                    wait_taken(sp, *uses[1])
                    if arg < 4:
                        sp.dma_start(t["out_y_prompt"][0, arg * P:(arg + 1) * P, :], y_out[:, arg % 3, :]
                                       ).then_inc(sem(f"y_saved{arg % 3}"), 16)
                    else:
                        sp.dma_start(t["out_y_sample"].rearrange("b q c -> (b q) c"), y_out[0:32, arg % 3, :]
                                       ).then_inc(sem(f"y_saved{arg % 3}"), 16)

        @block.gpsimd
        def _(pool):
            pool.memset(rel[BUCKETS:BUCKETS + 1, :], NEG).then_inc(sem("rel_set"), 1)
            pool.wait_ge(sem("rel_set"), 1)
            pool.memset(ones[:, :], 1.0).then_inc(sem("ones_set"), 1)
            pool.memset(eps[:, :], EPS).then_inc(sem("eps_set"), 1)
            fw = t["conv_ffn_w"][0].rearrange("w (k p) -> (w k) p", p=P)
            pool.dma_start(packed[0:88, 1, :], fw[0:88, :]).then_inc(sem("fvec_loaded"), 16)
            pool.dma_start(packed[0:44, 2, :], fw[88:132, :]).then_inc(sem("fvec_loaded"), 16)
            pool.dma_start(packed[44:88, 2, :], t["conv_ffn_b"][0].rearrange("(k p) -> k p", p=P)
                           ).then_inc(sem("fvec_loaded"), 16)
            pool.dma_start(mix_in[0:16, :], t["state_conv_mix"][0].rearrange("b w c -> (b w) c")
                           ).then_inc(sem("fvec_loaded"), 16)
            pool.dma_start(onehot[0:BUCKETS + 1, :], t["const_onehot"]).then_inc(sem("bias_loaded"), 16)
            pool.dma_start(rel[0:BUCKETS, :], t["rel_bias"]).then_inc(sem("bias_loaded"), 16)
            pool.dma_start(row_cols[:, :], t["const_rows"]).then_inc(sem("rows_loaded"), 16)
            for j, name in enumerate(("lambda_q1", "lambda_k1", "lambda_q2", "lambda_k2")):
                ap = t[name]
                pool.dma_start(lams[:, j, :], bass.AP(ap.tensor, ap.offset, [[0, P], [1, DK]])
                               ).then_inc(sem("lams_loaded"), 16)
            pool.memset(q_rows[:, :, :, :], 0.0).then_inc(sem("q_rows_zero"), 1)
            pool.memset(new_bias[:, :, :], NEG).then_inc(sem("new_bias_neg"), 1)
            pool.memset(pre[:, 0:2], 0.0).then_inc(sem("pre_zero"), 1)

            kp = t["out_k_prompt"][0, 0].rearrange("(i p) h d -> p i h d", p=P)
            vp = t["out_v_prompt"][0, 0].rearrange("(i p) h d -> p i (h d)", p=P)
            ks = t["out_k_sample"][0].rearrange("b q h d -> (b q) h d")
            vs = t["out_v_sample"][0].rearrange("b q h d -> (b q) (h d)")
            mk = t["out_mem_k"][0, 0].rearrange("(i p) h d -> p i (h d)", p=P)
            mv = t["out_mem_v"][0, 0].rearrange("(i p) h d -> p i (h d)", p=P)
            for step, uses, latest in NUMBERED:
                kind, arg = step[0], step[1] if len(step) > 1 else None
                if kind == "bias":
                    sc = t["scratch_bias"]
                    wait_taken(pool, *uses[0])
                    pool.dma_start(sc, dist_vec[0:HEADS, :]).then_inc(sem("dist_saved"), 16)
                    pool.wait_ge(sem("dist_saved"), 16)
                    pool.dma_start(near_raw, bass.AP(sc.tensor, sc.offset, [[1, P], [DIST, HEADS], [1, 2 * P]])
                                   ).then_inc(sem("near_loaded"), 16)
                    for b in range(GB):
                        for c in range(2):
                            r = 32 * b + 16 * c
                            pool.dma_start(near_s_raw[r:r + 16, :],
                                           bass.AP(sc.tensor, sc.offset + DIST - 4 - 2 * P,
                                                   [[DIST, HEADS], [1, DEC_SEQ], [1, P + DEC_SEQ]])
                                           ).then_inc(sem("near_loaded"), 16)
                    pool.memset(s_keys[:, :, 16:32], 0.0).then_inc(sem("s_keys_zero"), 1)
                    pool.wait_ge(sem("near_ready"), 2)
                    pool.wait_ge(sem("new_bias_neg"), 1)
                    for g in range(GROUPS):
                        for b in range(GB):
                            if g or b:
                                pool.wait_ge(sem("new_bias_ready"), GB * g + b)
                            pool.tensor_copy(new_bias[32 * b:32 * b + 32, g, 16 * g + 4 * b:16 * g + 4 * b + 4],
                                             near_s[32 * b:32 * b + 32, P:P + DEC_SEQ]
                                             ).then_inc(sem("new_bias_ready"), 1)
                if kind == "q_blocks":
                    pool.wait_ge(sem("q_rows_zero"), 1)
                    for h in range(HEADS):
                        wait_tile_out(pool, TILE["in", "q", h])
                        for c in range(2):
                            rows = slice(DK * c, DK * c + DK)
                            lo = 16 * c + 4 * h
                            if h or c:
                                pool.wait_ge(sem("q_rows_ready"), 2 * h + c)
                            pool.tensor_copy(seqs(q_rows[rows, h, :, :], lo, lo + 4), samples(q_t[rows, h, :])
                                             ).then_inc(sem("q_rows_ready"), 1)
                if kind == "k_out":
                    wait_taken(pool, *uses[0])
                    pool.dma_start(kp[:, :, arg, :], k_out.rearrange("p (i d) -> p i d", d=P)
                                   ).then_inc(sem("k_saved"), 16)
                    wait_taken(pool, *uses[1])
                    pool.dma_start(ks[:, arg, :], k_out_s).then_inc(sem("k_saved"), 16)
                if kind == "v_out" and arg == HEADS - 1:
                    wait_taken(pool, *uses[0])
                    pool.dma_start(vp, v_tok[:, 0:4, :]).then_inc(sem("v_saved"), 16)
                    wait_taken(pool, *uses[1])
                    pool.dma_start(vs, v_tok[0:32, 4, :]).then_inc(sem("v_saved"), 16)
                if kind == "mix_out":
                    wait_taken(pool, *uses[0])
                    pool.dma_start(t["out_conv_mix_prompt"][0, 0], mix_out[0:2, :]).then_inc(sem("mix_saved"), 16)
                    pool.dma_start(t["out_conv_mix_sample"][0].rearrange("b w c -> (b w) c"), mix_out[2:18, :]
                                   ).then_inc(sem("mix_saved"), 16)
                if kind == "mem_out":
                    if arg < KT:
                        wait_taken(pool, *uses[0])
                        pool.dma_start(mk[:, :, arg * P:(arg + 1) * P], m_stage[:, arg % 2, :, :]
                                       ).then_inc(sem(f"mk_saved{arg % 2}"), 16)
                    if arg == 2 * KT - 1:
                        wait_taken(pool, *uses[0])
                        pool.dma_start(mv, mv_tok[:, :, :]).then_inc(sem("mv_saved"), 16)
                if kind == "tile" and arg == MEM_FIRST + 1:
                    pool.wait_ge(tile_done, MEM_FIRST + 1)
                    pool.wait_ge(sem("k_saved"), 128)
                    pool.wait_ge(sem("v_saved"), 32)
                    pool.wait_ge(sem("mix_saved"), 32)
                    pool.memset(qc_rows[:, :, :, :], 0.0).then_inc(sem("qc_rows_zero"), 1)
                if kind == "cq_blocks":
                    pool.wait_ge(sem("qc_rows_zero"), 1)
                    for d in range(KT):
                        wait_tile_out(pool, TILE["cq", "cq", d])
                        lo = 4 * (d // 2)
                        pool.tensor_copy(seqs(qc_rows[:, d, :, :], lo, lo + 4), samples(qc_t[:, d, :])
                                         ).then_inc(sem("qc_rows_ready"), 1)
                if kind == "tile" and arg == CO_FIRST + 1:
                    pool.wait_ge(tile_done, CO_FIRST + 1)
                    pool.wait_ge(sem("mv_saved"), 16)
                    pool.wait_ge(sem("mk_saved0"), 16 * 4)
                    pool.wait_ge(sem("mk_saved1"), 16 * 4)
                    pool.memset(up_pad[:, :, :, 0:2], 0.0).then_inc(sem("up_pad_zero"), 1)
                if kind == "ffn":
                    g, i, j = step[1:]
                    if i == 0 and j == 0:
                        wait_taken(pool, *use_of["state_in",][0])
                        wait_taken(pool, *use_of["state_in",][1])
                    if i >= 2:
                        pool.wait_ge(sem("conv_ffn_done"), 2 * (i - 2) + 1 + j)
                    pool.tensor_copy(up_pad_s[:, j, i % 2, :, 0:2],
                                     f_prefix[:, j * FT + i, :].rearrange("p (b w) -> p b w", w=2)
                                     ).then_inc(sem("f_prefix_in"), 1)
                    wait_tile_out(pool, TILE["up", ("gate", "up")[j], i])
                    pool.wait_ge(sem("up_in"), 2 * i + 1 + j)
                    pool.tensor_copy(f_state[:, j * FT + i, 0:2], up_pad[:, j, i % 2, SEQ:SEQ + 2]
                                     ).then_inc(sem("f_state_ready"), 1)
                    pool.tensor_copy(f_state[:, j * FT + i, 2:18].rearrange("p (b w) -> p b w", w=2),
                                     up_pad_s[:, j, i % 2, :, DEC_SEQ:DEC_SEQ + 2]
                                     ).then_inc(sem("f_state_ready"), 1)
                if kind == "state_out" and arg == 2 * FT // 4 - 1:
                    wait_taken(pool, "T0", latest["T0"])
                    wait_taken(pool, "T1", latest["T1"])
                    pool.dma_start(t["out_conv_ffn_prompt"][0, 0], f_rows[0:2, :]).then_inc(sem("f_saved"), 16)
                    pool.dma_start(t["out_conv_ffn_sample"][0].rearrange("b w c -> (b w) c"), f_rows[2:18, :]
                                   ).then_inc(sem("f_saved"), 16)
            for name, n in (("k_saved", 128), ("v_saved", 32), ("mix_saved", 32), ("mk_saved0", 64), ("mk_saved1", 64),
                            ("mv_saved", 16), ("f_saved", 32), ("y_saved0", 32), ("y_saved1", 32),
                            ("y_saved2", 16), ("dist_saved", 16)):
                pool.wait_ge(sem(name), n)

        @block.tensor
        def _(pe):
            def tile(n, latest, first_half):
                w = TILES[n]
                hi, lo = split[w["phase"]]
                middle = w["kt"] // 2 if n in HALVED else 0
                pe.wait_ge(w_lo_ready, n + 1)
                if n >= 2:
                    wait_tile_out(pe, n - 2)
                width = HALF if w["phase"] != "mem" else N_MEM
                halves = 2 if w["phase"] != "mem" else 1
                for k in range(middle) if first_half else range(middle, w["kt"]):
                    if w["first"]:
                        if w["phase"] in ready:
                            pe.wait_ge(ready[w["phase"]], k + 1)
                        elif w["phase"] == "out" and k < CT:
                            pe.wait_ge(sem("mixer_ready"), k + 1)
                        elif w["phase"] == "out" and k == CT:
                            wait_taken(pe, "T0", latest["T0"])
                        elif w["phase"] == "co":
                            if k == 0:
                                wait_taken(pe, *use_of["cs_out", GROUPS - 1][2])
                                wait_taken(pe, *use_of["cs_out", GROUPS - 1][3])
                            wait_taken(pe, *use_of["c_pv", k][0])
                        elif w["phase"].startswith("down"):
                            pe.wait_ge(sem("act_ready"), FFN_GROUPS[int(w["phase"][4:])][k] + 1)
                    w_h, w_l = w_hi[:, n % W_HI_RING, k, :], w_lo[:, n % W_RING, k, :]
                    for a, (wt, act) in enumerate(((w_h, hi), (w_h, lo), (w_l, hi))):
                        for half in range(halves):
                            mm = pe.matmul(proj[n % 2][:, half, 0:width], wt,
                                           act[:, k, half * HALF:half * HALF + width], start=(k == 0 and a == 0),
                                           stop=(k == w["kt"] - 1 and a == 2))
                if not first_half:
                    mm.then_inc(tile_done, 1)

            def turn(use, parts):
                wait_empty(pe, use)
                for src, col in parts:
                    rows = src.shape[0]
                    width = int(np.prod(src.shape[1:]))
                    mm = pe.transpose(bank[use[0]][0:width, col:col + rows], src, ident[0:rows, 0:rows])
                mm.then_inc(full[use[0]], 1)

            for step, uses, latest in NUMBERED:
                kind, arg = step[0], step[1] if len(step) > 1 else None
                if kind == "setup":
                    pe.wait_ge(sem("packed_loaded"), 16 * 8)
                    turn(uses[0], [(packed[0:VEC_ROWS, 0, :], 0)])
                elif kind == "setup_2":
                    pe.wait_ge(sem("fvec_loaded"), 16 * 4)
                    turn(uses[0], [(packed[0:88, 1, :], 0), (packed[0:88, 2, :], 88)])
                    turn(uses[1], [(mix_in[0:16, c * P:(c + 1) * P], 16 * c) for c in range(CT)])
                elif kind == "x_in":
                    pe.wait_ge(sem("ident_loaded"), 16)
                    pe.wait_ge(sem(f"x_loaded{arg}"), 16)
                    src = x_tok[:, arg, :] if arg < 4 else x_tok_s[0:32, :]
                    for j in range(2):
                        turn(uses[j], [(src[:, (4 * j + d) * P:(4 * j + d + 1) * P], d * P) for d in range(4)])
                elif kind == "norm":
                    m = norms.index(arg)
                    pe.wait_ge(sem("ones_set"), 1)
                    pe.wait_ge(sem("sums_added"), KT * (m + 1))
                    if arg == "final":
                        wait_empty(pe, uses[0])
                        for i in range(5):
                            first = BLOCK[i] if i < 4 else HALF_P
                            mm = pe.matmul(bank["S0"][:, i:i + 1], sums[:, first:first + P], ones[:, 0:1],
                                           start=True, stop=True)
                        mm.then_inc(full["S0"], 1)
                        continue
                    for half, use in enumerate(uses):
                        wait_empty(pe, use)
                        width = N_MEM if arg == "mem" else HALF
                        pe.matmul(bank[use[0]][:, 0:width], ones[:, :], sums[:, half * HALF:half * HALF + width],
                                  start=True, stop=True).then_inc(full[use[0]], 1)
                elif kind == "bias":
                    pe.wait_ge(sem("bias_loaded"), 32)
                    pe.wait_ge(sem("rel_set"), 1)
                    wait_empty(pe, uses[0])
                    pe.matmul(bank["S0"][0:HEADS, 0:DIST], rel[0:BUCKETS + 1, :], onehot[0:BUCKETS + 1, :],
                              start=True, stop=True).then_inc(full["S0"], 1)
                elif kind in ("tile", "half_tile"):
                    tile(arg, latest, kind == "half_tile")
                elif kind in ("k_out", "v_out"):
                    wait_tile_out(pe, TILE["in", kind[0], arg])
                    if kind == "k_out":
                        turn(uses[0], [(block_cols(k_t, arg, i), i * P) for i in range(4)])
                        turn(uses[1], [(block_cols(k_t, arg, 4), 0)])
                    else:
                        turn(uses[0], [(block_cols(gates, arg % 2, i), i * P) for i in range(4)])
                        turn(uses[1], [(block_cols(gates, arg % 2, 4), 0)])
                elif kind == "k_turn":
                    g, kq, hp, pair = step[1:]
                    for j in range(2):
                        b = 2 * pair + j
                        if hp == 0:
                            for pg in range(2):
                                n = self_page(g, "k", kq, b, pg)
                                pe.wait_ge(sem(f"page_loaded{n % PAGE_RING}"), 16 * (n // PAGE_RING + 1))
                        parts = []
                        for h2 in range(2):
                            for pg in range(2):
                                n = self_page(g, "k", kq, b, pg)
                                h = 2 * hp + h2
                                parts.append((page(n)[:, h * P:(h + 1) * P], (2 * h2 + pg) * P))
                        turn(uses[j], parts)
                elif kind == "k_score":
                    g, kq, hp, h2 = step[1:]
                    if hp == 0 and h2 == 0:
                        pe.wait_ge(sem("q_rows_ready"), 2 * HEADS)
                        wait_empty(pe, uses[0])
                    half = (4 * g + kq) * 2 + hp
                    for pair in range(2):
                        for use in use_of["k_turn", g, kq, hp, pair]:
                            wait_taken(pe, *use)
                    h = 2 * hp + h2
                    for b in range(GB):
                        mm = pe.matmul(bank["S0"][32 * b:32 * b + 32, 0:2 * P], q_rows[:, h, GB * g + b, :],
                                       k_turned[:, half % 2, b, h2 * 2 * P:(h2 + 1) * 2 * P],
                                       start=(h == 0), stop=(h == HEADS - 1), tile_position=(0, 32 * b))
                    if h == HEADS - 1:
                        mm.then_inc(full["S0"], 1)
                    if len(uses) > 1:
                        wait_empty(pe, uses[1])
                        for h in range(HEADS):
                            mm = pe.matmul(bank["S1"][:, 0:32],
                                           q_rows[:, h, GB * g:GB * g + GB, :].rearrange("p b r -> p (b r)"),
                                           k_t[:, h, HALF_P:HALF + HALF_S], start=(h == 0), stop=(h == HEADS - 1))
                        mm.then_inc(full["S1"], 1)
                elif kind == "s_turn":
                    pe.wait_ge(sem("s_prob"), arg + 1)
                    turn(uses[0], [(s_sb[:, j * P:(j + 1) * P], j * P) for j in range(4)])
                    turn(uses[1], [(s_sb[:, (4 + j) * P:(5 + j) * P], j * P) for j in range(4)])
                    turn(uses[2], [(s_sb[:, PAST:PAST + 32], 0)])
                elif kind == "s_pv":
                    g, kq = step[1:]
                    if kq == 0:
                        wait_empty(pe, uses[0])
                        wait_taken(pe, *use_of["s_turn", g][1])
                        wait_taken(pe, *use_of["s_turn", g][2])
                        pe.wait_ge(sem("s_keys_zero"), 1)
                    for pg in range(2):
                        for b in range(GB):
                            n = self_page(g, "v", kq, b, pg)
                            pe.wait_ge(sem(f"page_loaded{n % PAGE_RING}"), 16 * (n // PAGE_RING + 1))
                            mm = pe.matmul(bank["S1"][32 * b:32 * b + 32, :], s_keys[:, (2 * kq + pg) * GB + b, :],
                                           page(n), start=(kq == 0 and pg == 0), stop=False,
                                           tile_position=(0, 32 * b))
                        mm.then_inc(sem("v_pages_read"), 1)
                elif kind == "s_new":
                    use = use_of["v_out", HEADS - 1][1]
                    wait_taken(pe, *use)
                    for b in range(GB):
                        mm = pe.matmul(bank["S1"][32 * b:32 * b + 32, :], s_keys[0:32, 8 * GB + b, :],
                                       v_tok[0:32, 4, :], start=False, stop=True, tile_position=(0, 32 * b))
                    mm.then_inc(full["S1"], 1)
                elif kind == "s_out":
                    wait_taken(pe, *use_of["s_norm", arg][0])
                    turn(uses[0], [(o_sb[:, h * P:(h + 1) * P], h * P) for h in range(HEADS)])
                elif kind == "p_score":
                    i, h = step[1:]
                    if h == 0 and i == 0:
                        for hh in range(HEADS):
                            wait_tile_out(pe, TILE["in", "k", hh])
                    for half in range(i // 2 + 1):
                        first = half * HALF_P
                        width = min((i + 1) * P - first, HALF_P)
                        for c in range(2):
                            if half == 0:
                                wait_empty(pe, uses[c])
                            rows = slice(DK * c, DK * c + DK)
                            mm = pe.matmul(bank[uses[c][0]][:, first:first + width], block_cols(q_t[rows, :, :], h, i),
                                           k_t[rows, h, BLOCK[2 * half]:BLOCK[2 * half] + width],
                                           start=True, stop=True)
                            if half == i // 2:
                                mm.then_inc(full[uses[c][0]], 1)
                elif kind == "p_turn":
                    i, h = step[1:]
                    u = i * HEADS + h
                    pe.wait_ge(sem("p_prob"), u + 1)
                    turn(uses[0], [(p_exp[:, u % 2, 0, j * P:(j + 1) * P], j * P) for j in range(i + 1)])
                elif kind == "p_pv":
                    i, h = step[1:]
                    u = i * HEADS + h
                    if h == 0:
                        wait_empty(pe, uses[0])
                    wait_taken(pe, *use_of["p_turn", i, h][0])
                    if u == 0:
                        wait_taken(pe, *use_of["v_out", HEADS - 1][0])
                    for j in range(i + 1):
                        mm = pe.matmul(bank["T1"][:, h * P:(h + 1) * P], p_keys[:, u % 2, j, :],
                                       v_tok[:, j, h * P:(h + 1) * P], start=(j == 0), stop=(j == i))
                    if h == HEADS - 1:
                        mm.then_inc(full["T1"], 1)
                elif kind == "p_out":
                    wait_taken(pe, *use_of["p_norm", arg][0])
                    turn(uses[0], [(o_blk[:, h * P:(h + 1) * P], h * P) for h in range(HEADS)])
                elif kind == "mem_in":
                    pe.wait_ge(sem("mem_loaded"), 16)
                    for i in range(2):
                        for j in range(2):
                            turn(uses[2 * i + j], [(mem_tok[:, i, (4 * j + d) * P:(4 * j + d + 1) * P], d * P)
                                                   for d in range(4)])
                elif kind == "mix_out":
                    pe.wait_ge(sem("mixer_ready"), CT)
                    turn(uses[0], [(mix_state[:, c, :], 0 + c * P) for c in range(CT)])
                elif kind == "mem_out":
                    wait_tile_out(pe, TILE["mem", "mem", arg])
                    src = mk_t[:, arg, :] if arg < KT else mv_t[:, arg % 2, :]
                    turn(uses[0], [(src[:, i * P:(i + 1) * P], i * P) for i in range(2)])
                elif kind == "c_score":
                    hp, i = step[1:]
                    if hp == 0 and i == 0:
                        for d in (KT - 2, KT - 1):
                            wait_tile_out(pe, TILE["cq", "cq", d])
                    wait_empty(pe, uses[0])
                    for h2 in range(2):
                        for d in range(2):
                            mm = pe.matmul(bank["S1"][:, h2 * N_MEM:(h2 + 1) * N_MEM],
                                           block_cols(qc_t, 2 * (2 * hp + h2) + d, i),
                                           mk_t[:, 2 * (2 * hp + h2) + d, :], start=(d == 0), stop=(d == 1))
                    mm.then_inc(full["S1"], 1)
                elif kind == "c_turn":
                    hp, i = step[1:]
                    v = 4 * hp + i
                    pe.wait_ge(sem("c_prob"), v + 1)
                    turn(uses[0], [(c_exp[:, v % 2, h2, kt * P:(kt + 1) * P], (2 * h2 + kt) * P)
                                   for h2 in range(2) for kt in range(2)])
                elif kind == "c_pv":
                    wait_taken(pe, *use_of["mem_out", 2 * KT - 1][0])
                    wait_taken(pe, *use_of["c_turn", 1, 3][0])
                    wait_empty(pe, uses[0])
                    for kt in range(2):
                        mm = pe.matmul(bank["S1"], mv_tok[:, kt, arg * P:(arg + 1) * P], c_keys[:, arg // 2 * 2 + kt, :],
                                       start=(kt == 0), stop=(kt == 1))
                    mm.then_inc(full["S1"], 1)
                elif kind == "ck_turn":
                    g, kt, dh = step[1:]
                    for b in range(GB):
                        n = cross_page(g, "k", kt, b)
                        pe.wait_ge(sem(f"c_page_loaded{n % C_PAGE_RING}"), 16 * (n // C_PAGE_RING + 1))
                        turn(uses[b], [(c_pages[:, n % C_PAGE_RING, (4 * dh + d) * P:(4 * dh + d + 1) * P], d * P) for d in range(4)])
                elif kind == "ck_score":
                    g, kt, dh = step[1:]
                    if dh == 0:
                        pe.wait_ge(sem("qc_rows_ready"), KT)
                        wait_empty(pe, uses[0])
                    for use in use_of["ck_turn", g, kt, dh][2:]:
                        wait_taken(pe, *use)
                    for d in range(4):
                        for b in range(GB):
                            mm = pe.matmul(bank["S0"][32 * b:32 * b + 32, 0:P], qc_rows[:, 4 * dh + d, GB * g + b, :],
                                           c_turned[:, b, d * P:(d + 1) * P], start=(dh == 0 and d == 0),
                                           stop=(dh == 1 and d == 3), tile_position=(0, 32 * b))
                    if dh == 1:
                        mm.then_inc(full["S0"], 1)
                elif kind == "cs_turn":
                    pe.wait_ge(sem("cs_prob"), arg + 1)
                    turn(uses[0], [(c_s[:, kt * P:(kt + 1) * P], kt * P) for kt in range(2)])
                elif kind == "cs_pv":
                    g, kt = step[1:]
                    if kt == 0:
                        wait_empty(pe, uses[0])
                        wait_empty(pe, uses[1])
                        wait_taken(pe, *use_of["cs_turn", g][0])
                    for half in range(2):
                        for b in range(GB):
                            n = cross_page(g, "v", kt, b)
                            if half == 0:
                                pe.wait_ge(sem(f"c_page_loaded{n % C_PAGE_RING}"), 16 * (n // C_PAGE_RING + 1))
                            mm = pe.matmul(bank[uses[half][0]][32 * b:32 * b + 32, :], cs_keys[:, kt, 32 * b:32 * b + 32],
                                           c_pages[:, n % C_PAGE_RING, half * 512:(half + 1) * 512], start=(kt == 0), stop=(kt == 1),
                                           tile_position=(0, 32 * b))
                        if kt == 1:
                            mm.then_inc(full[uses[half][0]], 1)
                    if kt == 0:
                        mm.then_inc(sem("cv_pages_read"), 1)
                elif kind == "cs_out":
                    wait_taken(pe, *uses[0])
                    wait_taken(pe, *uses[1])
                    for j in range(2):
                        turn(uses[2 + j], [(o_cross[:, (4 * j + d) * P:(4 * j + d + 1) * P], d * P) for d in range(4)])
                elif kind == "state_in":
                    pe.wait_ge(sem("f_rows_loaded"), 16)
                    for j in range(2):
                        turn(uses[j], [(f_rows[0:16, (FT * j + i) * P:(FT * j + i + 1) * P], 16 * i) for i in range(FT)])
                elif kind == "state_out":
                    pe.wait_ge(sem("f_state_ready"), 4 * FT)
                    turn(uses[0], [(f_state[:, 4 * arg + m, :], m * P) for m in range(4)])
                elif kind == "final":
                    pe.wait_ge(ready["final"], KT)
                    for j in range(2):
                        turn(uses[j], [(block_cols(x, 4 * j + d, arg), d * P) for d in range(4)])

        @block.scalar
        def _(act):
            chain = [0]
            squares = [0]

            def done(ins):
                chain[0] += 1
                ins.then_inc(sem("act_step"), 1)
                act.wait_ge(sem("act_step"), chain[0])

            def split_hi(n):
                if n >= len(TILES):
                    return
                kt = TILES[n]["kt"]
                act.wait_ge(w_loaded[n % W_RING], 16 * (n // W_RING + 1))
                if n >= W_HI_RING:
                    act.wait_ge(tile_done, n - W_HI_RING + 1)
                act.activation(w_hi[:, n % W_HI_RING, 0:kt, :], w_raw[:, n % W_RING, 0:kt, :],
                               ACT.Copy).then_inc(w_hi_ready, 1)

            def rstd_of(out, in_, width_scale):
                done(act.activation(out, in_, ACT.Ln, bias=eps[0:out.shape[0], 0:1], scale=width_scale))
                return act.activation(out, out, ACT.Exp, scale=-0.5)

            act.dma_start(ident[:, :], t["const_ident"]).then_inc(sem("ident_loaded"), 16)
            for step, uses, latest in NUMBERED:
                kind, arg = step[0], step[1] if len(step) > 1 else None
                if kind == "setup":
                    wait_full(act, uses[0])
                    act.activation(vec[:, :], bank["T0"][:, 0:VEC_ROWS], ACT.Copy).then_inc(free["T0"], 1)
                elif kind == "setup_2":
                    wait_full(act, uses[0])
                    act.activation(fvec[:, :], bank["T0"][:, 0:8 * FT], ACT.Copy).then_inc(free["T0"], 1)
                    wait_full(act, uses[1])
                    act.activation(mix_prefix[:, :], bank["T1"][:, 0:CT * 16], ACT.Copy).then_inc(free["T1"], 1)
                    act.wait_ge(sem("lam_dots"), 2)
                    act.activation(small[:, 42:44], small[:, 40:42], ACT.Exp).then_inc(sem("lam_exp"), 1)
                elif kind == "first_split":
                    split_hi(arg)
                elif kind == "x_in":
                    wait_full(act, uses[0])
                    if arg < 4:
                        act.activation(x[:, 0:4, BLOCK[arg]:BLOCK[arg] + P], quads["T0"], ACT.Copy
                                       ).then_inc(free["T0"], 1)
                    else:
                        act.activation(x[:, 0:4, HALF_P:HALF + HALF_S],
                                       quads["T0"][:, :, 0:32], ACT.Copy
                                       ).then_inc(free["T0"], 1)
                elif kind == "squares":
                    q = squares[0]
                    squares[0] += 1
                    if q >= 2:
                        act.wait_ge(sem("sums_added"), q - 1)
                    if q // KT == norms.index("in"):
                        wait_taken(act, *use_of["x_in", 4][0])
                        wait_taken(act, *use_of["x_in", 4][1])
                    elif step[2] == "mem":
                        wait_taken(act, *use_of["mem_in",][2])
                        wait_taken(act, *use_of["mem_in",][3])
                        act.wait_ge(full["T0"], use_of["s_out", 1][0][1] + 1)
                    else:
                        phase = {"cq": "out", "up": "co", "final": "down2"}[norms[q // KT]]
                        wait_tile_out(act, TILE[phase, "add", step[1]])
                    if step[2] == "mem":
                        act.activation(square[:, q % 2, 0:N_MEM], mem_t[:, step[1], :], ACT.Square
                                       ).then_inc(sem("squared"), 1)
                    else:
                        act.activation(square[:, q % 2, :], x[:, step[1], :], ACT.Square
                                       ).then_inc(sem("squared"), 1)
                elif kind == "norm":
                    act.wait_ge(sem("eps_set"), 1)
                    if arg == "final":
                        wait_full(act, uses[0])
                        act.activation(rstd_tok[:, :], bank["S0"][:, 0:5], ACT.Ln, bias=eps[:, 0:1],
                                       scale=1.0 / D_MODEL).then_inc(free["S0"], 1)
                        wait_taken(act, *uses[0])
                        act.activation(rstd_tok[:, :], rstd_tok[:, :], ACT.Exp, scale=-0.5).then_inc(sem("rstd_ready"), 1)
                        continue
                    width = N_MEM if arg == "mem" else HALF
                    for half, use in enumerate(uses):
                        wait_full(act, use)
                        act.activation(rstd[:, half * HALF:half * HALF + width], bank[use[0]][:, 0:width], ACT.Ln,
                                       bias=eps[:, 0:1], scale=1.0 / D_MODEL).then_inc(free[use[0]], 1)
                    for half, use in enumerate(uses):
                        wait_taken(act, *use)
                        act.activation(rstd[:, half * HALF:half * HALF + width],
                                       rstd[:, half * HALF:half * HALF + width], ACT.Exp, scale=-0.5
                                       ).then_inc(sem("rstd_ready"), 1)
                elif kind == "apply":
                    k, w = step[2], vec[:, norm_w[arg] + step[2]:norm_w[arg] + step[2] + 1]
                    if arg == "final":
                        act.activation(x[:, k, :], x[:, k, :], ACT.Copy, scale=w).then_inc(ready["final"], 1)
                    elif arg != "mem":
                        if arg == "cq":
                            act.wait_ge(tile_done, OUT_LAST + 1)
                            wait_tile_out(act, TILE["out", "add", k])
                        if arg == "in" and k == 0:
                            wait_taken(act, *use_of["x_in", 4][0])
                            wait_taken(act, *use_of["x_in", 4][1])
                            wait_taken(act, *use_of["setup",][0])
                        if arg == "up":
                            act.wait_ge(tile_done, CO_FIRST + 1)
                            wait_tile_out(act, TILE["co", "add", k])
                        act.activation(split[arg][0][:, k, :], x[:, k, :], ACT.Copy, scale=w
                                       ).then_inc(sem(f"{arg}_hi"), 1)
                    else:
                        m, k, hi = LATE_NORMS.index(arg), step[2], split[arg][0]
                        act.wait_ge(sem("normed_ready"), KT * m + k + 1)
                        if arg == "mem":
                            act.activation(hi[:, k, 0:N_MEM], normed[:, k % 3, 0:N_MEM], ACT.Copy
                                           ).then_inc(sem("normed_hi"), 1)
                        else:
                            act.activation(hi[:, k, :], normed[:, k % 3, :], ACT.Copy
                                           ).then_inc(sem("normed_hi"), 1)
                elif kind == "bias":
                    wait_full(act, uses[0])
                    act.activation(dist_vec[0:HEADS, :], bank["S0"][0:HEADS, 0:DIST], ACT.Copy).then_inc(free["S0"], 1)
                elif kind == "tile":
                    split_hi(arg + 2)
                    w = TILES[arg]
                    out = proj[arg % 2][:, :, :]
                    if w["kind"] != "mem":
                        continue
                    act.wait_ge(tile_done, arg + 1)
                    if w["kind"] == "mem":
                        if w["i"] == 0:
                            act.wait_ge(sem("k_saved"), 128)
                            act.wait_ge(sem("v_saved"), 32)
                            act.wait_ge(sem("mix_saved"), 32)
                        dst = mk_t[:, w["i"], :] if w["i"] < KT else mv_t[:, w["i"] % 2, :]
                        act.activation(dst, out[:, 0, 0:N_MEM], ACT.Copy).then_inc(tile_out[arg % 2], 1)
                elif kind == "k_out":
                    wait_full(act, uses[1])
                    if arg:
                        act.wait_ge(sem("k_saved"), 32 * arg)
                    act.activation(k_out_s, bank["T1"][0:32, 0:P], ACT.Copy).then_inc(free["T1"], 1)
                elif kind == "v_out":
                    wait_full(act, uses[1])
                    act.activation(v_tok[0:32, 4, arg * P:(arg + 1) * P], bank["T1"][0:32, 0:P], ACT.Copy
                                   ).then_inc(free["T1"], 1)
                elif kind == "k_turn":
                    half = (4 * step[1] + step[2]) * 2 + step[3]
                    wait_full(act, uses[0])
                    act.activation(k_turned[:, half % 2, 2 * step[4], :], bank["T0"], ACT.Copy).then_inc(free["T0"], 1)
                elif kind == "s_soft":
                    act.wait_ge(sem("s_max"), arg + 1)
                    act.activation(s_sb, s_sb, ACT.Exp, bias=small[:, 0:1], accum_out=small[:, 1:2]
                                   ).then_inc(sem("s_exp"), 1)
                elif kind == "s_norm":
                    wait_full(act, uses[0])
                    act.wait_ge(sem("k_saved"), 128)
                    for h in range(HEADS):
                        cols = slice(h * P, (h + 1) * P)
                        ins = act.activation(o_sb[:, cols], bank["S1"][:, cols], ACT.Square,
                                             scale=row_cols[:, h:h + 1], accum_out=small[:, 4 + h:5 + h])
                        ins.then_inc(sem("s_squares"), 1)
                    act.wait_ge(sem("s_sum"), arg + 1)
                    rstd_of(small[:, 9:10], small[:, 8:9], 1.0 / DV).then_inc(sem("s_rstd"), 1)
                    act.wait_ge(sem("s_row_scale"), arg + 1)
                    for h in range(HEADS):
                        cols = slice(h * P, (h + 1) * P)
                        ins = act.activation(o_sb[:, cols], bank["S1"][:, cols], ACT.Copy, scale=small[:, 10 + h:11 + h])
                        ins.then_inc(sem("act_side") if h < HEADS - 1 else free["S1"], 1)
                elif kind in ("s_out", "p_out"):
                    wait_full(act, uses[0])
                    if kind == "s_out":
                        act.activation(b_hi[:, 4:8, HALF_P + HALF_S * arg:HALF + HALF_S * arg].rearrange("p h (b q) -> p h b q", q=DEC_SEQ),
                                       head_rows("T0", P + 4, 0, HEADS), ACT.Copy, scale=sub_w[:, 0:1]
                                       ).then_inc(sem("attn_hi"), 1)
                    else:
                        act.activation(b_hi[:, 4:8, BLOCK[arg]:BLOCK[arg] + P], quads["T0"],
                                       ACT.Copy, scale=sub_w[:, 0:1]).then_inc(sem("attn_hi"), 1)
                elif kind == "p_score":
                    i, h = step[1:]
                    u = i * HEADS + h
                    act.wait_ge(sem("p_max"), u + 1)
                    for c in range(2):
                        act.activation(p_exp[:, u % 2, c, 0:(i + 1) * P], bank[uses[c][0]][:, 0:(i + 1) * P], ACT.Exp,
                                       bias=small[:, 16 + 2 * (u % 2) + c:17 + 2 * (u % 2) + c],
                                       accum_out=small[:, 20 + 2 * (u % 2) + c:21 + 2 * (u % 2) + c]
                                       ).then_inc(free[uses[c][0]], 1)
                elif kind == "p_turn":
                    i, h = step[1:]
                    u = i * HEADS + h
                    wait_full(act, uses[0])
                    act.activation(p_keys[:, u % 2, 0:i + 1, :], quads["T0"][:, 0:i + 1, :], ACT.Copy
                                   ).then_inc(free["T0"], 1)
                elif kind == "p_norm":
                    wait_full(act, uses[0])
                    for h in range(HEADS):
                        cols = slice(h * P, (h + 1) * P)
                        ins = act.activation(o_sq[:, cols], bank["T1"][:, cols], ACT.Square,
                                             accum_out=small[:, 28 + h:29 + h])
                        if h < HEADS - 1:
                            ins.then_inc(sem("act_side"), 1)
                        else:
                            done(ins)
                    rstd_of(small[:, 32:36], small[:, 28:32], 1.0 / DV).then_inc(sem("p_rstd"), 1)
                elif kind == "mem_in":
                    for n, use in enumerate(uses):
                        i, j = n // 2, n % 2
                        wait_full(act, use)
                        act.activation(mem_t[:, 4 * j:4 * j + 4, i * P:(i + 1) * P], quads[use[0]], ACT.Copy
                                       ).then_inc(free[use[0]], 1)
                elif kind == "mix_out":
                    wait_full(act, uses[0])
                    act.activation(mix_out[0:18, :], bank["S0"][0:18, :], ACT.Copy).then_inc(free["S0"], 1)
                elif kind == "mem_out":
                    wait_full(act, uses[0])
                    src = bank["T0"][:, 0:N_MEM].rearrange("p (i c) -> p i c", c=P)
                    if arg < KT:
                        if arg >= 2:
                            act.wait_ge(sem(f"mk_saved{arg % 2}"), 16 * (arg // 2))
                        act.activation(m_stage[:, arg % 2, :, :], src, ACT.Copy).then_inc(free["T0"], 1)
                    else:
                        act.activation(mv_tok[:, :, (arg - KT) * P:(arg - KT + 1) * P], src, ACT.Copy
                                       ).then_inc(free["T0"], 1)
                elif kind == "c_score":
                    v = 4 * step[1] + step[2]
                    act.wait_ge(sem("c_max"), v + 1)
                    for h2 in range(2):
                        col = 2 * (v % 2) + h2
                        act.activation(c_exp[:, v % 2, h2, :], bank["S1"][:, h2 * N_MEM:(h2 + 1) * N_MEM], ACT.Exp,
                                       bias=c_small[:, col:col + 1], accum_out=c_small[:, 4 + col:5 + col]
                                       ).then_inc(sem("act_side") if h2 == 0 else free["S1"], 1)
                elif kind == "c_pv":
                    wait_full(act, uses[0])
                    act.activation(prompt(a_hi[:, arg, :]), by_half(bank["S1"]), ACT.Copy).then_inc(sem("cross_hi"), 1)
                elif kind == "ck_turn":
                    for b in (0, 2):
                        wait_full(act, uses[b])
                        act.activation(c_turned[:, b, :], bank["T0"], ACT.Copy).then_inc(free["T0"], 1)
                elif kind == "cs_soft":
                    act.wait_ge(sem("cs_max"), arg + 1)
                    act.activation(c_s, c_s, ACT.Exp, bias=c_small[:, 16:17], accum_out=c_small[:, 17:18]
                                   ).then_inc(sem("cs_exp"), 1)
                elif kind == "cs_turn":
                    wait_full(act, uses[0])
                    act.activation(cs_keys, bank["T0"][:, 0:N_MEM].rearrange("p (i c) -> p i c", c=P), ACT.Copy
                                   ).then_inc(free["T0"], 1)
                elif kind == "cs_out":
                    wait_full(act, uses[0])
                    ins = act.activation(o_cross[:, 0:512], bank["S0"], ACT.Copy)
                    ins.then_inc(free["S0"], 1)
                    for j in range(2):
                        wait_full(act, uses[2 + j])
                        for h2 in range(2):
                            h = 2 * j + h2
                            act.activation(a_hi[:, 2 * h:2 * h + 2, HALF_P + HALF_S * arg:HALF + HALF_S * arg].rearrange("p d (b q) -> p d b q", q=DEC_SEQ),
                                           head_rows(uses[2 + j][0], P, h2 * 2 * P + 4 * h, 2), ACT.Copy
                                           ).then_inc(sem("cs_hi"), 1)
                elif kind == "state_in":
                    wait_full(act, uses[0])
                    act.activation(f_prefix[:, 0:FT, :], bank["T0"][:, 0:FT * 16].rearrange("p (i c) -> p i c", c=16),
                                   ACT.Copy).then_inc(free["T0"], 1)
                elif kind == "ffn":
                    g, i, j = step[1:]
                    if j:
                        act.wait_ge(sem("conv_ffn_done"), 2 * i + 1)
                        act.activation(conv[:, 0, :], conv[:, 0, :], ACT.Silu).then_inc(sem("silu_done"), 1)
                    if i and j == 0:
                        act.wait_ge(sem("act_ready"), i)
                    act.wait_ge(sem("up_pad_zero"), 1)
                    act.wait_ge(sem("up_in"), 2 * i + 1 + j)
                    act.wait_ge(sem("f_prefix_in"), 2 * i + 1 + j)
                    wait_tile_out(act, TILE["up", ("gate", "up")[j], i])
                    n = j * FT + i
                    w0, bias = fvec[:, n:n + 1], fvec[:, 6 * FT + n:6 * FT + n + 1]
                    act.activation(prompt(conv[:, j, :]), by_half(up_pad[:, j, i % 2, 0:SEQ]), ACT.Identity,
                                   bias=bias, scale=w0).then_inc(sem("first_tap"), 1)
                    act.activation(samples(conv[:, j, :]), seqs(up_pad_s[:, j, i % 2, :, :], 0, 4), ACT.Identity,
                                   bias=bias, scale=w0).then_inc(sem("first_tap"), 1)
                elif kind == "state_out":
                    if arg % 2 == 0:
                        wait_full(act, uses[0])
                        act.activation(f_rows[0:18, arg * 512:(arg + 1) * 512], bank["T0"][0:18, :], ACT.Copy
                                       ).then_inc(free["T0"], 1)
                elif kind == "final":
                    wait_full(act, uses[0])
                    if arg >= 3:
                        act.wait_ge(sem(f"y_saved{arg % 3}"), 16)
                    if arg == 0:
                        act.wait_ge(sem("rstd_ready"), 8)
                    rows = P if arg < 4 else 32
                    act.activation(y_out[0:rows, arg % 3, 0:512], bank["T0"][0:rows, :], ACT.Copy,
                                   scale=rstd_tok[0:rows, arg:arg + 1]).then_inc(free["T0"], 1)

        @block.vector
        def _(dve):
            chain = [0]
            squares = [0]

            def done(ins):
                chain[0] += 1
                ins.then_inc(sem("dve_step"), 1)
                dve.wait_ge(sem("dve_step"), chain[0])

            def side(ins):
                chain[0] += 1
                ins.then_inc(sem("dve_step"), 1)

            def settle():
                dve.wait_ge(sem("dve_step"), chain[0])

            def split_lo(n):
                if n >= len(TILES):
                    return
                kt = TILES[n]["kt"]
                dve.wait_ge(w_hi_ready, n + 1)
                dve.tensor_tensor(w_lo[:, n % W_RING, 0:kt, :], w_raw[:, n % W_RING, 0:kt, :],
                                  w_hi[:, n % W_HI_RING, 0:kt, :].bitcast(F32), ALU.subtract).then_inc(w_lo_ready, 1)

            def conv3(pads, outs, cols, first_tap=True):
                w, b = cols[0:3], cols[3]
                (pp, ps), (op, os) = pads, outs
                if first_tap:
                    side(dve.tensor_scalar(op, by_half(pp[:, 0:SEQ]), w[0], b, ALU.mult, ALU.add))
                    done(dve.tensor_scalar(os, seqs(ps, 0, 4), w[0], b, ALU.mult, ALU.add))
                side(dve.scalar_tensor_tensor(out=op, in0=by_half(pp[:, 1:1 + SEQ]), scalar=w[1], in1=op,
                                              op0=ALU.mult, op1=ALU.add))
                done(dve.scalar_tensor_tensor(out=os, in0=seqs(ps, 1, 5), scalar=w[1], in1=os,
                                              op0=ALU.mult, op1=ALU.add))
                side(dve.scalar_tensor_tensor(out=op, in0=by_half(pp[:, 2:2 + SEQ]), scalar=w[2], in1=op,
                                              op0=ALU.mult, op1=ALU.add))
                return dve.scalar_tensor_tensor(out=os, in0=seqs(ps, 2, 6), scalar=w[2], in1=os,
                                                op0=ALU.mult, op1=ALU.add)

            for step, uses, latest in NUMBERED:
                kind, arg = step[0], step[1] if len(step) > 1 else None
                if kind == "first_split":
                    split_lo(arg)
                elif kind == "setup_2":
                    dve.wait_ge(sem("lams_loaded"), 64)
                    for j in range(2):
                        dve.tensor_tensor_reduce(lams[:, 2 * j, :], lams[:, 2 * j, :], lams[:, 2 * j + 1, :], 1.0, 0.0,
                                                 ALU.mult, ALU.add, small[:, 40 + j:41 + j]).then_inc(sem("lam_dots"), 1)
                    dve.wait_ge(sem("lam_exp"), 1)
                    done(dve.tensor_tensor(small[:, 44:45], small[:, 43:44], small[:, 42:43], ALU.subtract))
                    done(dve.tensor_scalar(neg_lam[:, :], small[:, 44:45], -LAM_INIT, None, ALU.add))
                    dve.wait_ge(sem("rows_loaded"), 16)
                    done(dve.tensor_scalar(lam_row[:, :], neg_lam[:, :], -1.0, None, ALU.add))
                    done(dve.tensor_scalar(lam_row[:, :], lam_row[:, :], row_cols[:, 4:5], 1.0, ALU.mult, ALU.add))
                    done(dve.tensor_scalar(sub_w[:, :], vec[:, V_SUB:V_SUB + 1], 1.0 - LAM_INIT, None, ALU.mult))
                elif kind == "x_in":
                    wait_full(dve, uses[1])
                    if arg < 4:
                        dve.tensor_copy(x[:, 4:8, BLOCK[arg]:BLOCK[arg] + P], quads["T1"]
                                        ).then_inc(free["T1"], 1)
                    else:
                        dve.tensor_copy(x[:, 4:8, HALF_P:HALF + HALF_S],
                                        quads["T1"][:, :, 0:32]
                                        ).then_inc(free["T1"], 1)
                elif kind == "squares":
                    q = squares[0]
                    squares[0] += 1
                    dve.wait_ge(sem("squared"), q + 1)
                    mem = step[2] == "mem"
                    total = sums[:, 0:N_MEM] if mem else sums
                    new = square[:, q % 2, 0:N_MEM] if mem else square[:, q % 2, :]
                    if q % KT == 0:
                        if q:
                            use = use_of["norm", norms[q // KT - 1]][-1]
                            dve.wait_ge(full[use[0]], use[1] + 1)
                        dve.tensor_copy(total, new).then_inc(sem("sums_added"), 1)
                    else:
                        dve.wait_ge(sem("sums_added"), q)
                        dve.tensor_tensor(total, total, new, ALU.add).then_inc(sem("sums_added"), 1)
                elif kind == "apply" and arg not in ("mem", "final"):
                    k = step[2]
                    hi, lo = split[arg]
                    dve.wait_ge(sem(f"{arg}_hi"), k + 1)
                    dve.scalar_tensor_tensor(out=lo[:, k, :], in0=x[:, k, :],
                                             scalar=vec[:, norm_w[arg] + k:norm_w[arg] + k + 1],
                                             in1=hi[:, k, :].bitcast(F32), op0=ALU.mult, op1=ALU.subtract
                                             ).then_inc(ready[arg], 1)
                elif kind == "apply" and arg in LATE_NORMS:
                    m, mem, k = LATE_NORMS.index(arg), arg == "mem", step[2]
                    if k == 0:
                        dve.wait_ge(sem("rstd_ready"), {"mem": 3, "cq": 5}[arg])
                        if arg == "mem":
                            dve.wait_ge(sem("mixer_ready"), CT)
                            dve.wait_ge(tile_done, IN_LAST + 1)
                        if arg == "cq":
                            dve.wait_ge(tile_done, OUT_LAST + 1)

                    def low(k):
                        dve.wait_ge(sem("normed_hi"), KT * m + k + 1)
                        hi, lo = split[arg]
                        dve.tensor_tensor(lo[:, k, cols], normed[:, k % 3, cols], hi[:, k, cols].bitcast(F32),
                                          ALU.subtract).then_inc(ready[arg], 1)

                    cols = slice(0, N_MEM if mem else TOK)
                    if k >= 3:
                        dve.wait_ge(ready[arg], k - 2)
                    dve.scalar_tensor_tensor(out=normed[:, k % 3, cols], in0=mem_t[:, k, :] if mem else x[:, k, :],
                                             scalar=vec[:, norm_w[arg] + k:norm_w[arg] + k + 1], in1=rstd[:, cols],
                                             op0=ALU.mult, op1=ALU.mult).then_inc(sem("normed_ready"), 1)
                    if k:
                        low(k - 1)
                    if k == KT - 1:
                        low(k)
                elif kind == "near":
                    dve.wait_ge(sem("near_loaded"), 16 * 9)
                    dve.tensor_copy(near[:, :, :], near_raw[:, :, ::-1]).then_inc(sem("near_ready"), 1)
                    dve.tensor_copy(near_s[:, :], near_s_raw[:, ::-1]).then_inc(sem("near_ready"), 1)
                elif kind == "tile":
                    w = TILES[arg]
                    if w["phase"] != "up":
                        split_lo(arg + 2)
                    out = proj[arg % 2][:, :, :]
                    if w["kind"] == "add":
                        dve.wait_ge(tile_done, arg + 1)
                        dve.tensor_tensor(halves(x[:, w["i"], :]), out[:, :, 0:HALF], halves(x[:, w["i"], :]), ALU.add
                                          ).then_inc(tile_out[arg % 2], 1)
                    if w["phase"] in ("in", "cq", "up"):
                        if arg == TILE["in", "q", 0]:
                            dve.wait_ge(sem("rstd_ready"), 2)
                        if arg == TILE["cq", "cq", 0]:
                            dve.wait_ge(sem("rstd_ready"), 5)
                        if arg == TILE["up", "gate", 0]:
                            dve.wait_ge(sem("rstd_ready"), 7)
                        dve.wait_ge(tile_done, arg + 1)
                    if w["kind"] == "q":
                        dve.scalar_tensor_tensor(out=halves(q_t[:, w["i"], :]), in0=out[:, :, 0:HALF], scalar=DK ** -0.5,
                                                 in1=halves(rstd), op0=ALU.mult, op1=ALU.mult).then_inc(tile_out[arg % 2], 1)
                    if w["kind"] == "cq":
                        dve.scalar_tensor_tensor(out=halves(qc_t[:, w["i"], :]), in0=out[:, :, 0:HALF],
                                                 scalar=MEM_DH ** -0.5, in1=halves(rstd), op0=ALU.mult, op1=ALU.mult
                                                 ).then_inc(tile_out[arg % 2], 1)
                    if w["kind"] in ("k", "v", "gb", "gc"):
                        if w["kind"] in ("gb", "gc") and w["i"]:
                            dve.wait_ge(sem("mixer_ready"), w["i"])
                        dst = {"k": k_t[:, w["i"], :], "v": gates[:, w["i"] % 2, :], "gb": gates[:, 0, :],
                               "gc": gates[:, 1, :]}[w["kind"]]
                        dve.tensor_tensor(halves(dst), out[:, :, 0:HALF], halves(rstd), ALU.mult
                                          ).then_inc(tile_out[arg % 2], 1)
                    if w["kind"] in ("gate", "up"):
                        j, i = int(w["kind"] == "up"), w["i"]
                        if i >= 2:
                            dve.wait_ge(sem("conv_ffn_done"), 2 * (i - 2) + 1 + j)
                            dve.wait_ge(sem("f_state_ready"), 4 * (i - 2) + 2 * j + 2)
                        if i < 2:
                            dve.wait_ge(sem("f_rows_loaded"), 16)
                        dve.tensor_tensor(by_half(up_pad[:, j, i % 2, 2:2 + SEQ]), prompt_of(out), prompt(rstd),
                                          ALU.mult).then_inc(sem("up_in"), 1)
                        dve.tensor_tensor(seqs(up_pad_s[:, j, i % 2, :, :], 2, 6), samples_of(out), samples(rstd),
                                          ALU.mult).then_inc(tile_out[arg % 2], 1)
                    if w["kind"] == "u":
                        wait_tile_out(dve, arg - 1)
                        if w["i"]:
                            dve.wait_ge(sem("mixer_ready"), w["i"])
                        else:
                            dve.wait_ge(sem("k_saved"), 128)
                        side(dve.tensor_tensor(by_half(pre[:, 2:2 + SEQ]), prompt_of(out), prompt(gates[:, 1, :]), ALU.mult))
                        dve.tensor_tensor(seqs(pre_s, 2, 6), samples_of(out), samples(gates[:, 1, :]), ALU.mult
                                          ).then_inc(tile_out[arg % 2], 1)
                    if w["phase"] == "up" and arg != TILE["up", "up", FT - 1]:
                        split_lo(arg + 2)
                elif kind == "conv":
                    settle()
                    wait_tile_out(dve, TILE["in", "u", arg])
                    side(dve.tensor_tensor(by_half(pre[:, 2:2 + SEQ]), by_half(pre[:, 2:2 + SEQ]), prompt(rstd), ALU.mult))
                    side(dve.tensor_tensor(seqs(pre_s, 2, 6), seqs(pre_s, 2, 6), samples(rstd), ALU.mult))
                    settle()
                    dve.wait_ge(sem("pre_zero"), 1)
                    wait_taken(dve, *use_of["setup_2",][1])
                    side(dve.tensor_copy(pre_s[:, :, 0:2],
                                         mix_prefix[:, arg * 16:(arg + 1) * 16].rearrange("p (b w) -> p b w", w=2)))
                    side(dve.tensor_copy(mix_state[:, arg, 0:2], pre[:, SEQ:SEQ + 2]))
                    done(dve.tensor_copy(mix_state[:, arg, 2:18].rearrange("p (b w) -> p b w", w=2), pre_s[:, :, 4:6]))
                    cols = [vec[:, c:c + 1] for c in (V_CW + arg, V_CW + CT + arg, V_CW + 2 * CT + arg, V_CB + arg)]
                    y = gates[:, 1, :]
                    done(conv3((pre, pre_s), (prompt(y), samples(y)), cols))
                elif kind == "mix":
                    y = gates[:, 1, :]
                    done(dve.tensor_tensor(y, y, gates[:, 0, :], ALU.mult))
                    done(dve.tensor_copy(b_hi[:, arg, :], y))
                    dve.tensor_tensor(b_lo[:, arg, :], y, b_hi[:, arg, :].bitcast(F32), ALU.subtract
                                      ).then_inc(sem("mixer_ready"), 1)
                elif kind == "k_out":
                    wait_full(dve, uses[0])
                    if arg:
                        dve.wait_ge(sem("k_saved"), 32 * arg)
                    dve.tensor_copy(k_out, bank["T0"]).then_inc(free["T0"], 1)
                elif kind == "v_out":
                    wait_full(dve, uses[0])
                    dve.tensor_copy(v_tok[:, 0:4, arg * P:(arg + 1) * P], quads["T0"]).then_inc(free["T0"], 1)
                elif kind == "k_turn":
                    half = (4 * step[1] + step[2]) * 2 + step[3]
                    wait_full(dve, uses[1])
                    dve.tensor_copy(k_turned[:, half % 2, 2 * step[4] + 1, :], bank["T1"]).then_inc(free["T1"], 1)
                elif kind == "k_score":
                    g, kq, hp, h2 = step[1:]
                    if (hp, h2) != (1, 1):
                        continue
                    wait_full(dve, uses[0])
                    if g == 0 and kq == 0:
                        dve.wait_ge(sem("near_ready"), 2)
                    far = near_s[:, 0:1]
                    if kq < 3:
                        dve.tensor_scalar(s_sb[:, kq * 256:kq * 256 + 256], bank["S0"][:, 0:256], far, None, ALU.add
                                          ).then_inc(free["S0"], 1)
                    else:
                        side(dve.tensor_scalar(s_sb[:, 768:896], bank["S0"][:, 0:P], far, None, ALU.add))
                        dve.tensor_tensor(s_sb[:, 896:1024], bank["S0"][:, P:2 * P], near_s[:, 0:P], ALU.add
                                          ).then_inc(free["S0"], 1)
                        wait_full(dve, uses[1])
                        dve.wait_ge(sem("new_bias_ready"), 8)
                        dve.tensor_tensor(s_sb[:, PAST:PAST + 32], bank["S1"][:, 0:32], new_bias[:, g, :], ALU.add
                                          ).then_inc(free["S1"], 1)
                elif kind == "s_soft":
                    settle()
                    wait_taken(dve, *use_of["k_score", arg, 3, 1, 1][0])
                    wait_taken(dve, *use_of["k_score", arg, 3, 1, 1][1])
                    dve.tensor_reduce(small[:, 0:1], s_sb, AX.X, ALU.max, negate=True).then_inc(sem("s_max"), 1)
                    dve.wait_ge(sem("s_exp"), arg + 1)
                    done(dve.reciprocal(small[:, 2:3], small[:, 1:2]))
                    done(dve.tensor_tensor(small[:, 3:4], small[:, 2:3], lam_row[:, :], ALU.mult))
                    dve.tensor_scalar(s_sb, s_sb, small[:, 3:4], None, ALU.mult).then_inc(sem("s_prob"), 1)
                elif kind == "s_turn":
                    for j, use in enumerate(uses[:2]):
                        wait_full(dve, use)
                        src = bank[use[0]].rearrange("p (a r) -> p a r", r=32)
                        side(dve.tensor_copy(s_keys[:, 16 * j:16 * j + 16, 0:16], src[:, :, 0:16]))
                        settle()
                        dve.tensor_tensor(s_keys[:, 16 * j:16 * j + 16, 0:16], src[:, :, 16:32],
                                          s_keys[:, 16 * j:16 * j + 16, 0:16], ALU.add).then_inc(free[use[0]], 1)
                    wait_full(dve, uses[2])
                    src = bank["T0"][0:32, 0:P].rearrange("p (a r) -> p a r", r=32)
                    done(dve.tensor_copy(s_keys[0:32, 32:36, 0:16], src[:, :, 0:16]))
                    dve.tensor_tensor(s_keys[0:32, 32:36, 0:16], src[:, :, 16:32], s_keys[0:32, 32:36, 0:16], ALU.add
                                      ).then_inc(free["T0"], 1)
                elif kind == "s_norm":
                    dve.wait_ge(sem("s_squares"), HEADS * (arg + 1))
                    dve.tensor_reduce(small[:, 8:9], small[:, 4:8], AX.X, ALU.add).then_inc(sem("s_sum"), 1)
                    dve.wait_ge(sem("s_rstd"), arg + 1)
                    dve.tensor_scalar(small[:, 10:14], row_cols[:, 0:4], small[:, 9:10], None, ALU.mult
                                      ).then_inc(sem("s_row_scale"), 1)
                elif kind in ("s_out", "p_out"):
                    wait_full(dve, uses[0])
                    dve.wait_ge(sem("attn_hi"), attn_parts[step] + 1)
                    if kind == "s_out":
                        cols = slice(HALF_P + HALF_S * arg, HALF + HALF_S * arg)
                        for h in range(HEADS):
                            dve.scalar_tensor_tensor(
                                out=b_lo[:, CT + h, cols].rearrange("p (b q) -> p b q", q=DEC_SEQ),
                                in0=free_dims(bank["T0"], h * (P + DEC_SEQ), [(32, GB), (1, DEC_SEQ)]), scalar=sub_w[:, 0:1],
                                in1=b_hi[:, CT + h, cols].bitcast(F32).rearrange("p (b q) -> p b q", q=DEC_SEQ),
                                op0=ALU.mult, op1=ALU.subtract
                            ).then_inc(sem("dve_side") if h < HEADS - 1 else free["T0"], 1)
                        continue
                    cols = slice(BLOCK[arg], BLOCK[arg] + P)
                    dve.scalar_tensor_tensor(out=b_lo[:, CT:KT, cols], in0=quads["T0"], scalar=sub_w[:, 0:1],
                                             in1=b_hi[:, CT:KT, cols].bitcast(F32), op0=ALU.mult,
                                             op1=ALU.subtract).then_inc(free["T0"], 1)
                elif kind == "p_score":
                    i, h = step[1:]
                    u = i * HEADS + h
                    w = min(2, i + 1) * P
                    wait_full(dve, uses[0])
                    wait_full(dve, uses[1])
                    if i >= 2:
                        side(dve.tensor_scalar(score[:, :, 0:(i - 1) * P], score[:, :, 0:(i - 1) * P], near[:, h, 0:1],
                                               None, ALU.add))
                    for c in range(2):
                        lo = (i + 1) * P - w
                        side(dve.tensor_tensor(score[:, c, lo:lo + w], score[:, c, lo:lo + w],
                                               near[:, h, 2 * P - w:2 * P], ALU.add))
                    settle()
                    if u == 0:
                        dve.wait_ge(sem("near_ready"), 2)
                    dve.tensor_reduce(small[:, 16 + 2 * (u % 2):18 + 2 * (u % 2)], score[:, :, 0:(i + 1) * P], AX.X,
                                      ALU.max, negate=True).then_inc(sem("p_max"), 1)
                elif kind == "p_scale":
                    dve.wait_ge(sem("p_rstd"), arg + 1)
                    wait_full(dve, uses[0])
                    dve.tensor_tensor(o_blk.rearrange("p (h d) -> p h d", h=HEADS), quads["T1"],
                                      free_dims(small[:, 32:36], 0, [(1, HEADS), (0, DV)]), ALU.mult
                                      ).then_inc(free["T1"], 1)
                elif kind == "p_mix":
                    i, h = step[1:]
                    u = i * HEADS + h
                    for use in use_of["p_score", i, h]:
                        wait_taken(dve, *use)
                    z, r = small[:, 20 + 2 * (u % 2):22 + 2 * (u % 2)], small[:, 24 + 2 * (u % 2):26 + 2 * (u % 2)]
                    done(dve.reciprocal(r, z))
                    done(dve.tensor_tensor(r[:, 1:2], r[:, 1:2], neg_lam[:, :], ALU.mult))
                    e = [p_exp[:, u % 2, c, 0:(i + 1) * P] for c in range(2)]
                    done(dve.tensor_scalar(e[0], e[0], r[:, 0:1], None, ALU.mult))
                    dve.scalar_tensor_tensor(out=e[0], in0=e[1], scalar=r[:, 1:2], in1=e[0], op0=ALU.mult,
                                             op1=ALU.add).then_inc(sem("p_prob"), 1)
                elif kind == "c_score":
                    v = 4 * step[1] + step[2]
                    wait_full(dve, uses[0])
                    dve.tensor_reduce(c_small[:, 2 * (v % 2):2 * (v % 2) + 2],
                                      bank["S1"].rearrange("p (h k) -> p h k", h=2), AX.X, ALU.max, negate=True
                                      ).then_inc(sem("c_max"), 1)
                elif kind == "c_mix":
                    v = 4 * step[1] + step[2]
                    wait_taken(dve, *use_of["c_score", step[1], step[2]][0])
                    r = c_small[:, 8 + 2 * (v % 2):10 + 2 * (v % 2)]
                    done(dve.reciprocal(r, c_small[:, 4 + 2 * (v % 2):6 + 2 * (v % 2)]))
                    for h2 in range(2):
                        e = c_exp[:, v % 2, h2, :]
                        ins = dve.tensor_scalar(e, e, r[:, h2:h2 + 1], None, ALU.mult)
                        side(ins) if h2 == 0 else ins.then_inc(sem("c_prob"), 1)
                elif kind == "c_turn":
                    wait_full(dve, uses[0])
                    hp, i = step[1:]
                    dve.tensor_copy(c_keys[:, 4 * hp:4 * hp + 4, i * P:(i + 1) * P], quads["T0"]).then_inc(free["T0"], 1)
                elif kind == "c_pv":
                    dve.wait_ge(sem("cross_hi"), arg + 1)
                    dve.tensor_tensor(prompt(a_lo[:, arg, :]), by_half(bank["S1"]),
                                      prompt(a_hi[:, arg, :]).bitcast(F32), ALU.subtract).then_inc(free["S1"], 1)
                elif kind == "ck_turn":
                    for b in (1, 3):
                        wait_full(dve, uses[b])
                        dve.tensor_copy(c_turned[:, b, :], bank["T1"]).then_inc(free["T1"], 1)
                elif kind == "ck_score":
                    g, kt, dh = step[1:]
                    if dh == 1:
                        wait_full(dve, uses[0])
                        dve.tensor_copy(c_s[:, kt * P:(kt + 1) * P], bank["S0"][:, 0:P]).then_inc(free["S0"], 1)
                elif kind == "cs_soft":
                    wait_taken(dve, *use_of["ck_score", arg, 1, 1][0])
                    dve.tensor_reduce(c_small[:, 16:17], c_s, AX.X, ALU.max, negate=True).then_inc(sem("cs_max"), 1)
                    dve.wait_ge(sem("cs_exp"), arg + 1)
                    done(dve.reciprocal(c_small[:, 18:19], c_small[:, 17:18]))
                    dve.tensor_scalar(c_s, c_s, c_small[:, 18:19], None, ALU.mult).then_inc(sem("cs_prob"), 1)
                elif kind == "cs_out":
                    wait_full(dve, uses[1])
                    dve.tensor_copy(o_cross[:, 512:1024], bank["T1"]).then_inc(free["T1"], 1)
                    for j in range(2):
                        for h2 in range(2):
                            h = 2 * j + h2
                            dve.wait_ge(sem("cs_hi"), 4 * arg + 2 * j + 2)
                            cols = (slice(None), slice(2 * h, 2 * h + 2),
                                    slice(HALF_P + HALF_S * arg, HALF + HALF_S * arg))
                            ins = dve.tensor_tensor(
                                a_lo[cols].rearrange("p d (b q) -> p d b q", q=DEC_SEQ),
                                head_rows(uses[2 + j][0], P, h2 * 2 * P + 4 * h, 2),
                                a_hi[cols].bitcast(F32).rearrange("p d (b q) -> p d b q", q=DEC_SEQ), ALU.subtract)
                            ins.then_inc(sem("dve_side") if h2 == 0 else free[uses[2 + j][0]], 1)
                elif kind == "state_in":
                    wait_full(dve, uses[1])
                    dve.tensor_copy(f_prefix[:, FT:2 * FT, :], bank["T1"][:, 0:FT * 16].rearrange("p (i c) -> p i c", c=16)
                                    ).then_inc(free["T1"], 1)
                elif kind == "ffn":
                    g, i, j = step[1:]
                    dve.wait_ge(sem("first_tap"), 4 * i + 2 * j + 2)
                    n = j * FT + i
                    cols = [fvec[:, c * 2 * FT + n:c * 2 * FT + n + 1] for c in range(4)]
                    out = conv[:, j, :]
                    ins = conv3((up_pad[:, j, i % 2, :], up_pad_s[:, j, i % 2, :, :]), (prompt(out), samples(out)), cols,
                                first_tap=False)
                    ins.then_inc(sem("conv_ffn_done"), 1)
                    if j == 0:
                        continue
                    dve.wait_ge(sem("silu_done"), i + 1)
                    dve.wait_ge(sem("conv_ffn_done"), 2 * i + 2)
                    dve.tensor_tensor(conv[:, 1, :], conv[:, 0, :], conv[:, 1, :], ALU.mult
                                      ).then_inc(sem("gated"), 1)
                    dve.wait_ge(sem("gated"), i + 1)
                    if i == FFN_GROUPS[g][0]:
                        last = TILE["co", "add", KT - 1] if g == 0 else TILE[f"down{g - 1}", "add", KT - 1]
                        dve.wait_ge(tile_done, last + 1)
                    k = i - FFN_GROUPS[g][0]
                    done(dve.tensor_copy(a_hi[:, k, :], conv[:, 1, :]))
                    dve.tensor_tensor(a_lo[:, k, :], conv[:, 1, :], a_hi[:, k, :].bitcast(F32), ALU.subtract
                                      ).then_inc(sem("act_ready"), 1)
                    if i == FT - 1:
                        split_lo(TILE["up", "up", i] + 2)
                elif kind == "state_out":
                    if arg % 2:
                        wait_full(dve, uses[0])
                        dve.tensor_copy(f_rows[0:18, arg * 512:(arg + 1) * 512], bank["T1"][0:18, :]).then_inc(free["T1"], 1)
                elif kind == "final":
                    wait_full(dve, uses[1])
                    if arg >= 3:
                        dve.wait_ge(sem(f"y_saved{arg % 3}"), 16)
                    if arg == 0:
                        dve.wait_ge(sem("rstd_ready"), 8)
                    rows = P if arg < 4 else 32
                    dve.tensor_scalar(y_out[0:rows, arg % 3, 512:1024], bank["T1"][0:rows, :],
                                      rstd_tok[0:rows, arg:arg + 1], None, ALU.mult).then_inc(free["T1"], 1)


_OUTS = [("y_prompt", (1, SEQ, D_MODEL)), ("y_sample", (DEC_BATCH, DEC_SEQ, D_MODEL)),
         ("k_prompt", (1, 1, SEQ, HEADS, 2 * DK)), ("v_prompt", (1, 1, SEQ, HEADS, DV)),
         ("k_sample", (1, DEC_BATCH, DEC_SEQ, HEADS, 2 * DK)), ("v_sample", (1, DEC_BATCH, DEC_SEQ, HEADS, DV)),
         ("conv_mix_prompt", (1, 1, 2, D_CONV)), ("conv_mix_sample", (1, DEC_BATCH, 2, D_CONV)),
         ("conv_ffn_prompt", (1, 1, 2, 2 * D_FF)), ("conv_ffn_sample", (1, DEC_BATCH, 2, 2 * D_FF)),
         ("mem_k", (1, 1, N_MEM, HEADS, MEM_DH)), ("mem_v", (1, 1, N_MEM, HEADS, MEM_DH))]


def kernel(**inputs):
    import concourse.bacc as bacc
    from concourse.bass_utils import run_bass_kernel_spmd

    nc = bacc.Bacc("TRN2", target_bir_lowering=False, num_devices=1)
    arrays, t = {}, {}
    given = {name: np.ascontiguousarray(a) for name, a in inputs.items()}
    given["const_ident"] = np.eye(P, dtype=np.float32)
    given["const_onehot"] = bucket_onehot()
    given["const_rows"] = row_columns()
    for name, a in given.items():
        arrays[f"in_{name}"] = a
        t[name] = nc.dram_tensor(f"in_{name}", a.shape, mybir.dt.from_np(a.dtype), kind="ExternalInput").ap()
    for name, shape in _OUTS:
        t[f"out_{name}"] = nc.dram_tensor(f"out_{name}", shape, F32, kind="ExternalOutput").ap()
    t["scratch_bias"] = nc.dram_tensor("scratch_bias", (HEADS, DIST), F32, kind="Internal").ap()
    build(nc, t)
    result = run_bass_kernel_spmd(nc, [arrays], core_ids=[0]).results[0]
    return tuple(result[f"out_{name}"] for name, _ in _OUTS)
```
